# Optimizing a Trainium2 kernel written in Bass

```python
import math
import jax, jax.numpy as jnp
from jax import lax
import numpy as np

D_MODEL = 1024
BATCH = 1
SEQ = 512
DEPTH = 1

D_DN = 512
DN_HEADS = 4
DN_HEAD_DIM = 128
CONV_WIDTH = 4
CHUNK = 64
D_ATT = 512
ATT_HEADS = 8
ATT_HEAD_DIM = 64
DILATED_PATTERNS = ((128, 1), (512, 4), (2048, 16))
N_BUCKETS = 32
MAX_DISTANCE = 2048
D_MIX = D_DN + D_ATT
D_IN = 4 * D_DN + 2 * DN_HEADS + 4 * D_ATT
EPS = 1e-6


def rms_norm(x, w):
    xf = x.astype(jnp.float32)
    return xf * lax.rsqrt(jnp.mean(xf * xf, axis=-1, keepdims=True) + EPS) * w.astype(jnp.float32)

def l2_norm(x):
    return x * lax.rsqrt(jnp.sum(x * x, axis=-1, keepdims=True) + EPS)

def split_heads(t, n_heads):
    b, s, _ = t.shape
    return t.reshape(b, s, n_heads, -1).transpose(0, 2, 1, 3)

def causal_depthwise_conv(u, w):
    k_width = w.shape[0]
    s = u.shape[1]
    up = jnp.pad(u, ((0, 0), (k_width - 1, 0), (0, 0)))
    y = up[:, 0:s] * w[0]
    for i in range(1, k_width):
        y = y + up[:, i:i + s] * w[i]
    return y

def gated_delta_rule(q, k, v, g, beta):
    b, h, s, dk = q.shape
    dv = v.shape[-1]
    n = s // CHUNK
    q = q * (dk ** -0.5)
    qc = q.reshape(b, h, n, CHUNK, dk)
    kc = k.reshape(b, h, n, CHUNK, dk)
    vc = v.reshape(b, h, n, CHUNK, dv)
    bc = beta.reshape(b, h, n, CHUNK)
    gc = jnp.cumsum(g.reshape(b, h, n, CHUNK), axis=-1)
    tril_incl = np.tril(np.ones((CHUNK, CHUNK), dtype=bool))
    tril_strict = np.tril(np.ones((CHUNK, CHUNK), dtype=bool), -1)
    diff = gc[..., :, None] - gc[..., None, :]
    decay = jnp.exp(jnp.where(tril_incl, diff, -jnp.inf))
    kb = kc * bc[..., None]
    a_mat = jnp.where(tril_strict, jnp.einsum('bhnid,bhnjd->bhnij', kb, kc) * decay, 0.0)
    l_mat = a_mat + jnp.eye(CHUNK, dtype=a_mat.dtype)
    u = lax.linalg.triangular_solve(l_mat, vc * bc[..., None], left_side=True, lower=True, unit_diagonal=True)
    w = lax.linalg.triangular_solve(l_mat, kb * jnp.exp(gc)[..., None], left_side=True, lower=True, unit_diagonal=True)
    attn_intra = jnp.einsum('bhnid,bhnjd->bhnij', qc, kc) * decay
    q_dec = qc * jnp.exp(gc)[..., None]
    k_tail = kc * jnp.exp(gc[..., -1:] - gc)[..., None]
    g_last = jnp.exp(gc[..., -1])
    xs = tuple(jnp.moveaxis(t, 2, 0) for t in (attn_intra, q_dec, k_tail, u, w, g_last))

    def step(state, inp):
        a_i, qd_i, kt_i, u_i, w_i, gl_i = inp
        v_new = u_i - jnp.einsum('bhck,bhkv->bhcv', w_i, state)
        o_i = jnp.einsum('bhck,bhkv->bhcv', qd_i, state) + jnp.einsum('bhij,bhjv->bhiv', a_i, v_new)
        state = state * gl_i[..., None, None] + jnp.einsum('bhck,bhcv->bhkv', kt_i, v_new)
        return state, o_i

    s0 = jnp.zeros((b, h, dk, dv), jnp.float32)
    _, o = lax.scan(step, s0, xs)
    return jnp.moveaxis(o, 0, 2).reshape(b, h, s, dv)

def t5_bucket(dist):
    max_exact = N_BUCKETS // 2
    d = np.maximum(dist, 1).astype(np.float64)
    large = max_exact + (np.log(d / max_exact) / math.log(MAX_DISTANCE / max_exact)
                         * (N_BUCKETS - max_exact)).astype(np.int32)
    large = np.minimum(large, N_BUCKETS - 1)
    return np.where(dist < max_exact, dist, large).astype(np.int32)

def dilated_pattern(q, k, v, rel_bias, window, dilation):
    b, h, s, hd = q.shape
    r = dilation
    l_sub = s // r
    w_steps = window // r
    blk = w_steps
    n_blk = -(-l_sub // blk)
    l_pad = n_blk * blk

    def to_blocks(t):
        t = t.reshape(b, h, l_sub, r, hd).transpose(0, 1, 3, 2, 4)
        t = jnp.pad(t, ((0, 0), (0, 0), (0, 0), (0, l_pad - l_sub), (0, 0)))
        return t.reshape(b, h, r, n_blk, blk, hd)

    def with_prev(t):
        prev = jnp.pad(t, ((0, 0), (0, 0), (0, 0), (1, 0), (0, 0), (0, 0)))[:, :, :, :-1]
        return jnp.concatenate([prev, t], axis=4)

    qb = to_blocks(q)
    kw = with_prev(to_blocks(k))
    vw = with_prev(to_blocks(v))
    qi = np.arange(blk)[:, None]
    kj = np.arange(2 * blk)[None, :]
    step = qi - kj + blk
    band = (step >= 0) & (step <= w_steps)
    key_idx = np.arange(n_blk)[:, None, None] * blk + kj[None] - blk
    mask = band[None] & (key_idx >= 0)
    buckets = t5_bucket(np.clip(step, 0, None) * r)
    bias = rel_bias.astype(jnp.float32)[:, buckets]
    scores = jnp.einsum('bhrnqd,bhrnkd->bhrnqk', qb, kw).astype(jnp.float32) + bias[:, None, None]
    scores = jnp.where(mask, scores, -jnp.inf)
    lse = jax.nn.logsumexp(scores, axis=-1)
    p = jnp.exp(scores - lse[..., None])
    o = jnp.einsum('bhrnqk,bhrnkd->bhrnqd', p, vw.astype(jnp.float32))
    o = o.reshape(b, h, r, l_pad, hd)[:, :, :, :l_sub].transpose(0, 1, 3, 2, 4).reshape(b, h, s, hd)
    lse = lse.reshape(b, h, r, l_pad)[:, :, :, :l_sub].transpose(0, 1, 3, 2).reshape(b, h, s)
    return o, lse

def deltanet_branch(qkv, z, b_proj, a_proj, conv_w, a_log, dt_bias, dn_norm_w):
    bsz, s, _ = qkv.shape
    qkv = jax.nn.silu(causal_depthwise_conv(qkv.astype(jnp.float32), conv_w.astype(jnp.float32)))
    q, k, v = jnp.split(qkv, 3, axis=-1)
    q = l2_norm(split_heads(q, DN_HEADS))
    k = l2_norm(split_heads(k, DN_HEADS))
    v = split_heads(v, DN_HEADS)
    beta = jax.nn.sigmoid(b_proj.astype(jnp.float32)).transpose(0, 2, 1)
    g = -jnp.exp(a_log.astype(jnp.float32)) * jax.nn.softplus(a_proj.astype(jnp.float32) + dt_bias.astype(jnp.float32))
    g = g.transpose(0, 2, 1)
    o = gated_delta_rule(q, k, v, g, beta)
    o = rms_norm(o, dn_norm_w).transpose(0, 2, 1, 3).reshape(bsz, s, D_DN)
    return o * jax.nn.silu(z.astype(jnp.float32))

def dilated_attention_branch(qkv, gate, q_norm_w, k_norm_w, rel_bias):
    bsz, s, _ = qkv.shape
    q, k, v = jnp.split(qkv, 3, axis=-1)
    q = rms_norm(split_heads(q, ATT_HEADS), q_norm_w) * (ATT_HEAD_DIM ** -0.5)
    k = rms_norm(split_heads(k, ATT_HEADS), k_norm_w)
    v = split_heads(v, ATT_HEADS).astype(jnp.float32)
    outs, lses = [], []
    for window, dilation in DILATED_PATTERNS:
        o_p, lse_p = dilated_pattern(q, k, v, rel_bias, window, dilation)
        outs.append(o_p)
        lses.append(lse_p)
    wts = jax.nn.softmax(jnp.stack(lses), axis=0)
    o = jnp.sum(wts[..., None] * jnp.stack(outs), axis=0)
    o = o.transpose(0, 2, 1, 3).reshape(bsz, s, D_ATT)
    return o * jax.nn.silu(gate.astype(jnp.float32))

def hybrid_layer(x, norm_w, w_in, conv_w, a_log, dt_bias, dn_norm_w, q_norm_w, k_norm_w, rel_bias, w_out):
    h = rms_norm(x, norm_w).astype(x.dtype)
    proj = h @ w_in
    cuts = [3 * D_DN, 4 * D_DN, 4 * D_DN + DN_HEADS, 4 * D_DN + 2 * DN_HEADS,
            4 * D_DN + 2 * DN_HEADS + 3 * D_ATT]
    qkv_dn, z_dn, b_dn, a_dn, qkv_att, gate_att = jnp.split(proj, cuts, axis=-1)
    y_dn = deltanet_branch(qkv_dn, z_dn, b_dn, a_dn, conv_w, a_log, dt_bias, dn_norm_w)
    y_att = dilated_attention_branch(qkv_att, gate_att, q_norm_w, k_norm_w, rel_bias)
    mixed = jnp.concatenate([y_dn, y_att], axis=-1).astype(x.dtype)
    return x + mixed @ w_out

def first_inputs(seed: int = 0) -> dict:
    key = jax.random.key(seed)
    ks = jax.random.split(key, 11)
    x = jax.random.normal(ks[0], (BATCH, SEQ, D_MODEL), jnp.float32)
    norm_w = 1.0 + 0.1 * jax.random.normal(ks[1], (DEPTH, D_MODEL), jnp.float32)
    w_in = jax.random.normal(ks[2], (DEPTH, D_MODEL, D_IN), jnp.float32) * (D_MODEL ** -0.5)
    conv_w = jax.random.normal(ks[3], (DEPTH, CONV_WIDTH, 3 * D_DN), jnp.float32) * (CONV_WIDTH ** -0.5)
    a_log = jnp.log(jax.random.uniform(ks[4], (DEPTH, DN_HEADS), jnp.float32, minval=1.0, maxval=16.0))
    dt = jnp.exp(jax.random.uniform(ks[5], (DEPTH, DN_HEADS), jnp.float32,
                                    minval=math.log(1e-3), maxval=math.log(1e-1)))
    dt_bias = dt + jnp.log(-jnp.expm1(-dt))
    dn_norm_w = 1.0 + 0.1 * jax.random.normal(ks[6], (DEPTH, DN_HEAD_DIM), jnp.float32)
    q_norm_w = 1.0 + 0.1 * jax.random.normal(ks[7], (DEPTH, ATT_HEAD_DIM), jnp.float32)
    k_norm_w = 1.0 + 0.1 * jax.random.normal(ks[8], (DEPTH, ATT_HEAD_DIM), jnp.float32)
    rel_bias = 0.5 * jax.random.normal(ks[9], (ATT_HEADS, N_BUCKETS), jnp.float32)
    w_out = jax.random.normal(ks[10], (DEPTH, D_MIX, D_MODEL), jnp.float32) * (D_MIX ** -0.5)
    return {"x": x, "norm_w": norm_w, "w_in": w_in, "conv_w": conv_w, "a_log": a_log,
            "dt_bias": dt_bias, "dn_norm_w": dn_norm_w, "q_norm_w": q_norm_w,
            "k_norm_w": k_norm_w, "rel_bias": rel_bias, "w_out": w_out}

def first_block(x, norm_w, w_in, conv_w, a_log, dt_bias, dn_norm_w, q_norm_w, k_norm_w, rel_bias, w_out):
    for layer in range(DEPTH):
        x = hybrid_layer(x, norm_w[layer], w_in[layer], conv_w[layer], a_log[layer], dt_bias[layer],
                         dn_norm_w[layer], q_norm_w[layer], k_norm_w[layer], rel_bias, w_out[layer])
    return x


HEAD_DIM = 64
SWA_HEADS = 8
SWA_KV_HEADS = 2
SWA_GROUP = SWA_HEADS // SWA_KV_HEADS
WINDOW = 128
DIFF_HEADS = 4
DIFF_VDIM = 2 * HEAD_DIM
BLOCK = 128
D_FF = 2816
CONV_WIDTH_2 = 3
RMS_EPS = 1e-6
NEG_INF = -1e30

SWA_Q = SWA_HEADS * HEAD_DIM
SWA_KV = SWA_KV_HEADS * HEAD_DIM
DIFF_QK = DIFF_HEADS * 2 * HEAD_DIM
DIFF_V = DIFF_HEADS * DIFF_VDIM
IN_COLS = SWA_Q + 2 * SWA_KV + 2 * DIFF_QK + DIFF_V + 2 * D_MODEL


def _rmsnorm(x, g):
    xf = x.astype(jnp.float32)
    y = xf * lax.rsqrt(jnp.mean(xf * xf, axis=-1, keepdims=True) + RMS_EPS)
    return (y * g.astype(jnp.float32)).astype(x.dtype)

def _alibi_slopes(n):
    return jnp.array([2.0 ** (-8.0 * (i + 1) / n) for i in range(n)], dtype=jnp.float32)

def _sliding_window_attention(q, k, v, sinks, slopes):
    b, s, _, d = q.shape
    nb = s // BLOCK
    qb = q.reshape(b, nb, BLOCK, SWA_KV_HEADS, SWA_GROUP, d)

    def with_prev(t):
        tb = t.reshape(b, nb, BLOCK, SWA_KV_HEADS, d)
        prev = jnp.concatenate([jnp.zeros_like(tb[:, :1]), tb[:, :-1]], axis=1)
        return jnp.concatenate([prev, tb], axis=2)

    kb, vb = with_prev(k), with_prev(v)
    scores = jnp.einsum('bnqkgd,bnskd->bnkgqs', qb, kb).astype(jnp.float32) * (d ** -0.5)
    qi = jnp.arange(BLOCK)[:, None]
    kj = jnp.arange(2 * BLOCK)[None, :]
    delta = qi + BLOCK - kj
    key_pos = jnp.arange(nb)[:, None, None] * BLOCK - BLOCK + kj[None]
    valid = (delta >= 0) & (delta < WINDOW) & (key_pos >= 0)
    bias = -slopes[:, :, None, None] * delta.astype(jnp.float32)
    scores = jnp.where(valid[None, :, None, None], scores + bias, NEG_INF)
    sink = jnp.broadcast_to(sinks.astype(jnp.float32).reshape(SWA_KV_HEADS, SWA_GROUP, 1, 1),
                            scores.shape[:-1] + (1,))
    probs = jax.nn.softmax(jnp.concatenate([scores, sink], axis=-1), axis=-1)[..., :-1]
    out = jnp.einsum('bnkgqs,bnskd->bnqkgd', probs.astype(v.dtype), vb)
    return out.reshape(b, s, SWA_HEADS * d)

def _diff_attention(q, k, v, lam, lam_init, subln_g, slopes):
    b, s = q.shape[:2]
    nb = s // BLOCK
    qb = jnp.moveaxis(q.reshape(b, nb, BLOCK, DIFF_HEADS, 2, HEAD_DIM), 1, 0)
    key_pos = jnp.arange(s)
    scale = HEAD_DIM ** -0.5

    def block_fn(args):
        qblk, n = args
        scores = jnp.einsum('bqhmd,bshmd->bhmqs', qblk, k).astype(jnp.float32) * scale
        q_pos = n * BLOCK + jnp.arange(BLOCK)
        delta = q_pos[:, None] - key_pos[None, :]
        scores = scores - slopes[:, None, None, None] * delta.astype(jnp.float32)
        scores = jnp.where(delta >= 0, scores, NEG_INF)
        p = jax.nn.softmax(scores, axis=-1)
        a = p[:, :, 0] - lam * p[:, :, 1]
        return jnp.einsum('bhqs,bshe->bqhe', a.astype(v.dtype), v)

    out = lax.map(block_fn, (qb, jnp.arange(nb)))
    out = jnp.moveaxis(out, 0, 1).reshape(b, s, DIFF_HEADS, DIFF_VDIM)
    out = _rmsnorm(out, subln_g) * (1.0 - lam_init)
    return out.reshape(b, s, DIFF_V)

def _conv_ffn(h, w_up, conv_w, conv_b, w_down):
    u = h @ w_up
    a, g = jnp.split(u, 2, axis=-1)
    s = a.shape[1]
    ap = jnp.pad(a, ((0, 0), (CONV_WIDTH_2 - 1, 0), (0, 0)))
    a = ap[:, 0:s] * conv_w[0] + ap[:, 1:s + 1] * conv_w[1] + ap[:, 2:s + 2] * conv_w[2] + conv_b
    return (jax.nn.gelu(a, approximate=False) * g) @ w_down

def second_inputs(seed: int = 0) -> dict:
    key = jax.random.key(seed)
    ks = jax.random.split(key, 20)
    nrm = lambda k, shape, s: jax.random.normal(k, shape, jnp.float32) * s
    D = D_MODEL
    return {
        "x": nrm(ks[0], (BATCH, SEQ, D), 1.0),
        "c": nrm(ks[1], (BATCH, D), 1.0),
        "w_ada": nrm(ks[2], (DEPTH, D, 6 * D), 0.5 * D ** -0.5),
        "b_ada": nrm(ks[3], (DEPTH, 6 * D), 0.02),
        "norm1_g": 1.0 + nrm(ks[4], (DEPTH, D), 0.02),
        "w_in": nrm(ks[5], (DEPTH, D, IN_COLS), D ** -0.5),
        "swa_sinks": nrm(ks[6], (DEPTH, SWA_HEADS), 1.0),
        "diff_lambda": nrm(ks[7], (DEPTH, 4, HEAD_DIM), 0.1),
        "diff_subln_g": 1.0 + nrm(ks[8], (DEPTH, DIFF_VDIM), 0.02),
        "w_branch_swa": nrm(ks[9], (DEPTH, SWA_Q, D), SWA_Q ** -0.5),
        "w_branch_diff": nrm(ks[10], (DEPTH, DIFF_V, D), DIFF_V ** -0.5),
        "w_out": nrm(ks[11], (DEPTH, D, D), D ** -0.5),
        "norm2_g": 1.0 + nrm(ks[12], (DEPTH, D), 0.02),
        "w_up": nrm(ks[13], (DEPTH, D, 2 * D_FF), D ** -0.5),
        "conv_w": nrm(ks[14], (DEPTH, CONV_WIDTH_2, D_FF), CONV_WIDTH_2 ** -0.5),
        "conv_b": nrm(ks[15], (DEPTH, D_FF), 0.02),
        "w_down": nrm(ks[16], (DEPTH, D_FF, D), D_FF ** -0.5),
        "final_g": 1.0 + nrm(ks[17], (D,), 0.02),
    }

def second_block(x, c, w_ada, b_ada, norm1_g, w_in, swa_sinks, diff_lambda, diff_subln_g,
              w_branch_swa, w_branch_diff, w_out, norm2_g, w_up, conv_w, conv_b, w_down, final_g):
    b, s, _ = x.shape
    sizes = [SWA_Q, SWA_KV, SWA_KV, DIFF_QK, DIFF_QK, DIFF_V, D_MODEL, D_MODEL]
    points = [int(p) for p in np.cumsum(sizes)[:-1]]
    slopes_swa = _alibi_slopes(SWA_HEADS).reshape(SWA_KV_HEADS, SWA_GROUP)
    slopes_diff = _alibi_slopes(DIFF_HEADS)
    cs = jax.nn.silu(c)
    for l in range(DEPTH):
        mod = cs @ w_ada[l] + b_ada[l]
        shift1, scale1, gate1, shift2, scale2, gate2 = [m[:, None, :] for m in jnp.split(mod, 6, axis=-1)]

        h = _rmsnorm(x, norm1_g[l]) * (1.0 + scale1) + shift1
        proj = h @ w_in[l]
        qa, ka, va, qd, kd, vd, ga, gd = jnp.split(proj, points, axis=-1)
        out_a = _sliding_window_attention(
            qa.reshape(b, s, SWA_HEADS, HEAD_DIM),
            ka.reshape(b, s, SWA_KV_HEADS, HEAD_DIM),
            va.reshape(b, s, SWA_KV_HEADS, HEAD_DIM),
            swa_sinks[l], slopes_swa)
        lam_init = 0.8 - 0.6 * math.exp(-0.3 * l)
        lp = diff_lambda[l].astype(jnp.float32)
        lam = jnp.exp(jnp.sum(lp[0] * lp[1])) - jnp.exp(jnp.sum(lp[2] * lp[3])) + lam_init
        out_d = _diff_attention(
            qd.reshape(b, s, DIFF_HEADS, 2, HEAD_DIM),
            kd.reshape(b, s, DIFF_HEADS, 2, HEAD_DIM),
            vd.reshape(b, s, DIFF_HEADS, DIFF_VDIM),
            lam, lam_init, diff_subln_g[l], slopes_diff)
        merged = (jax.nn.sigmoid(ga) * (out_a @ w_branch_swa[l])
                  + jax.nn.sigmoid(gd) * (out_d @ w_branch_diff[l]))
        x = x + gate1 * (merged @ w_out[l])

        h2 = _rmsnorm(x, norm2_g[l]) * (1.0 + scale2) + shift2
        x = x + gate2 * _conv_ffn(h2, w_up[l], conv_w[l], conv_b[l], w_down[l])
    return _rmsnorm(x, final_g)


def setup_inputs(seed=0):
    out = dict(first_inputs(seed))
    for name, value in second_inputs(seed + 1).items():
        if name != "x":
            out[name + "_2"] = value
    return out


def reference(
    x, norm_w, w_in, conv_w, a_log, dt_bias, dn_norm_w, q_norm_w, k_norm_w, rel_bias, w_out,
    c_2, w_ada_2, b_ada_2, norm1_g_2, w_in_2, swa_sinks_2, diff_lambda_2, diff_subln_g_2,
    w_branch_swa_2, w_branch_diff_2, w_out_2, norm2_g_2, w_up_2, conv_w_2, conv_b_2, w_down_2,
    final_g_2,
):
    x = first_block(
        x, norm_w, w_in, conv_w, a_log, dt_bias, dn_norm_w, q_norm_w, k_norm_w, rel_bias, w_out,
    )
    return second_block(
        x, c_2, w_ada_2, b_ada_2, norm1_g_2, w_in_2, swa_sinks_2, diff_lambda_2, diff_subln_g_2,
        w_branch_swa_2, w_branch_diff_2, w_out_2, norm2_g_2, w_up_2, conv_w_2, conv_b_2,
        w_down_2, final_g_2,
    )


_drawn_inputs = setup_inputs


def setup_inputs(seed=0):
    import zlib

    import numpy as np

    out = dict(_drawn_inputs(seed))
    spreads = {}
    factors = {'q_norm_w': 8.0,
     'k_norm_w': 8.0,
     'norm1_g_2': 8.0,
     'swa_sinks_2': 159.012,
     'diff_lambda_2': 2.68,
     'diff_subln_g_2': 30.997,
     'norm2_g_2': 8.0,
     'conv_b_2': 24.741,
     'final_g_2': 22.953}
    for name, (base, spread) in spreads.items():
        noise = np.random.default_rng([zlib.crc32(name.encode()), seed]).standard_normal(out[name].shape)
        drawn = base * np.exp(spread * noise) if base else spread * noise
        out[name] = __import__('jax').numpy.asarray(drawn.astype(out[name].dtype))
    for name, factor in factors.items():
        out[name] = (out[name] * factor).astype(out[name].dtype)
    return out
```

```python
import math
from contextlib import ExitStack

import numpy as np
import concourse.bass as bass
from concourse import mybir

F32 = mybir.dt.float32
F32R = mybir.dt.float32r
ACT = mybir.ActivationFunctionType
ALU = mybir.AluOpType

P = 128
SEQ = 512
D = 1024
KT = D // P
TT = SEQ // P
D_DN, DN_H = 512, 4
ATT_H, HD = 8, 64
D_IN = 4 * D_DN + 2 * DN_H + 4 * 512
IN2 = 4352
DFF = 2816
FT = DFF // P
N_BUCKETS, MAX_DISTANCE = 32, 2048
BLK = 2048
EPS = 1e-6
MASK = -1e30
LAM_INIT = 0.8 - 0.6 * math.exp(0.0)

ROWS_A = {"norm_w": 0, "norm1_g": 8, "norm2_g": 16, "final_g": 24, "c": 32, "dn_norm_w": 40,
          "subln": 41, "q_norm": 42, "k_norm": 43, "conv_w": 44, "conv_b": 92}
NA = 92 + FT
NB = 3 * FT
C_ID, C_ONE, C_INVD, C_INVH, C_BLK, C_TRIU, C_STRIU, C_NM0, C_NMT0, C_LVL = range(10)
N_LVL = 6
NC128 = C_LVL + N_LVL


def t5_bucket(dist):
    max_exact = N_BUCKETS // 2
    d = np.maximum(dist, 1).astype(np.float64)
    large = max_exact + (np.log(d / max_exact) / math.log(MAX_DISTANCE / max_exact)
                         * (N_BUCKETS - max_exact)).astype(np.int32)
    large = np.minimum(large, N_BUCKETS - 1)
    return np.where(dist < max_exact, dist, large).astype(np.int32)


def constants():
    i = np.arange(P)[:, None]
    j = np.arange(P)[None, :]
    c = np.zeros((P, NC128, P), np.float32)
    c[:, C_ID] = i == j
    c[:, C_ONE] = 1.0
    c[:, C_INVD] = 1.0 / D
    c[:, C_INVH] = 1.0 / P
    c[:, C_BLK] = (i // HD == j // HD) / HD
    c[:, C_TRIU] = i <= j
    c[:, C_STRIU] = i < j
    merge = lambda b: (i // (2 * b) == j // (2 * b)) & (i // b == j // b + 1)
    c[:, C_NM0] = -1.0 * merge(1)
    c[:, C_NMT0] = -1.0 * merge(1).T
    for n in range(N_LVL):
        c[:, C_LVL + n] = merge(2 << n)
    d = i - (np.arange(SEQ)[None, :] - 3 * P)
    alibi = np.where(d >= 0, -d, MASK).astype(np.float32)
    d2 = d[:, 2 * P:]
    window = np.where((d2 >= 0) & (d2 < P), -d2, MASK).astype(np.float32)
    dist = SEQ - 1 - np.arange(SEQ + P)
    onehot = np.zeros((N_BUCKETS, SEQ + P), np.float32)
    ok = dist >= 0
    onehot[t5_bucket(dist[ok]), np.arange(SEQ + P)[ok]] = 1.0
    times = (dist <= 128) * 1 + (dist % 4 == 0) * 1 + (dist % 16 == 0) * 1
    logm = np.where(ok & (times > 0), np.log(np.maximum(times, 1)), MASK).astype(np.float32)
    select = np.zeros((P, 95), np.float32)
    select[:, 47] = 1.0
    return {"k_mats": c.reshape(P, NC128 * P), "k_alibi": np.concatenate([alibi, window], 1),
            "k_onehot": onehot, "k_logm": logm[None], "k_select": select}


def build(nc, a, out, toep):
    with ExitStack() as ctx:
        top = [0]

        def at(name, shape, dt=F32, offset=None):
            size = 4 * int(np.prod(shape[1:]))
            if offset is None:
                offset = top[0]
                top[0] += (size + 31) // 32 * 32
            return nc.alloc_sbuf_tensor_at(name, shape, dt, offset=offset), offset + (size + 31) // 32 * 32

        def sb(name, shape, dt=F32):
            return at(name, shape, dt)[0]

        top[0] = (nc.sbuf_base + 31) // 32 * 32
        raw = [sb(f"raw{s}", [P, BLK]) for s in range(2)]
        whi = [sb(f"whi{s}", [P, BLK], F32R) for s in range(2)]
        wlo = [sb(f"wlo{s}", [P, BLK], F32R) for s in range(2)]
        split_at = top[0]
        hh = sb("h_hi", [P, KT, SEQ], F32R)
        hl = sb("h_lo", [P, KT, SEQ], F32R)
        xT = sb("x_res", [P, KT, SEQ])
        mats = sb("mats", [P, NC128, P])
        colA = sb("colA", [P, NA])
        colB = sb("colB", [P, NB])
        modc = sb("modc", [P, 48])
        sc = sb("small", [P, 512])
        U = top[0]

        def m(n):
            return mats[:, n, :]

        ident = m(C_ID)
        eps = sc[:, 0:1]
        lams = sc[:, 1:8]
        sinks = sc[:, 8:16]
        dtb, alog = sc[:, 16:20], sc[:, 20:24]
        qcol, kcol, nw1, dncol, subcol = sc[:, 24:25], sc[:, 25:26], sc[:, 26:34], sc[:, 34:35], sc[:, 35:36]
        g1c, g2c, gfc = sc[:, 36:44], sc[:, 44:52], sc[:, 52:60]
        csil = sc[:, 60:68]
        beta, gdec, gc, egc, tail, bege, glst = (sc[:, 80 + 16 * k:96 + 16 * k] for k in range(7))
        ba_tok = sc[:, 192:224].rearrange("p (c e) -> p c e", c=TT)
        sa, sb_, sr, sl = (sc[:, 224 + 16 * k:240 + 16 * k] for k in range(4))
        ea = sc[:, 288:292]
        mx = [sc[:, 300 + 8 * k:301 + 8 * k] for k in range(4)]
        st = [sc[:, 340 + 8 * k:348 + 8 * k] for k in range(4)]
        select = sc[:, 380:475]

        def col(name, n=0):
            return colA[:, ROWS_A[name] + n:ROWS_A[name] + n + 1]

        top[0] = U
        qkv = sb("dn_qkv", [P, 12, SEQ])
        zs = sb("dn_z", [P, 4, SEQ])
        gate = sb("att_gate", [P, 4, SEQ])
        qk_att = sb("att_qk", [P, 8, SEQ])
        v_att = sb("att_v", [P, 4, SEQ])
        V = top[0]
        x_tok = at("x_tok", [P, TT, D], offset=U)[0]
        h_f1 = [at(f"h_f1{s}", [P, SEQ], offset=U + 16384 + 2048 * s)[0] for s in range(2)]
        baT = at("baT", [2 * DN_H, SEQ], offset=V)[0]
        top[0] = V + 2048
        cv = [sb(f"conv{s}", [P, SEQ]) for s in range(2)]
        sq = [sb(f"sq{s}", [P, SEQ]) for s in range(2)]
        ry = [sb(f"ry{s}", [P, SEQ]) for s in range(2)]
        ryy = [sb(f"ryy{s}", [P, SEQ]) for s in range(2)]
        ada_w = [sb(f"ada_w{s}", [P, D]) for s in range(2)]
        ada_acc = [sb(f"ada_acc{s}", [P, D]) for s in range(2)]
        modrow = sb("modrow", [48, P])
        rowsM = sb("rowsM", [48, P])
        rowsA = sb("rowsA", [NA, P])
        rowsB = sb("rowsB", [NB, P])
        lamrow = sb("lamrow", [P, 4 * HD])
        relT = sb("relT", [N_BUCKETS, ATT_H])
        onehot = sb("onehot", [N_BUCKETS, SEQ + P])
        logm = sb("logm", [ATT_H, SEQ + P])
        brow = sb("brow", [ATT_H, SEQ + P])
        ends = [top[0]]
        top[0] = V
        kbe = sb("dn_kbe", [P, TT, DN_H, P])
        ktail = sb("dn_ktail", [P, TT, DN_H, P])
        vb = sb("dn_vb", [P, TT, DN_H, P])
        attnT = sb("dn_attnT", [P, TT, DN_H, P])
        Dk = [sb(f"dn_D{s}", [P, DN_H, P]) for s in range(2)]
        state = sb("dn_state", [P, DN_H, P])
        toe_at = top[0]
        TOE = 5
        toe = [sb(f"toe{h}", [P, SEQ]) for h in range(TOE)]
        ends.append(top[0])
        X = at("dn_X", [P, TT, DN_H, P], offset=split_at)[0]
        XT = at("dn_XT", [P, TT, DN_H, P], offset=split_at + 8192)[0]
        AT = at("dn_AT", [P, TT, DN_H, P], offset=split_at + 16384)[0]
        P1 = at("dn_P1", [P, TT, DN_H, P], offset=split_at + 24576)[0]
        top[0] = V
        s_a1 = [sb(f"s_a1{s}", [P, SEQ]) for s in range(2)]
        p_a1 = [sb(f"p_a1{s}", [P, SEQ]) for s in range(2)]
        pT_a1 = [sb(f"pT_a1{s}", [P, SEQ]) for s in range(2)]
        mixf = [sb(f"mixf{s}", [P, SEQ]) for s in range(2)]
        nsq = [sb(f"nsq{s}", [P, SEQ]) for s in range(2)]
        nry = [sb(f"nry{s}", [P, SEQ]) for s in range(2)]
        nhf = [sb(f"nhf{s}", [P, SEQ]) for s in range(2)]
        top[0] = U
        q_a2 = sb("swa_q", [P, 4, SEQ])
        k_a2 = sb("swa_k", [P, 2, SEQ])
        v_a2 = sb("swa_v", [P, TT, P])
        q_a3 = sb("diff_q", [P, 4, SEQ])
        k_a3 = sb("diff_k", [P, 4, SEQ])
        v_a3 = sb("diff_v", [P, TT, SEQ])
        vf = sb("v_fm", [P, 5, SEQ])
        sg = sb("gates", [P, 16, SEQ])
        s_a3 = [sb(f"s_a3{s}", [P, SEQ]) for s in range(4)]
        p_a3 = [sb(f"p_a3{s}", [P, SEQ]) for s in range(2)]
        pT_a3 = [sb(f"pT_a3{s}", [P, SEQ]) for s in range(2)]
        of = [sb(f"of{s}", [P, SEQ]) for s in range(2)]
        osq = sb("osq", [P, SEQ])
        ory = [sb(f"ory{s}", [P, SEQ]) for s in range(2)]
        ends.append(top[0])
        abase = sb("abase", [P, SEQ + 2 * P])
        bias2 = [sb(f"bias2{s}", [P, SEQ]) for s in range(2)]
        ends.append(top[0])
        top[0] = U
        mh = sb("merged_hi", [P, KT, SEQ], F32R)
        ml = sb("merged_lo", [P, KT, SEQ], F32R)
        top[0] = V + 16384
        mA, mD, mS = ([sb(f"m{k}{s}", [P, SEQ]) for s in range(2)] for k in "ADS")
        top[0] = U
        fh = sb("ffn_hi", [P, FT, SEQ], F32R)
        fl = sb("ffn_lo", [P, FT, SEQ], F32R)
        top[0] = V + 16384 + 6 * 2048
        fc = [sb(f"fc{s}", [P, SEQ]) for s in range(2)]
        fg = [sb(f"fg{s}", [P, SEQ]) for s in range(2)]
        ff = [sb(f"ff{s}", [P, SEQ]) for s in range(2)]
        ends.append(top[0])
        top[0] = U
        yT = sb("yT", [P, KT, SEQ])
        y_tok = sb("y_tok", [P, TT, D])
        assert max(ends) <= nc.sbuf_usable_end

        bank = [ctx.enter_context(nc.psum_tensor(f"bank{b}", [P, SEQ], F32)) for b in range(8)]

        def four(ap):
            return ap.rearrange("p (h i) -> p h i", h=4)

        def over(ap, n=P):
            return ap.rearrange("p (h o) -> p h o", o=1).to_broadcast([P, 4, n])

        def each(ap):
            return ap.rearrange("p (o i) -> p o i", o=1).to_broadcast([P, 4, P])

        class Signals(dict):

            def __missing__(self, name):
                self[name] = ctx.enter_context(nc.semaphore(name))
                return self[name]

        S = Signals()

        def before(tag, what):
            n = int(tag[1])
            if tag[0] == "n":
                return n if what == "rs" else KT * n - KT * (n > 0 and what == "aff")
            return (n - 1) * (4 if what in ("out", "hi", "lo") else 32)

        class Chain:

            def __init__(self, eng, name):
                self.eng, self.sem, self.n = eng, S[name], 0

            def __call__(self, ins):
                ins.then_inc(self.sem, 1)
                self.n += 1
                self.eng.wait_ge(self.sem, self.n)

        w_in = a["w_in"][0].rearrange("(k p) c -> p k c", p=P)
        w_out = a["w_out"][0].rearrange("(k p) c -> p k c", p=P)
        w_in2 = a["w_in_2"][0].rearrange("(k p) c -> p k c", p=P)
        w_out2 = a["w_out_2"][0].rearrange("(k p) c -> p k c", p=P)
        w_bs = a["w_branch_swa_2"][0].rearrange("(k p) c -> p k c", p=P)
        w_bd = a["w_branch_diff_2"][0].rearrange("(k p) c -> p k c", p=P)
        w_up = a["w_up_2"][0].rearrange("(k p) c -> p k c", p=P)
        w_dn = a["w_down_2"][0].rearrange("(k p) c -> p k c", p=P)
        N_S1, N_S2, N_S3, N_S4, N_S5, N_S6 = 17, 21, 38, 42, 46, 68
        T_S1, T_S2, T_S3, T_S4, T_S5 = 33, 41, 75, 91, 99
        ADA_STEP = {5: 3, 6: 2, 7: 7, 8: 7, 9: 3, 10: 2, 11: 2, 12: 2, 13: 4, 14: 5, 15: 6, 16: 5}
        OFFS = [256 * n for n in range(6)] + [2048] + [1536, 1792] + [2056 + 256 * n for n in range(8)]

        def norm_of(n):
            if n < 4:
                return [2 * n, 2 * n + 1]
            return [8 + 2 * (n - 9), 9 + 2 * (n - 9)] if 9 <= n < 13 else []

        def tiles_of(n):
            return [2 * n, 2 * n + 1] if n < 6 else [12] if n == 6 else [13 + 2 * (n - 7), 14 + 2 * (n - 7)]

        def fold_at(n):
            before = sum(v for k, v in ADA_STEP.items() if k < n - 1)
            after = sum(v for k, v in ADA_STEP.items() if k < n)
            return range(before // 8, after // 8)

        block = ctx.enter_context(nc.Block())

        @block.sync
        def _(sp):
            def weights(n, dsts, i=0):
                s, use = n % 2, n // 2 + i
                if n >= 2:
                    sp.wait_ge(S["hi_ready"], n - 1 + 2 * i)
                    sp.wait_ge(S["lo_ready"], n - 1 + 2 * i)
                for dst, src in dsts(raw[s]):
                    sp.dma_start(dst, src).then_inc(S[f"raw_full{s}"], 16)

            def cols(w, c, width=256):
                def dsts(r):
                    v = r[:, :].rearrange("p (k c) -> p k c", k=KT)
                    return [(v[:, 4 * h:4 * h + 4, 0:width], w[:, 4 * h:4 * h + 4, bass.ds(c, width)])
                            for h in range(2)]
                return dsts

            sp.dma_start(mats[:, C_ID, :], a["k_mats"][:, 0:P]).then_inc(S["x_in_ident"], 16)
            for t in range(TT):
                sp.dma_start(x_tok[:, t, :], a["x"][0, t * P:(t + 1) * P, :]).then_inc(S[f"x_in{t}"], 16)
            for n in range(17):
                if n == 6:
                    weights(n, cols(w_in, OFFS[n], P))
                else:
                    weights(n, cols(w_in, OFFS[n]))
            for j in range(4):
                weights(N_S1 + j, cols(w_out, 256 * j))
            with sp.Fori(0, 8) as i:
                for s in range(2):
                    weights(N_S2 + s, cols(w_in2, 512 * i + 256 * s), i)
            weights(N_S2 + 16, cols(w_in2, 4096))
            for j in range(4):
                def both(r, j=j):
                    v = r[:, :].rearrange("p (g k c) -> p g k c", g=2, k=4)
                    return [(v[:, 0], w_bs[:, :, 256 * j:256 * j + 256]),
                            (v[:, 1], w_bd[:, :, 256 * j:256 * j + 256])]
                weights(N_S3 + j, both)
            for j in range(4):
                weights(N_S4 + j, cols(w_out2, 256 * j))
            with sp.Fori(0, 11) as i:
                for s in range(2):
                    def pair(r, s=s):
                        v = r[:, :].rearrange("p (k g c) -> p k g c", k=KT, g=2)
                        return [(v[:, :, g, :], w_up[:, :, bass.ds(g * DFF + s * P + 2 * P * i, P)])
                                for g in range(2)]
                    weights(N_S5 + s, pair, i)

            def down(n, i=0):
                def rows(r):
                    v = r[:, :].rearrange("p (k c) -> p k c", k=2)
                    j = n - N_S6
                    return [(v[:, h, :], w_dn[:, bass.ds(2 * j + h + 4 * i, 1), :].rearrange("p k c -> p (k c)"))
                            for h in range(2)]
                weights(n, rows, i)

            with sp.Fori(0, 5) as i:
                for s in range(2):
                    down(N_S6 + s, i)
            down(N_S6 + 10)
            for t in range(TT):
                for h in range(2):
                    sp.wait_ge(S[f"y_out{h}"], t + 1)
                    sp.dma_start(out[0, t * P:(t + 1) * P, h * 512:(h + 1) * 512],
                                 y_tok[:, t, h * 512:(h + 1) * 512]).then_inc(S["out_done"], 16)
            sp.wait_ge(S["out_done"], 16 * 2 * TT)

        @block.gpsimd
        def _(pool):
            pool.dma_start(relT[:, :], a["rel_bias"].rearrange("h b -> b h"), allow_slow_non_contiguous=True).then_inc(S["in_rel"], 16)
            pool.dma_start(onehot[:, :], a["k_onehot"]).then_inc(S["in_rel"], 16)
            pool.dma_start(logm[:, :], a["k_logm"].to_broadcast([ATT_H, SEQ + P])).then_inc(S["in_rel"], 16)
            pool.dma_start(rowsM[:, :], a["b_ada_2"].rearrange("o (j p) -> (o j) p", p=P)).then_inc(S["in_rowsM"], 16)
            for p in range(48):
                if p >= 2:
                    pool.wait_ge(S["ada_piece"], p - 1)
                c, kt = divmod(p, KT)
                pool.dma_start(ada_w[p % 2][:, :], a["w_ada_2"][0, kt * P:(kt + 1) * P, c * D:(c + 1) * D])\
                    .then_inc(S[f"ada_in{p % 2}"], 16)
            pool.wait_ge(S["mod_ready"], 1)
            pool.wait_ge(S["toep_out"], 16)
            for h in range(ATT_H):
                if h >= TOE:
                    pool.wait_ge(S["att_s"], before("a1", "s") + 4 * (h - TOE + 1))
                pool.dma_start(toe[h % TOE][:, :],
                               bass.AP(toep.tensor, h * P * (SEQ + P) + P - 1, [[SEQ + P - 1, P], [1, SEQ]]))\
                    .then_inc(S[f"toe_in{h % TOE}"], 16)
            pool.wait_ge(S["att_out"], before("a1", "out") + 4)
            pool.dma_start(abase[:, :], a["k_alibi"]).then_inc(S["in_alibi"], 16)
            pool.wait_ge(S["in_alibi"], 16)
            for g in range(ATT_H + DN_H):
                if g >= 2:
                    done = 4 * (g - 1)
                    if g - 2 >= ATT_H:
                        pool.wait_ge(S["att_s"], before("a3", "s") + 8 * (g - 1 - ATT_H))
                    else:
                        pool.wait_ge(S["att_s"], before("a2", "s") + done)
                if g < ATT_H:
                    pool.tensor_scalar(bias2[g % 2][:, 0:256], abase[:, SEQ:], 2.0 ** -(g + 1), None, ALU.mult)\
                        .then_inc(S["bias_ready"], 1)
                else:
                    pool.tensor_scalar(bias2[g % 2][:, :], abase[:, 0:SEQ], 2.0 ** (-2 * (g - ATT_H + 1)), None,
                                       ALU.mult).then_inc(S["bias_ready"], 1)

        def units_a1():
            for h in range(ATT_H):
                for i in range(TT):
                    r = slice(64 * (h % 2), 64 * (h % 2) + 64)
                    yield dict(maps=[dict(q=qk_att[r, h // 2, i * P:(i + 1) * P], k=qk_att[r, 4 + h // 2, 0:(i + 1) * P],
                                          bias=toe[h % TOE][:, (3 - i) * P:], sink=None)],
                               n=i + 1, v=[v_att[:, j, h * HD:(h + 1) * HD] for j in range(i + 1)],
                               out=(r, slice(i * P, (i + 1) * P)), group=h // 2, last=h % 2 == 1 and i == 3,
                               head=h, new=(h % 2, i) == (0, 0))

        def units_a2():
            for h in range(ATT_H):
                for i in range(TT):
                    r = slice(64 * (h % 2), 64 * (h % 2) + 64)
                    j0 = max(i - 1, 0)
                    yield dict(maps=[dict(q=q_a2[r, h // 2, i * P:(i + 1) * P], k=k_a2[r, h // 4, j0 * P:(i + 1) * P],
                                          bias=bias2[h % 2][:, (1 - (i - j0)) * P:2 * P], sink=sinks[:, h:h + 1])],
                               n=i + 1 - j0, v=[v_a2[:, j, (h // 4) * HD:(h // 4 + 1) * HD] for j in range(j0, i + 1)],
                               out=(r, slice(i * P, (i + 1) * P)), group=h // 2, last=h % 2 == 1 and i == 3,
                               head=h, new=(h % 2, i) == (0, 0))

        def units_a3():
            for h in range(DN_H):
                for i in range(TT):
                    yield dict(maps=[dict(q=q_a3[64 * mp:64 * mp + 64, h, i * P:(i + 1) * P],
                                          k=k_a3[64 * mp:64 * mp + 64, h, 0:(i + 1) * P],
                                          bias=bias2[h % 2][:, (3 - i) * P:], sink=None) for mp in range(2)],
                               n=i + 1, v=[v_a3[:, j, h * P:(h + 1) * P] for j in range(i + 1)],
                               out=(slice(0, P), slice(i * P, (i + 1) * P)), group=h, last=i == 3,
                               head=h, new=i == 0)

        QK, TB, OB = (2, 3), (4, 5), (6, 7)
        bufs = {"a1": (s_a1, p_a1, pT_a1), "a2": (s_a3, p_a3, pT_a3), "a3": (s_a3, p_a3, pT_a3)}

        def tiles_through(n):
            if n < N_S1:
                return tiles_of(n)[-1] + 1
            for first, T, per in ((N_S5, T_S5, 2), (N_S4, T_S4, 2), (N_S3, T_S3, 4), (N_S2, T_S2, 2), (N_S1, T_S1, 2)):
                if n >= first:
                    return T + per * (n - first + 1)

        def slot_free(eng, n, i=0):
            if n >= N_S6 + 2:
                eng.wait_ge(S["block_done"], n - N_S6 - 1 + 2 * i)
            elif n >= 2:
                eng.wait_ge(S["tile_ready"], tiles_through(n - 2) + 4 * i)

        def evac(eng, T, i=0, per=2):
            eng.wait_ge(S[f"evac{T % 2}"], T // 2 + 1 + per * i)

        @block.tensor
        def _(pe):
            def bank_free(T, i=0, per=0):
                if T >= 2:
                    pe.wait_ge(S[f"evac{T % 2}"], T // 2 + per * i)

            def three(ps, lo, wcol, h_hi, h_lo, start, stop):
                wh, wl = whi[lo][:, wcol:wcol + P], wlo[lo][:, wcol:wcol + P]
                pe.matmul(ps, wh, h_hi, start=start, stop=False)
                pe.matmul(ps, wh, h_lo, start=False, stop=False)
                return pe.matmul(ps, wl, h_hi, start=False, stop=stop)

            def gemm(n, T, us=(0, 1), acts=None, ks=KT, stride=256, first=0, ready=None, i=0, per=0):
                ah, al = acts or (hh, hl)
                pe.wait_ge(S["lo_ready"], n + 1 + 2 * i)
                for k, u in enumerate(us):
                    bank_free(T + k, i, per)
                    for kt in range(ks):
                        if ready and k == 0:
                            pe.wait_ge(ready[0], ready[1] + kt)
                        mm = three(bank[(T + k) % 2][:, :], n % 2, kt * stride + u * P + first,
                                   ah[:, kt, :], al[:, kt, :], kt == 0, kt == ks - 1)
                    mm.then_inc(S["tile_ready"], 1)

            def norm_sum(tag, b, kt):
                pe.wait_ge(S["rms_sq"], before(tag, "sq") + kt + 1)
                pe.matmul(bank[b][:, :], m(C_INVD), (sq if tag == "n0" else nsq)[kt % 2][:, :],
                          start=kt == 0, stop=kt == KT - 1).then_inc(S["rms_sum"], 1)

            pe.wait_ge(S["x_in_ident"], 16)
            for t in range(TT):
                pe.wait_ge(S[f"x_in{t}"], 16)
            for kt in range(KT):
                for t in range(TT):
                    mm = pe.transpose(bank[kt][:, t * P:(t + 1) * P], x_tok[:, t, kt * P:(kt + 1) * P], ident)
                mm.then_inc(S["xt_done"], 1)
            pe.wait_ge(S["xT_ready"], 3)
            pe.wait_ge(S["in_rowsA"], 16 * 13)
            pe.transpose(bank[1][:, 0:NA], rowsA[:, :], ident[0:NA, 0:NA]).then_inc(S["vecs_done"], 1)
            pe.wait_ge(S["in_rowsB"], 16)
            pe.transpose(bank[2][:, 0:NB], rowsB[:, :], ident[0:NB, 0:NB]).then_inc(S["vecs_done"], 1)
            pe.wait_ge(S["in_mats"], 16)
            for kt in range(KT):
                norm_sum("n0", 0, kt)
            pe.wait_ge(S["xT_ready"], 5)
            pe.wait_ge(S["in_rel"], 48)
            pe.matmul(bank[3][0:ATT_H, :], relT[:, :], onehot[:, 0:SEQ], start=True, stop=True)
            pe.matmul(bank[4][0:ATT_H, 0:P], relT[:, :], onehot[:, SEQ:], start=True, stop=True)\
                .then_inc(S["rel_done"], 1)

            def fold(c):
                pe.wait_ge(S["ada_piece"], 8 * (c + 1))
                for j in range(8):
                    jj = 8 * c + j
                    mm = pe.matmul(bank[5][0:48, 0:P], select[:, 47 - jj:95 - jj], ada_acc[c % 2][:, j * P:(j + 1) * P],
                                   start=jj == 0, stop=jj == 47)
                mm.then_inc(S["ada_fold"], 1)

            for n in range(17):
                if n == 0:
                    pe.wait_ge(S["rms_hf"], before("n0", "hf") + 1)
                    pe.wait_ge(S["xT_ready"], 8)
                    pe.wait_ge(S["cols_ready"], 2)
                gemm(n, tiles_of(n)[0], (0,) if n == 6 else (0, 1), ready=(S["rms_lo"], before("n0", "lo") + 1) if n == 0 else None)
                if n >= 1:
                    for k in norm_of(n - 1):
                        pe.wait_ge(S["sq_done"], k + 1)
                        if k == 0:
                            pe.wait_ge(S["brow_ready"], 2)
                        if k >= 2:
                            pe.wait_ge(S["nt_done"], k - 1)
                        pe.matmul(bank[2 + k % 2][:, :], m(C_ONE if k < 8 else C_BLK), sq[k % 2][:, :],
                                  start=True, stop=True).then_inc(S["sum_done"], 1)
                if n == 7:
                    pe.wait_ge(S["evac0"], 7)
                    pe.wait_ge(S["brow_ready"], 2)
                    for t in range(TT):
                        mm = pe.transpose(bank[4][:, 8 * t:8 * t + 8], baT[:, t * P:(t + 1) * P], ident[0:8, 0:8])
                    mm.then_inc(S["ba_tr"], 1)
                for c in fold_at(n):
                    if c == 0:
                        pe.wait_ge(S["xT_ready"], 8)
                    fold(c)
            for c in fold_at(17):
                fold(c)
            pe.wait_ge(S["modrow_ready"], 1)
            pe.transpose(bank[4][:, 0:48], modrow[:, :], ident[0:48, 0:48]).then_inc(S["mod_tr"], 1)
            pe.wait_ge(S["nt_done"], 16)
            pe.wait_ge(S["evac0"], 15)
            pe.wait_ge(S["evac1"], 14)
            for t in range(TT):
                for f in range(4):
                    mm = pe.transpose(bank[(2, 3, 6, 7)[t]][:, f * P:(f + 1) * P], v_att[:, f, t * P:(t + 1) * P], ident)
            mm.then_inc(S["v_tr"], 1)

            pe.wait_ge(S["norm_done"], 8)
            pe.wait_ge(S["g_ready"], 1)
            pe.matmul(bank[5][:, 0:16], m(C_TRIU), gdec, start=True, stop=True).then_inc(S["dn_gct"], 1)
            pe.wait_ge(S["v_ready"], 4)
            pe.wait_ge(S["evac0"], 17)
            pe.wait_ge(S["evac1"], 16)
            for c in range(TT):
                pe.wait_ge(S["dn_gtri"], 2 * c + 2)
                if c >= 2:
                    pe.wait_ge(S["dn_exp"], c - 1)
                    pe.wait_ge(S["dn_dtb"], c - 1)
                pe.matmul(bank[c % 2][:, :], m(C_ONE), P1[:, c % 2].rearrange("p h i -> p (h i)"), start=True, stop=True)\
                    .then_inc(S["dn_grow"], 1)
                pe.matmul(bank[2 + c % 2][:, :], m(C_ONE), P1[:, 2 + c % 2].rearrange("p h i -> p (h i)"),
                          start=True, stop=True).then_inc(S["dn_brow"], 1)
                if c == 0:
                    pe.wait_ge(S["dn_egc"], 1)
                    pe.wait_ge(S["mod_ready"], 1)
                if c >= 1:
                    pe.wait_ge(S["dn_at"], 2 * c)
                tok = slice(c * P, (c + 1) * P)
                for h in range(DN_H):
                    pe.matmul(bank[5][:, h * P:(h + 1) * P], qkv[:, 4 + h, tok], qkv[:, 4 + h, tok], start=True, stop=True)
                for h in range(DN_H):
                    mm = pe.matmul(bank[6][:, h * P:(h + 1) * P], qkv[:, 4 + h, tok], qkv[:, h, tok], start=True, stop=True)
                mm.then_inc(S["dn_prod"], 1)
                for b, f in ((4, 4), (7, 8)):
                    if c >= 1:
                        pe.wait_ge(S["dn_kv"], 2 * c if b == 4 else 2 * c)
                    if b == 7 and c >= 1:
                        pe.wait_ge(S["dn_x"], c)
                    for h in range(DN_H):
                        mm = pe.transpose(bank[b][:, h * P:(h + 1) * P], qkv[:, f + h, tok], ident)
                    mm.then_inc(S["dn_ktr"], 1)
                pe.wait_ge(S["dn_at"], 2 * c + 1)
                pe.wait_ge(S["dn_kv"], 2 * c + 2)
                for h in range(DN_H):
                    mm = pe.transpose(bank[7][:, h * P:(h + 1) * P], AT[:, c, h, :], ident)
                mm.then_inc(S["dn_a"], 1)

            def prod1(l, c):
                pe.wait_ge(S["dn_x"] if l == 0 else S["dn_upd"], 4 if l == 0 else 4 * (l - 1) + c + 1)
                if l == 0:
                    pe.wait_ge(S["dn_dtb"], 4)
                for h in range(DN_H):
                    mm = pe.matmul(bank[c % 2][:, h * P:(h + 1) * P], AT[:, c, h, :], X[:, c, h, :], start=True, stop=True)
                mm.then_inc(S["dn_p1"], 1)

            def prod2(l, c):
                pe.wait_ge(S["dn_p1s"], 4 * l + c + 1)
                if l * 4 + c >= 2:
                    pe.wait_ge(S["dn_upd"], 4 * l + c - 1)
                for h in range(DN_H):
                    if l < N_LVL - 1:
                        pe.matmul(bank[2 + c % 2][:, h * P:(h + 1) * P], XT[:, c, h, :], P1[:, c, h, :], start=True, stop=True)
                for h in range(DN_H):
                    mm = pe.matmul(bank[4 + c % 2][:, h * P:(h + 1) * P], P1[:, c, h, :], XT[:, c, h, :], start=True, stop=True)
                mm.then_inc(S["dn_z"], 1)

            for l in range(N_LVL):
                prod1(l, 0)
                for c in range(TT):
                    if c + 1 < TT:
                        prod1(l, c + 1)
                    prod2(l, c)
            for c in range(TT):
                pe.wait_ge(S["dn_upd"], 4 * (N_LVL - 1) + c + 1)
                if c >= 1:
                    pe.wait_ge(S["dn_u"], c)
                    pe.wait_ge(S["dn_w"], c)
                for h in range(DN_H):
                    pe.matmul(bank[6][:, h * P:(h + 1) * P], XT[:, c, h, :], vb[:, c, h, :], start=True, stop=True)
                for h in range(DN_H):
                    mm = pe.matmul(bank[7][:, h * P:(h + 1) * P], kbe[:, c, h, :], XT[:, c, h, :], start=True, stop=True)
                mm.then_inc(S["dn_uw"], 1)
            for c in range(TT):
                tok = slice(c * P, (c + 1) * P)
                if c >= 1:
                    pe.wait_ge(S["dn_s"], c)
                    for h in range(DN_H):
                        mm = pe.matmul(bank[0][:, h * P:(h + 1) * P], kbe[:, c, h, :], state[:, h, :], start=True, stop=True)
                    mm.then_inc(S["dn_ws"], 1)
                pe.wait_ge(S["dn_vn"], c + 1)
                if c < TT - 1:
                    for h in range(DN_H):
                        mm = pe.matmul(bank[1][:, h * P:(h + 1) * P], ktail[:, c, h, :], P1[:, c % 2, h, :], start=True, stop=True)
                    mm.then_inc(S["dn_su"], 1)
                ob = (4, 5, 6, 7)[c]
                if c == 0:
                    pe.wait_ge(S["dn_u"], 4)
                    pe.wait_ge(S["dn_w"], 4)
                for h in range(DN_H):
                    if c >= 1:
                        pe.matmul(bank[ob][:, h * P:(h + 1) * P], state[:, h, :], qkv[:, h, tok], start=True, stop=False)
                    mm = pe.matmul(bank[ob][:, h * P:(h + 1) * P], P1[:, c % 2, h, :], attnT[:, c, h, :],
                                   start=c == 0, stop=True)
                mm.then_inc(S["dn_o"], 1)
            for c in range(TT):
                pe.wait_ge(S["dn_osq"], c + 1)
                if c >= 2:
                    pe.wait_ge(S["dn_mix"], c - 1)
                pe.matmul(bank[2 + c % 2][:, :], m(C_INVH), Dk[c % 2][:, :, :].rearrange("p h i -> p (h i)"),
                          start=True, stop=True).then_inc(S["dn_osum"], 1)
            pe.wait_ge(S["dn_lo"], 4)

            def attention(tag, units, tail=None):
                units = list(units)
                p_, pT_ = bufs[tag][1:]
                M = len(units[0]["maps"])
                maps = [mp for u in units for mp in u["maps"]]

                def qk(g):
                    if g >= len(maps):
                        return
                    if g >= 2:
                        pe.wait_ge(S["att_s"], before(tag, "s") + g - 1)
                    mp = maps[g]
                    pe.matmul(bank[QK[g % 2]][:, 0:mp["k"].shape[-1]], mp["q"], mp["k"], start=True, stop=True)\
                        .then_inc(S["att_qk"], 1)

                def turn(w):
                    pe.wait_ge(S["att_p"], before(tag, "p") + w + 1)
                    if w >= 2:
                        pe.wait_ge(S["att_pT"], before(tag, "pT") + w - 1)
                    for j in range(units[w]["n"]):
                        mm = pe.transpose(bank[TB[w % 2]][:, j * P:(j + 1) * P], p_[w % 2][:, j * P:(j + 1) * P], ident)
                    mm.then_inc(S["att_t"], 1)

                def values(w):
                    u = units[w]
                    pe.wait_ge(S["att_pT"], before(tag, "pT") + w + 1)
                    if u["new"] and u["group"] >= 2:
                        pe.wait_ge(S["att_out"], before(tag, "out") + u["group"] - 1)
                    r, c = u["out"]
                    for j in range(u["n"]):
                        mm = pe.matmul(bank[OB[u["group"] % 2]][r, c], u["v"][j], pT_[w % 2][:, j * P:(j + 1) * P],
                                       start=j == 0, stop=j == u["n"] - 1)
                    mm.then_inc(S["att_pv"], 1)

                qk(0)
                qk(1)
                for w in range(len(units)):
                    for g in range(M * w + 2, M * w + M + 2):
                        qk(g)
                    turn(w)
                    if w >= 1:
                        values(w - 1)
                    if tail:
                        tail(w)
                values(len(units) - 1)
                if tail:
                    tail(len(units))
                    tail(len(units) + 1)

            attention("a1", units_a1())

            for j in range(4):
                if j == 0:
                    pe.wait_ge(S["att_lo"], before("a1", "lo") + 4)
                gemm(N_S1 + j, T_S1 + 2 * j)
                for kt in (2 * j - 2, 2 * j - 1):
                    if kt >= 0:
                        norm_sum("n1", 2, kt)
            norm_sum("n1", 2, 6)
            norm_sum("n1", 2, 7)

            gemm(N_S2, T_S2, ready=(S["rms_lo"], before("n1", "lo") + 1))
            for j in range(1, 9):
                gemm(N_S2 + j, T_S2 + 2 * j)
            with pe.Fori(0, 4) as i:
                for s in range(2):
                    gemm(N_S2 + 9 + s, T_S2 + 18 + 2 * s, i=i, per=2)
            pe.wait_ge(S["evac0"], (T_S2 + 17) // 2 + 1)
            pe.wait_ge(S["evac1"], (T_S2 + 16) // 2 + 1)
            for t in range(TT):
                pe.transpose(bank[6][:, t * P:(t + 1) * P], vf[:, 0, t * P:(t + 1) * P], ident)
            for t in range(TT):
                for f in range(4):
                    mm = pe.transpose(bank[2 + t][:, f * P:(f + 1) * P], vf[:, 1 + f, t * P:(t + 1) * P], ident)
            mm.then_inc(S["v2_tr"], 1)
            pe.wait_ge(S["v2_ready"], 5)
            attention("a2", units_a2())
            pe.wait_ge(S["att_lo"], before("a2", "lo") + 4)

            def diff_norm(w):
                if w >= 5 and (w - 5) % 4 == 0:
                    h = (w - 5) // 4
                    pe.wait_ge(S["d_sq"], h + 1)
                    if h == 0:
                        pe.wait_ge(S["evac0"], T_S3 // 2 + 1)
                    pe.matmul(bank[0][:, :], m(C_INVH), osq[:, :], start=True, stop=True).then_inc(S["d_sum"], 1)

            attention("a3", units_a3(), diff_norm)

            pe.wait_ge(S["att_lo"], before("a3", "lo") + 4)
            for j in range(4):
                pe.wait_ge(S["lo_ready"], N_S3 + j + 1)
                for u in range(2):
                    for g in range(2):
                        T = T_S3 + 4 * j + 2 * u + g
                        bank_free(T)
                        for kt in range(4):
                            mm = three(bank[T % 2][:, :], (N_S3 + j) % 2, g * 1024 + kt * 256 + u * P,
                                       hh[:, 4 * g + kt, :], hl[:, 4 * g + kt, :], kt == 0, kt == 3)
                        mm.then_inc(S["tile_ready"], 1)
            for j in range(4):
                gemm(N_S4 + j, T_S4 + 2 * j, acts=(mh, ml), ready=(S["mg_lo"], 1) if j == 0 else None)
                for kt in (2 * j - 2, 2 * j - 1):
                    if kt >= 0:
                        norm_sum("n2", 2, kt)
            norm_sum("n2", 2, 6)
            norm_sum("n2", 2, 7)
            pe.wait_ge(S["rms_lo"], before("n2", "lo") + 8)
            with pe.Fori(0, 11) as i:
                for s in range(2):
                    gemm(N_S5 + s, T_S5 + 2 * s, i=i, per=2)
            pe.wait_ge(S["evac0"], (T_S5 + 44 + 1) // 2)
            pe.wait_ge(S["evac1"], (T_S5 + 44) // 2)
            pe.wait_ge(S["f_lo"], FT)

            def down(n, i=0, start=False, stop=False):
                pe.wait_ge(S["lo_ready"], n + 1 + 2 * i)
                for t in range(KT):
                    for h in range(2):
                        kt = bass.ds(2 * (n - N_S6) + h + 4 * i, 1)
                        mm = three(bank[t][:, :], n % 2, h * 1024 + t * P,
                                   fh[:, kt, :].rearrange("p k c -> p (k c)"), fl[:, kt, :].rearrange("p k c -> p (k c)"),
                                   start and h == 0, stop and h == 1)
                    if stop:
                        mm.then_inc(S["tile_ready"], 1)
                if not stop:
                    mm.then_inc(S["block_done"], 1)

            down(N_S6, start=True)
            with pe.Fori(0, 4) as i:
                down(N_S6 + 1, i)
                down(N_S6 + 2, i)
            down(N_S6 + 9)
            down(N_S6 + 10, stop=True)
            pe.wait_ge(S["x3_ready"], 1)
            for kt in range(KT):
                norm_sum("n3", 0, kt)
            for t in range(TT):
                for h in range(2):
                    k = 2 * t + h
                    if k == 0:
                        pe.wait_ge(S["x3_ready"], 8)
                    for f in range(4):
                        pe.wait_ge(S["y_ready"], 4 * h + f + 1)
                        mm = pe.transpose(bank[(k + 1) % 8][:, f * P:(f + 1) * P], yT[:, 4 * h + f, t * P:(t + 1) * P], ident)
                    mm.then_inc(S["y_tr"], 1)

        @block.scalar
        def _(act):
            link = Chain(act, "act_chain")

            def rows(name, src):
                n = ROWS_A[name]
                act.dma_start(rowsA[n:n + src.shape[0], :], src).then_inc(S["in_rowsA"], 16)

            vec = lambda ap: ap.rearrange("o (k p) -> (o k) p", p=P)
            rows("norm_w", vec(a["norm_w"]))
            act.dma_start(mats[:, 1:, :].rearrange("p n c -> p (n c)"), a["k_mats"][:, P:]).then_inc(S["in_mats"], 16)
            rows("norm1_g", vec(a["norm1_g_2"]))
            rows("norm2_g", vec(a["norm2_g_2"]))
            rows("final_g", a["final_g_2"].rearrange("(k p) -> k p", p=P))
            rows("c", vec(a["c_2"]))
            rows("dn_norm_w", a["dn_norm_w"])
            rows("subln", a["diff_subln_g_2"])
            rows("conv_w", a["conv_w"][0].rearrange("k (t p) -> (k t) p", p=P))
            rows("conv_b", vec(a["conv_b_2"]))
            for name, ap in (("q_norm", a["q_norm_w"]), ("k_norm", a["k_norm_w"])):
                n = ROWS_A[name]
                for h in range(2):
                    act.dma_start(rowsA[n:n + 1, h * HD:(h + 1) * HD], ap).then_inc(S["in_rowsA"], 16)
            act.dma_start(rowsB[:, :], a["conv_w_2"][0].rearrange("k (t p) -> (k t) p", p=P)).then_inc(S["in_rowsB"], 16)
            act.dma_start(select, a["k_select"]).then_inc(S["in_small"], 16)
            act.dma_start(sinks, a["swa_sinks_2"].to_broadcast([P, 8])).then_inc(S["in_small"], 16)
            act.dma_start(dtb, a["dt_bias"].to_broadcast([P, DN_H])).then_inc(S["in_small"], 16)
            act.dma_start(alog, a["a_log"].to_broadcast([P, DN_H])).then_inc(S["in_small"], 16)
            act.dma_start(lamrow[:, :], a["diff_lambda_2"].rearrange("o f d -> o (f d)").to_broadcast([P, 4 * HD]))\
                .then_inc(S["in_small"], 16)

            def hi(n, i=0):
                s = n % 2
                act.wait_ge(S[f"raw_full{s}"], 32 * (n // 2 + 1) + 32 * i)
                slot_free(act, n, i)
                act.activation(whi[s][:, :], raw[s][:, :], ACT.Copy).then_inc(S["hi_ready"], 1)

            def squares(tag, kt, src, buf):
                if kt >= 2:
                    act.wait_ge(S["rms_sum"], before(tag, "sum") + kt - 1)
                act.activation(buf[kt % 2][:, :], src, ACT.Square).then_inc(S["rms_sq"], 1)

            def rsqrt(ps, y, yy, done):
                act.preload_act_table_set("natural_log_exp_and_others")
                link(act.activation(yy, ps, ACT.Ln, bias=eps))
                link(act.activation(y, yy, ACT.Exp, scale=-0.5))
                act.activation(yy, y, ACT.Square).then_inc(S[done], 1)

            act.wait_ge(S["scal_done"], 1)
            for kt in range(KT):
                act.wait_ge(S["xT_ready"], kt + 1)
                squares("n0", kt, xT[:, kt, :], sq)
            hi(0)
            act.wait_ge(S["rms_sum"], before("n0", "sum") + KT)
            rsqrt(bank[0][:, :], ry[0][:, :], ryy[0][:, :], "rms_rs")
            for kt in range(KT):
                act.wait_ge(S["rms_hf"], before("n0", "hf") + kt + 1)
                act.activation(hh[:, kt, :], h_f1[kt % 2][:, :], ACT.Copy).then_inc(S["rms_hi"], 1)
            act.wait_ge(S["scal_done"], 2)
            act.activation(lams[:, 2:4], lams[:, 0:2], ACT.Exp).then_inc(S["lam_exp"], 1)
            act.wait_ge(S["cols_ready"], 1)
            act.activation(csil, colA[:, ROWS_A["c"]:ROWS_A["c"] + 8], ACT.Silu).then_inc(S["csil_ready"], 1)

            for n in range(17):
                hi(n + 1)
                if n == 1:
                    act.wait_ge(S["brow_ready"], 2)
                    act.dma_start(toep, brow[:, :].rearrange("h (o x) -> h o x", o=1).to_broadcast([ATT_H, P, SEQ + P]))\
                        .then_inc(S["toep_out"], 16)
                ts = tiles_of(n)
                for T in ts:
                    if n < 6:
                        evac(act, T)
                        act.activation(qkv[:, T, :], cv[T % 2][:, :], ACT.Silu).then_inc(S["silu_done"], 1)
                    elif n in (7, 8, 15, 16):
                        act.wait_ge(S["tile_ready"], T + 1)
                        dst = zs[:, T - 13, :] if n < 9 else gate[:, T - 29, :]
                        act.activation(dst, bank[T % 2][:, :], ACT.Silu).then_inc(S[f"evac{T % 2}"], 1)
                for k, T in zip(norm_of(n), ts):
                    if k >= 2:
                        act.wait_ge(S["sum_done"], k - 1)
                    if n < 6:
                        act.wait_ge(S["silu_done"], T + 1)
                        src = qkv[:, T, :]
                    else:
                        evac(act, T)
                        src = qk_att[:, T - 17, :]
                    act.activation(sq[k % 2][:, :], src, ACT.Square).then_inc(S["sq_done"], 1)
                if n >= 1:
                    for k in norm_of(n - 1):
                        act.wait_ge(S["sum_done"], k + 1)
                        if k >= 2:
                            act.wait_ge(S["norm_done"], k - 1)
                        rsqrt(bank[2 + k % 2][:, :], ry[k % 2][:, :], ryy[k % 2][:, :], "rs_done")
                if n == 9:
                    act.wait_ge(S["ba_pre"], 1)
                    act.activation(ea, alog, ACT.Exp)
                    link(act.activation(sl, sb_, ACT.Exp, scale=-1.0))
                    act.activation(sl, sl, ACT.Ln, bias=1.0)
                    act.activation(beta.rearrange("p (c h) -> p c h", c=TT), ba_tok[:, :, 0:4], ACT.Sigmoid)\
                        .then_inc(S["ba_act"], 1)

            act.preload_act_table_set("natural_log_exp_and_others")
            act.wait_ge(S["dn_egc"], 1)
            link(act.activation(egc, gc, ACT.Exp))
            for c in range(TT):
                act.wait_ge(S["dn_dsub"], c + 1)
                if c >= 1:
                    act.wait_ge(S["dn_qd"], c)
                act.activation(state[:, :, :], four(bank[c % 2][:, :]), ACT.Exp)
                act.activation(tail[:, 4 * c:4 * c + 4], tail[:, 4 * c:4 * c + 4], ACT.Exp)
                act.activation(Dk[c % 2][:, :, :], Dk[c % 2][:, :, :], ACT.Exp).then_inc(S["dn_exp"], 1)
            for c in range(TT):
                act.wait_ge(S["dn_uw"], c + 1)
                act.activation(kbe[:, c], four(bank[7][:, :]), ACT.Copy).then_inc(S["dn_w"], 1)

            def osq1(c):
                act.wait_ge(S["dn_o"], c + 1)
                if c >= 2:
                    act.wait_ge(S["dn_osum"], c - 1)
                act.activation(Dk[c % 2][:, :, :], four(bank[4 + c][:, :]), ACT.Square).then_inc(S["dn_osq"], 1)

            osq1(0)
            osq1(1)
            for c in range(TT):
                act.wait_ge(S["dn_osum"], c + 1)
                if c >= 1:
                    act.wait_ge(S["dn_mix"], c)
                rsqrt(four(bank[2 + c % 2][:, :]), P1[:, 2], P1[:, 3], "dn_ors")
                if c + 2 < TT:
                    osq1(c + 2)
                act.wait_ge(S["dn_mix"], c + 1)
                act.activation(hh[:, 0:4, c * P:(c + 1) * P], four(mixf[c % 2][:, :]), ACT.Copy).then_inc(S["dn_hi"], 1)

            def attention(tag, units, tail):
                units = list(units)
                s_, p_, pT_ = bufs[tag]
                M = len(units[0]["maps"])
                maps = [mp for u in units for mp in u["maps"]]

                def exps(w):
                    if w >= len(units):
                        return
                    for g in range(M * w, M * w + M):
                        n = maps[g]["k"].shape[-1]
                        stat = st[g % 4]
                        act.wait_ge(S["att_s"], before(tag, "s") + g + 1)
                        if maps[g]["sink"] is not None:
                            act.activation(stat[:, 4:5], maps[g]["sink"], ACT.Exp, bias=stat[:, 1:2])
                        act.activation(s_[g % (2 * M)][:, 0:n], s_[g % (2 * M)][:, 0:n], ACT.Exp, bias=stat[:, 1:2],
                                       accum_out=stat[:, 2:3]).then_inc(S["att_e"], 1)

                exps(0)
                for w in range(len(units) + 4):
                    exps(w + 1)
                    if w < len(units):
                        n = units[w]["n"] * P
                        act.wait_ge(S["att_t"], before(tag, "t") + w + 1)
                        if w >= 2:
                            act.wait_ge(S["att_pv"], before(tag, "pv") + w - 1)
                        act.activation(pT_[w % 2][:, 0:n], bank[TB[w % 2]][:, 0:n], ACT.Copy).then_inc(S["att_pT"], 1)
                    tail(w)

            def split_out(tag, src, first, last_step):
                def tail(w):
                    if w >= last_step and (w - last_step) % per == 0 and (w - last_step) // per < 4:
                        p = (w - last_step) // per
                        act.wait_ge(S["att_out"], before(tag, "out") + p + 1)
                        act.activation(hh[:, first + p, :], src[p % 2][:, :], ACT.Copy).then_inc(S["att_hi"], 1)
                per = 8
                return tail

            attention("a1", units_a1(), split_out("a1", mixf, 4, 9))

            for j in range(4):
                hi(N_S1 + j + 1)
                for kt in (2 * j, 2 * j + 1):
                    evac(act, T_S1 + kt)
                    squares("n1", kt, xT[:, kt, :], nsq)

            def norm_h(tag, shift):
                act.wait_ge(S["rms_sum"], before(tag, "sum") + KT)
                rsqrt(bank[2][:, :], nry[0][:, :], nry[1][:, :], "rms_rs")
                for kt in range(KT):
                    act.wait_ge(S["rms_hf"], before(tag, "hf") + kt + 1)
                    act.activation(nhf[kt % 2][:, :], nhf[kt % 2][:, :], ACT.Identity,
                                   bias=modc[:, shift + kt:shift + kt + 1]).then_inc(S["rms_aff"], 1)
                    act.wait_ge(S["rms_aff"], before(tag, "aff") + kt + 1)
                    act.activation(hh[:, kt, :], nhf[kt % 2][:, :], ACT.Copy).then_inc(S["rms_hi"], 1)

            norm_h("n1", 0)
            for j in range(9):
                hi(N_S2 + j + 1)
                for T in (T_S2 + 2 * j, T_S2 + 2 * j + 1):
                    if j in (0, 1, 3, 4):
                        dst = q_a2[:, T - T_S2, :] if j < 2 else q_a3[:, T - T_S2 - 6, :]
                        act.wait_ge(S["tile_ready"], T + 1)
                        act.activation(dst, bank[T % 2][:, :], ACT.Copy, scale=HD ** -0.5).then_inc(S[f"evac{T % 2}"], 1)
            with act.Fori(0, 4) as i:
                for s in range(2):
                    hi(N_S2 + 9 + s + 1, i)
                    for u in range(2):
                        T = T_S2 + 18 + 2 * s + u
                        act.wait_ge(S["tile_ready"], T + 1 + 4 * i)
                        act.activation(sg[:, bass.ds(2 * s + u + 4 * i, 1), :].rearrange("p k c -> p (k c)"), bank[T % 2][:, :],
                                       ACT.Sigmoid).then_inc(S[f"evac{T % 2}"], 1)
            act.preload_act_table_set("natural_log_exp_and_others")
            attention("a2", units_a2(), split_out("a2", of, 0, 9))

            def diff_tail(w):
                if w >= 5 and (w - 5) % 4 == 0 and (w - 5) // 4 < DN_H:
                    h = (w - 5) // 4
                    act.wait_ge(S["att_out"], before("a3", "out") + h + 1)
                    if h >= 1:
                        act.wait_ge(S["d_sum"], h)
                    act.activation(osq[:, :], of[h % 2][:, :], ACT.Square).then_inc(S["d_sq"], 1)
                if w >= 6 and (w - 6) % 4 == 0 and (w - 6) // 4 < DN_H:
                    h = (w - 6) // 4
                    act.wait_ge(S["d_sum"], h + 1)
                    if h >= 1:
                        act.wait_ge(S["d_mix"], h)
                    rsqrt(bank[0][:, :], ory[0][:, :], ory[1][:, :], "d_rs")
                if w >= 7 and (w - 7) % 4 == 0 and (w - 7) // 4 < DN_H:
                    h = (w - 7) // 4
                    act.wait_ge(S["d_mix"], h + 1)
                    act.activation(hh[:, 4 + h, :], of[h % 2][:, :], ACT.Copy).then_inc(S["att_hi"], 1)

            attention("a3", units_a3(), diff_tail)

            for j in range(4):
                hi(N_S3 + j + 1)
                for q in (2 * j, 2 * j + 1):
                    act.wait_ge(S["merged_ready"], q + 1)
                    act.activation(mh[:, q, :], mS[q % 2][:, :], ACT.Copy).then_inc(S["mg_hi"], 1)
            for j in range(4):
                hi(N_S4 + j + 1)
                for kt in (2 * j, 2 * j + 1):
                    evac(act, T_S4 + kt)
                    squares("n2", kt, xT[:, kt, :], nsq)
            norm_h("n2", 24)
            with act.Fori(0, 11) as i:
                for s in range(2):
                    hi(N_S5 + s + 1, i)
                    T = T_S5 + 2 * s
                    evac(act, T, i)
                    act.activation(fg[s][:, :], fc[s][:, :], ACT.Gelu).then_inc(S["f_gelu"], 1)
                    evac(act, T + 1, i)
                    act.activation(fh[:, bass.ds(s + 2 * i, 1), :].rearrange("p k c -> p (k c)"), ff[s][:, :], ACT.Copy)\
                        .then_inc(S["f_hi"], 1)
            hi(N_S6 + 1)
            with act.Fori(0, 4) as i:
                for s in range(2):
                    hi(N_S6 + 2 + s, i)
            hi(N_S6 + 10)
            for kt in range(KT):
                act.wait_ge(S["x3_ready"], kt + 1)
                squares("n3", kt, xT[:, kt, :], nsq)
            act.wait_ge(S["rms_sum"], before("n3", "sum") + KT)
            rsqrt(bank[0][:, :], nry[0][:, :], nry[1][:, :], "rms_rs")
            for t in range(TT):
                act.wait_ge(S["y_tr"], 2 * t + 1)
                act.activation(y_tok[:, t, 0:512], bank[(2 * t + 1) % 8][:, :], ACT.Copy).then_inc(S["y_out0"], 1)

        @block.vector
        def _(dve):
            link = Chain(dve, "dve_chain")

            def lo(n, i=0):
                s = n % 2
                dve.wait_ge(S["hi_ready"], n + 1 + 2 * i)
                dve.tensor_tensor(wlo[s][:, :], raw[s][:, :], whi[s][:, :].bitcast(F32), ALU.subtract)\
                    .then_inc(S["lo_ready"], 1)

            def rest(dst, src, high, done):
                return dve.tensor_tensor(dst, src, high.bitcast(F32), ALU.subtract).then_inc(S[done], 1)

            def newton(ps, y, yy, done=None):
                ins = dve.scalar_tensor_tensor(yy, ps, eps, yy, op0=ALU.add, op1=ALU.mult)
                if done:
                    ins.then_inc(S[done[0]], 1)
                    dve.wait_ge(S[done[0]], done[1])
                else:
                    link(ins)
                link(dve.scalar_tensor_tensor(yy, yy, -3.0, y, op0=ALU.add, op1=ALU.mult))

            dve.memset(eps, EPS).then_inc(S["scal_done"], 1)
            for kt in range(KT):
                dve.wait_ge(S["xt_done"], kt + 1)
                dve.tensor_copy(xT[:, kt, :], bank[kt][:, :]).then_inc(S["xT_ready"], 1)
            dve.wait_ge(S["vecs_done"], 1)
            dve.tensor_copy(colA[:, :], bank[1][:, 0:NA]).then_inc(S["cols_ready"], 1)
            dve.wait_ge(S["vecs_done"], 2)
            dve.tensor_copy(colB[:, :], bank[2][:, 0:NB]).then_inc(S["cols_ready"], 1)
            dve.wait_ge(S["cols_ready"], 2)
            dve.tensor_scalar(nw1, colA[:, 0:8], -0.5, None, ALU.mult)
            dve.tensor_scalar(gfc, colA[:, 24:32], -0.5, None, ALU.mult)
            dve.tensor_scalar(dncol, col("dn_norm_w"), -0.5, None, ALU.mult)
            dve.tensor_scalar(subcol, col("subln"), -0.5 * (1.0 - LAM_INIT), None, ALU.mult)
            dve.tensor_scalar(qcol, col("q_norm"), -0.5 * HD ** -0.5, None, ALU.mult)
            link(dve.tensor_scalar(kcol, col("k_norm"), -0.5, None, ALU.mult))
            dve.wait_ge(S["rms_rs"], before("n0", "rs") + 1)
            newton(bank[0][:, :], ry[0][:, :], ryy[0][:, :])

            def norm_h(tag, g, z, buf):
                for kt in range(KT + 1):
                    if 2 <= kt < KT:
                        dve.wait_ge(S["rms_lo"], before(tag, "lo") + kt - 1)
                    if kt < KT:
                        dve.scalar_tensor_tensor(buf[kt % 2][:, :], xT[:, kt, :], g[:, kt:kt + 1], z,
                                                 op0=ALU.mult, op1=ALU.mult).then_inc(S["rms_hf"], 1)
                    if kt >= 1:
                        dve.wait_ge(S["rms_hi"], before(tag, "hi") + kt)
                        rest(hl[:, kt - 1, :], buf[(kt - 1) % 2][:, :], hh[:, kt - 1, :], "rms_lo")

            lo(0)
            norm_h("n0", nw1, ryy[0][:, :], h_f1)
            dve.wait_ge(S["rel_done"], 1)
            dve.tensor_tensor(brow[:, 0:SEQ], bank[3][0:ATT_H, :], logm[:, 0:SEQ], ALU.add).then_inc(S["brow_ready"], 1)
            dve.tensor_tensor(brow[:, SEQ:], bank[4][0:ATT_H, 0:P], logm[:, SEQ:], ALU.add).then_inc(S["brow_ready"], 1)
            dve.wait_ge(S["in_small"], 16 * 5)
            for k in range(2):
                ins = dve.tensor_tensor_reduce(out=lamrow[:, 128 * k:128 * k + 64], in0=lamrow[:, 128 * k:128 * k + 64],
                                               in1=lamrow[:, 128 * k + 64:128 * k + 128], scale=1.0, scalar=0.0,
                                               op0=ALU.mult, op1=ALU.add, accum_out=lams[:, k:k + 1])
            ins.then_inc(S["scal_done"], 1)
            dve.wait_ge(S["lam_exp"], 1)
            link(dve.tensor_tensor(lams[:, 4:5], lams[:, 2:3], lams[:, 3:4], ALU.subtract))
            link(dve.tensor_scalar(lams[:, 5:6], lams[:, 4:5], -1.0, -LAM_INIT, ALU.mult, ALU.add))
            dve.wait_ge(S["csil_ready"], 1)

            piece = [0]

            def ada():
                p = piece[0]
                piece[0] += 1
                c, kt = divmod(p, KT)
                dve.wait_ge(S[f"ada_in{p % 2}"], 16 * (p // 2 + 1))
                acc = ada_acc[c % 2][:, :]
                if kt == 0:
                    if c >= 2:
                        dve.wait_ge(S["ada_fold"], c - 1)
                    ins = dve.tensor_scalar(acc, ada_w[p % 2][:, :], csil[:, 0:1], None, ALU.mult)
                else:
                    dve.wait_ge(S["ada_piece"], p)
                    ins = dve.scalar_tensor_tensor(acc, ada_w[p % 2][:, :], csil[:, kt:kt + 1], acc, op0=ALU.mult, op1=ALU.add)
                ins.then_inc(S["ada_piece"], 1)

            for n in range(17):
                lo(n + 1)
                for T in tiles_of(n):
                    ps = bank[T % 2]
                    if n < 6:
                        y = cv[T % 2]
                        dve.wait_ge(S["tile_ready"], T + 1)
                        if T >= 2:
                            dve.wait_ge(S["silu_done"], T - 1)
                        link(dve.tensor_scalar(y[:, :], ps[:, :], col("conv_w", 36 + T), None, ALU.mult))
                        for k in range(1, 4):
                            ins = dve.scalar_tensor_tensor(y[:, k:], ps[:, 0:SEQ - k], col("conv_w", 12 * (3 - k) + T), y[:, k:],
                                                           op0=ALU.mult, op1=ALU.add)
                            if k < 3:
                                link(ins)
                        ins.then_inc(S[f"evac{T % 2}"], 1)
                    elif n == 6:
                        dve.wait_ge(S["tile_ready"], T + 1)
                        dve.tensor_copy(baT[:, :], ps[0:8, :]).then_inc(S[f"evac{T % 2}"], 1)
                    elif 9 <= n < 15:
                        dve.wait_ge(S["tile_ready"], T + 1)
                        dst = qk_att[:, T - 17, :] if n < 13 else v_att[:, T - 25, :]
                        dve.tensor_copy(dst, ps[:, :]).then_inc(S[f"evac{T % 2}"], 1)
                for _ in range(ADA_STEP.get(n, 0)):
                    ada()
                if n >= 1:
                    for k in norm_of(n - 1):
                        dve.wait_ge(S["rs_done"], k + 1)
                        newton(bank[2 + k % 2][:, :], ry[k % 2][:, :], ryy[k % 2][:, :], ("nt_done", k + 1))
                        if k < 8:
                            t, g = qkv[:, k, :], -0.5 * P ** -0.5 if k < 4 else -0.5
                        else:
                            t, g = qk_att[:, k - 8, :], qcol if k < 12 else kcol
                        dve.scalar_tensor_tensor(t, t, g, ryy[k % 2][:, :], op0=ALU.mult, op1=ALU.mult)\
                            .then_inc(S["norm_done"], 1)
                if n == 8:
                    dve.wait_ge(S["ba_tr"], 1)
                    link(dve.tensor_copy(ba_tok, bank[4][:, 0:32].rearrange("p (c e) -> p c e", c=TT)))
                    x4 = lambda ap: ap.rearrange("p (c h) -> p c h", c=TT)
                    link(dve.tensor_tensor(x4(sa), ba_tok[:, :, 4:8],
                                           dtb.rearrange("p (o h) -> p o h", o=1).to_broadcast([P, TT, DN_H]), ALU.add))
                    dve.tensor_scalar(sr, sa, 0.0, None, ALU.max)
                    link(dve.tensor_scalar(sb_, sa, -1.0, None, ALU.mult))
                    dve.tensor_tensor(sb_, sb_, sa, ALU.max).then_inc(S["ba_pre"], 1)
                if n == 10:
                    dve.wait_ge(S["ba_act"], 1)
                    link(dve.tensor_tensor(sr, sr, sl, ALU.add))
                    dve.scalar_tensor_tensor(x4(gdec), x4(sr), -1.0,
                                             ea.rearrange("p (o h) -> p o h", o=1).to_broadcast([P, TT, DN_H]),
                                             op0=ALU.mult, op1=ALU.mult).then_inc(S["g_ready"], 1)
            dve.wait_ge(S["ada_fold"], 6)
            dve.wait_ge(S["in_rowsM"], 16)
            dve.tensor_tensor(modrow[:, :], bank[5][0:48, 0:P], rowsM[:, :], ALU.add).then_inc(S["modrow_ready"], 1)
            dve.wait_ge(S["mod_tr"], 1)
            link(dve.tensor_copy(modc[:, :], bank[4][:, 0:48]))
            for g, row, scale in ((g1c, ROWS_A["norm1_g"], 8), (g2c, ROWS_A["norm2_g"], 32)):
                link(dve.scalar_tensor_tensor(g, modc[:, scale:scale + 8], 1.0, colA[:, row:row + 8], op0=ALU.add, op1=ALU.mult))
                ins = dve.tensor_scalar(g, g, -0.5, None, ALU.mult)
            ins.then_inc(S["mod_ready"], 1)
            dve.wait_ge(S["v_tr"], 1)
            for t in range(TT):
                dve.tensor_copy(v_att[:, t, :], bank[(2, 3, 6, 7)[t]][:, :]).then_inc(S["v_ready"], 1)

            dve.wait_ge(S["toep_out"], 16)
            dve.wait_ge(S["tile_ready"], 33)
            dve.wait_ge(S["dn_gct"], 1)
            dve.tensor_copy(gc, bank[5][:, 0:16]).then_inc(S["dn_egc"], 1)

            def spread(c):
                if c >= 2:
                    dve.wait_ge(S["dn_grow"], c - 1)
                    dve.wait_ge(S["dn_brow"], c - 1)
                dve.tensor_tensor(P1[:, c % 2], over(gdec[:, 4 * c:4 * c + 4]), each(m(C_TRIU)), ALU.mult).then_inc(S["dn_gtri"], 1)
                dve.tensor_tensor(P1[:, 2 + c % 2], over(beta[:, 4 * c:4 * c + 4]), each(ident), ALU.mult).then_inc(S["dn_gtri"], 1)

            spread(0)
            dve.wait_ge(S["dn_egc"], 1)
            for c in range(TT):
                if c + 1 < TT:
                    spread(c + 1)
                four_c = slice(4 * c, 4 * c + 4)
                tok = slice(c * P, (c + 1) * P)
                dve.wait_ge(S["dn_grow"], c + 1)
                for h in range(DN_H):
                    dve.tensor_scalar(Dk[c % 2][:, h, :], bank[c % 2][:, h * P:(h + 1) * P], gc[:, 4 * c + h:4 * c + h + 1],
                                      0.0, ALU.subtract, ALU.min)
                last = four(bank[c % 2][:, :])[:, :, P - 1:P].rearrange("p h o -> p (h o)")
                dve.tensor_tensor(tail[:, four_c], last, gc[:, four_c], ALU.subtract).then_inc(S["dn_dsub"], 1)
                dve.wait_ge(S["dn_exp"], c + 1)
                if c == 0:
                    dve.tensor_tensor(bege, beta, egc, ALU.mult)
                link(dve.tensor_tensor(Dk[c % 2][:, :, :], Dk[c % 2][:, :, :], each(m(C_TRIU)), ALU.mult))
                dve.wait_ge(S["dn_brow"], c + 1)
                dve.tensor_tensor(attnT[:, c], four(bank[2 + c % 2][:, :]), Dk[c % 2][:, :, :], ALU.mult).then_inc(S["dn_dtb"], 1)
                dve.wait_ge(S["dn_dtb"], c + 1)
                link(dve.tensor_tensor(attnT[:, c], attnT[:, c], each(m(C_STRIU)), ALU.mult))
                dve.wait_ge(S["dn_prod"], c + 1)
                dve.tensor_tensor(AT[:, c], four(bank[5][:, :]), attnT[:, c], ALU.mult).then_inc(S["dn_at"], 1)
                dve.wait_ge(S["dn_at"], 2 * c + 1)
                dve.tensor_tensor(attnT[:, c], four(bank[6][:, :]), Dk[c % 2][:, :, :], ALU.mult).then_inc(S["dn_at"], 1)
                dve.tensor_copy(glst[:, four_c], state[:, :, P - 1:P].rearrange("p h o -> p (h o)"))
                dve.tensor_tensor(qkv[:, 0:4, tok], qkv[:, 0:4, tok], state[:, :, :], ALU.mult).then_inc(S["dn_qd"], 1)
                dve.wait_ge(S["dn_ktr"], 2 * c + 1)
                dve.tensor_tensor(kbe[:, c], four(bank[4][:, :]), over(bege[:, four_c]), ALU.mult)
                dve.tensor_tensor(ktail[:, c], four(bank[4][:, :]), over(tail[:, four_c]), ALU.mult).then_inc(S["dn_kv"], 1)
                dve.wait_ge(S["dn_ktr"], 2 * c + 2)
                dve.tensor_tensor(vb[:, c], four(bank[7][:, :]), over(beta[:, four_c]), ALU.mult).then_inc(S["dn_kv"], 1)
                dve.wait_ge(S["dn_a"], c + 1)
                dve.tensor_tensor(X[:, c], four(bank[7][:, :]), each(m(C_NM0)), ALU.mult)
                link(dve.tensor_tensor(XT[:, c], AT[:, c], each(m(C_NMT0)), ALU.mult))
                dve.tensor_tensor(X[:, c], X[:, c], each(ident), ALU.add)
                dve.tensor_tensor(XT[:, c], XT[:, c], each(ident), ALU.add).then_inc(S["dn_x"], 1)

            def masked(l, c):
                dve.wait_ge(S["dn_p1"], 4 * l + c + 1)
                dve.tensor_tensor(P1[:, c], four(bank[c % 2][:, :]), each(m(C_LVL + l)), ALU.mult).then_inc(S["dn_p1s"], 1)

            def update(l, c):
                dve.wait_ge(S["dn_z"], 4 * l + c + 1)
                if l < N_LVL - 1:
                    dve.tensor_tensor(X[:, c], X[:, c], four(bank[2 + c % 2][:, :]), ALU.subtract)
                dve.tensor_tensor(XT[:, c], XT[:, c], four(bank[4 + c % 2][:, :]), ALU.subtract).then_inc(S["dn_upd"], 1)

            for l in range(N_LVL):
                masked(l, 0)
                for c in range(TT):
                    if c + 1 < TT:
                        masked(l, c + 1)
                    update(l, c)
            for c in range(TT):
                dve.wait_ge(S["dn_uw"], c + 1)
                dve.tensor_copy(vb[:, c], four(bank[6][:, :])).then_inc(S["dn_u"], 1)
            dve.wait_ge(S["dn_u"], 4)
            for c in range(TT):
                if c == 0:
                    dve.tensor_copy(P1[:, 0], vb[:, 0]).then_inc(S["dn_vn"], 1)
                else:
                    dve.wait_ge(S["dn_ws"], c)
                    dve.tensor_tensor(P1[:, c % 2], vb[:, c], four(bank[0][:, :]), ALU.subtract).then_inc(S["dn_vn"], 1)
                if c < TT - 1:
                    dve.wait_ge(S["dn_su"], c + 1)
                    if c == 0:
                        dve.tensor_copy(state[:, :, :], four(bank[1][:, :])).then_inc(S["dn_s"], 1)
                    else:
                        dve.wait_ge(S["dn_o"], c + 1)
                        link(dve.tensor_tensor(state[:, :, :], state[:, :, :], over(glst[:, 4 * c:4 * c + 4]), ALU.mult))
                        dve.tensor_tensor(state[:, :, :], state[:, :, :], four(bank[1][:, :]), ALU.add).then_inc(S["dn_s"], 1)
                    dve.wait_ge(S["dn_s"], c + 1)
            for c in range(TT):
                tok = slice(c * P, (c + 1) * P)
                dve.wait_ge(S["dn_ors"], c + 1)
                newton(four(bank[2 + c % 2][:, :]), P1[:, 2], P1[:, 3])
                if c >= 2:
                    dve.wait_ge(S["dn_hi"], c - 1)
                mx4 = four(mixf[c % 2][:, :])
                link(dve.scalar_tensor_tensor(mx4, four(bank[4 + c][:, :]), dncol, P1[:, 3], op0=ALU.mult, op1=ALU.mult))
                dve.tensor_tensor(mx4, mx4, zs[:, 0:4, tok], ALU.mult).then_inc(S["dn_mix"], 1)
                dve.wait_ge(S["dn_hi"], c + 1)
                rest(hl[:, 0:4, tok], mx4, hh[:, 0:4, tok], "dn_lo")

            def attention(tag, units, bias_wait, tail):
                units = list(units)
                s_, p_, pT_ = bufs[tag]
                M = len(units[0]["maps"])
                maps = [mp for u in units for mp in u["maps"]]

                def scores(w):
                    if w >= len(units):
                        return
                    if w >= 2:
                        dve.wait_ge(S["att_p"], before(tag, "p") + w - 1)
                    for g in range(M * w, M * w + M):
                        mp = maps[g]
                        n = mp["k"].shape[-1]
                        stat = st[g % 4]
                        if g % (TT * M) == 0:
                            bias_wait(units[w]["head"])
                        dve.wait_ge(S["att_qk"], before(tag, "qk") + g + 1)
                        link(dve.tensor_tensor_reduce(out=s_[g % (2 * M)][:, 0:n], in0=bank[QK[g % 2]][:, 0:n], in1=mp["bias"],
                                                      scale=1.0, scalar=-3e38, op0=ALU.add, op1=ALU.max, accum_out=stat[:, 0:1]))
                        if mp["sink"] is None:
                            ins = dve.tensor_scalar(stat[:, 1:2], stat[:, 0:1], -1.0, None, ALU.mult)
                        else:
                            ins = dve.tensor_scalar(stat[:, 1:2], stat[:, 0:1], mp["sink"], -1.0, ALU.max, ALU.mult)
                        ins.then_inc(S["att_s"], 1)

                def probs(w):
                    n = units[w]["n"] * P
                    p = p_[w % 2][:, 0:n]
                    for k in range(M):
                        g = M * w + k
                        stat = st[g % 4]
                        s = s_[g % (2 * M)][:, 0:n]
                        dve.wait_ge(S["att_e"], before(tag, "e") + g + 1)
                        if maps[g]["sink"] is not None:
                            link(dve.tensor_tensor(stat[:, 2:3], stat[:, 2:3], stat[:, 4:5], ALU.add))
                        link(dve.reciprocal(stat[:, 3:4], stat[:, 2:3]))
                        if k == 0:
                            if w >= 2:
                                dve.wait_ge(S["att_t"], before(tag, "t") + w - 1)
                            ins = dve.tensor_scalar(p, s, stat[:, 3:4], None, ALU.mult)
                            if M == 2:
                                link(ins)
                        else:
                            link(dve.tensor_tensor(stat[:, 5:6], stat[:, 3:4], lams[:, 5:6], ALU.mult))
                            ins = dve.scalar_tensor_tensor(p, s, stat[:, 5:6], p, op0=ALU.mult, op1=ALU.add)
                    ins.then_inc(S["att_p"], 1)

                scores(0)
                for w in range(len(units) + 4):
                    scores(w + 1)
                    if w < len(units):
                        probs(w)
                    tail(w)

            def tail1(w):
                if w >= 9 and (w - 9) % 8 == 0:
                    p = (w - 9) // 8
                    dve.wait_ge(S["att_pv"], before("a1", "pv") + 8 * p + 8)
                    if p >= 2:
                        dve.wait_ge(S["att_hi"], before("a1", "hi") + p - 1)
                    dve.tensor_tensor(mixf[p % 2][:, :], bank[OB[p % 2]][:, :], gate[:, p, :], ALU.mult).then_inc(S["att_out"], 1)
                if w >= 10 and (w - 10) % 8 == 0:
                    p = (w - 10) // 8
                    dve.wait_ge(S["att_hi"], before("a1", "hi") + p + 1)
                    rest(hl[:, 4 + p, :], mixf[p % 2][:, :], hh[:, 4 + p, :], "att_lo")

            attention("a1", units_a1(), lambda h: dve.wait_ge(S[f"toe_in{h % TOE}"], 16 * (h // TOE + 1)), tail1)

            for j in range(4):
                lo(N_S1 + j + 1)
                for kt in (2 * j, 2 * j + 1):
                    T = T_S1 + kt
                    dve.wait_ge(S["tile_ready"], T + 1)
                    dve.tensor_tensor(xT[:, kt, :], xT[:, kt, :], bank[T % 2][:, :], ALU.add).then_inc(S[f"evac{T % 2}"], 1)
            dve.wait_ge(S["rms_rs"], before("n1", "rs") + 1)
            newton(bank[2][:, :], nry[0][:, :], nry[1][:, :])
            norm_h2 = lambda tag, g: norm_h(tag, g, nry[1][:, :], nhf)
            norm_h2("n1", g1c)
            for j in range(9):
                lo(N_S2 + j + 1)
                for T in (T_S2 + 2 * j, T_S2 + 2 * j + 1):
                    t = T - T_S2
                    ps = bank[T % 2]
                    if j in (2, 5, 6, 7, 8):
                        dve.wait_ge(S["tile_ready"], T + 1)
                    if t == 4:
                        for g in range(2):
                            for half in range(2):
                                ins = dve.tensor_copy(k_a2[64 * half:64 * half + 64, g, :], ps[64 * g:64 * g + 64, :])
                        ins.then_inc(S[f"evac{T % 2}"], 1)
                    elif t == 5 or j in (5, 6, 7, 8):
                        dst = vf[:, 0, :] if t == 5 else k_a3[:, t - 10, :] if t < 14 else vf[:, t - 13, :]
                        dve.tensor_copy(dst, ps[:, :]).then_inc(S[f"evac{T % 2}"], 1)
            with dve.Fori(0, 4) as i:
                for s in range(2):
                    lo(N_S2 + 9 + s + 1, i)
            dve.wait_ge(S["v2_tr"], 1)
            dve.tensor_copy(v_a2[:, :, :], four(bank[6][:, :])).then_inc(S["v2_ready"], 1)
            for t in range(TT):
                dve.tensor_copy(v_a3[:, t, :], bank[2 + t][:, :]).then_inc(S["v2_ready"], 1)

            def tail2(w):
                if w >= 9 and (w - 9) % 8 == 0:
                    p = (w - 9) // 8
                    dve.wait_ge(S["att_pv"], before("a2", "pv") + 8 * p + 8)
                    if p >= 2:
                        dve.wait_ge(S["att_hi"], before("a2", "hi") + p - 1)
                    dve.tensor_copy(of[p % 2][:, :], bank[OB[p % 2]][:, :]).then_inc(S["att_out"], 1)
                if w >= 10 and (w - 10) % 8 == 0:
                    p = (w - 10) // 8
                    dve.wait_ge(S["att_hi"], before("a2", "hi") + p + 1)
                    rest(hl[:, p, :], of[p % 2][:, :], hh[:, p, :], "att_lo")

            attention("a2", units_a2(), lambda h: dve.wait_ge(S["bias_ready"], h + 1), tail2)

            def tail3(w):
                if w >= 5 and (w - 5) % 4 == 0 and (w - 5) // 4 < DN_H:
                    h = (w - 5) // 4
                    dve.wait_ge(S["att_pv"], before("a3", "pv") + 4 * h + 4)
                    if h >= 2:
                        dve.wait_ge(S["att_hi"], before("a3", "hi") + h - 1)
                    dve.tensor_copy(of[h % 2][:, :], bank[OB[h % 2]][:, :]).then_inc(S["att_out"], 1)
                if w >= 7 and (w - 7) % 4 == 0 and (w - 7) // 4 < DN_H:
                    h = (w - 7) // 4
                    dve.wait_ge(S["d_rs"], h + 1)
                    newton(bank[0][:, :], ory[0][:, :], ory[1][:, :])
                    dve.scalar_tensor_tensor(of[h % 2][:, :], of[h % 2][:, :], subcol, ory[1][:, :], op0=ALU.mult, op1=ALU.mult)\
                        .then_inc(S["d_mix"], 1)
                    dve.wait_ge(S["att_hi"], before("a3", "hi") + h + 1)
                    rest(hl[:, 4 + h, :], of[h % 2][:, :], hh[:, 4 + h, :], "att_lo")

            attention("a3", units_a3(), lambda h: dve.wait_ge(S["bias_ready"], 9 + h), tail3)

            for j in range(4):
                lo(N_S3 + j + 1)
                for q in (2 * j, 2 * j + 1):
                    for g, buf in ((0, mA), (1, mD)):
                        T = T_S3 + 2 * q + g
                        dve.wait_ge(S["tile_ready"], T + 1)
                        dve.tensor_tensor(buf[q % 2][:, :], bank[T % 2][:, :], sg[:, 8 * g + q, :], ALU.mult)\
                            .then_inc(S[f"evac{T % 2}"], 1)
                    evac(dve, T_S3 + 2 * q)
                    evac(dve, T_S3 + 2 * q + 1)
                    dve.tensor_tensor(mS[q % 2][:, :], mA[q % 2][:, :], mD[q % 2][:, :], ALU.add).then_inc(S["merged_ready"], 1)
                    dve.wait_ge(S["mg_hi"], q + 1)
                    rest(ml[:, q, :], mS[q % 2][:, :], mh[:, q, :], "mg_lo")
            for j in range(4):
                lo(N_S4 + j + 1)
                for kt in (2 * j, 2 * j + 1):
                    T = T_S4 + kt
                    dve.wait_ge(S["tile_ready"], T + 1)
                    dve.scalar_tensor_tensor(xT[:, kt, :], bank[T % 2][:, :], modc[:, 16 + kt:17 + kt], xT[:, kt, :],
                                             op0=ALU.mult, op1=ALU.add).then_inc(S[f"evac{T % 2}"], 1)
            dve.wait_ge(S["rms_rs"], before("n2", "rs") + 1)
            newton(bank[2][:, :], nry[0][:, :], nry[1][:, :])
            norm_h2("n2", g2c)
            with dve.Fori(0, 11) as i:
                for s in range(2):
                    lo(N_S5 + s + 1, i)
                    T = T_S5 + 2 * s
                    pa, pg = bank[T % 2], bank[(T + 1) % 2]
                    cw = lambda tap: colB[:, bass.ds(tap * FT + s + 2 * i, 1)]
                    dve.wait_ge(S["tile_ready"], T + 1 + 4 * i)
                    dve.tensor_scalar(fc[s][:, :], pa[:, :], cw(2), colA[:, bass.ds(ROWS_A["conv_b"] + s + 2 * i, 1)],
                                      ALU.mult, ALU.add).then_inc(S["f_chain"], 1)
                    dve.wait_ge(S["f_chain"], 2 * s + 1 + 4 * i)
                    dve.scalar_tensor_tensor(fc[s][:, 1:], pa[:, 0:SEQ - 1], cw(1), fc[s][:, 1:], op0=ALU.mult, op1=ALU.add)\
                        .then_inc(S["f_chain"], 1)
                    dve.wait_ge(S["f_chain"], 2 * s + 2 + 4 * i)
                    dve.scalar_tensor_tensor(fc[s][:, 2:], pa[:, 0:SEQ - 2], cw(0), fc[s][:, 2:], op0=ALU.mult, op1=ALU.add)\
                        .then_inc(S[f"evac{T % 2}"], 1)
                    dve.wait_ge(S["tile_ready"], T + 2 + 4 * i)
                    dve.wait_ge(S["f_gelu"], s + 1 + 2 * i)
                    dve.tensor_tensor(ff[s][:, :], pg[:, :], fg[s][:, :], ALU.mult).then_inc(S[f"evac{(T + 1) % 2}"], 1)
                    dve.wait_ge(S["f_hi"], s + 1 + 2 * i)
                    j = bass.ds(s + 2 * i, 1)
                    rest(fl[:, j, :].rearrange("p k c -> p (k c)"), ff[s][:, :], fh[:, j, :].rearrange("p k c -> p (k c)"), "f_lo")
            lo(N_S6 + 1)
            with dve.Fori(0, 4) as i:
                for s in range(2):
                    lo(N_S6 + 2 + s, i)
            lo(N_S6 + 10)
            for kt in range(KT):
                dve.wait_ge(S["tile_ready"], T_S5 + 44 + kt + 1)
                dve.scalar_tensor_tensor(xT[:, kt, :], bank[kt][:, :], modc[:, 40 + kt:41 + kt], xT[:, kt, :],
                                         op0=ALU.mult, op1=ALU.add).then_inc(S["x3_ready"], 1)
            dve.wait_ge(S["rms_rs"], before("n3", "rs") + 1)
            newton(bank[0][:, :], nry[0][:, :], nry[1][:, :])
            for kt in range(KT):
                dve.scalar_tensor_tensor(yT[:, kt, :], xT[:, kt, :], gfc[:, kt:kt + 1], nry[1][:, :], op0=ALU.mult, op1=ALU.mult)\
                    .then_inc(S["y_ready"], 1)
            for t in range(TT):
                dve.wait_ge(S["y_tr"], 2 * t + 2)
                dve.tensor_copy(y_tok[:, t, 512:1024], bank[(2 * t + 2) % 8][:, :]).then_inc(S["y_out1"], 1)


INPUTS = ["x", "norm_w", "w_in", "conv_w", "a_log", "dt_bias", "dn_norm_w", "q_norm_w", "k_norm_w", "rel_bias",
          "w_out", "c_2", "w_ada_2", "b_ada_2", "norm1_g_2", "w_in_2", "swa_sinks_2", "diff_lambda_2",
          "diff_subln_g_2", "w_branch_swa_2", "w_branch_diff_2", "w_out_2", "norm2_g_2", "w_up_2", "conv_w_2",
          "conv_b_2", "w_down_2", "final_g_2"]


def kernel(**inputs):
    import concourse.bacc as bacc
    from concourse.bass_utils import run_bass_kernel_spmd

    nc = bacc.Bacc("TRN2", target_bir_lowering=False, num_devices=1, dynamic_dma_scratch_size=2048)
    arrays = {n: np.ascontiguousarray(inputs[n]) for n in INPUTS}
    arrays.update(constants())
    aps = {n: nc.dram_tensor(n, v.shape, mybir.dt.from_np(v.dtype), kind="ExternalInput").ap() for n, v in arrays.items()}
    out = nc.dram_tensor("out", (1, SEQ, D), F32, kind="ExternalOutput").ap()
    toep = nc.dram_tensor("bias_rows", (ATT_H, P, SEQ + P), F32, kind="Internal").ap()
    build(nc, aps, out, toep)
    r = run_bass_kernel_spmd(nc, [arrays], core_ids=[0])
    return r.results[0]["out"]
```

```python
import math
from contextlib import ExitStack

import numpy as np
import concourse.bass as bass
from concourse import mybir

F32 = mybir.dt.float32
F32R = mybir.dt.float32r
ACT = mybir.ActivationFunctionType
ALU = mybir.AluOpType

P = 128
SEQ = 512
D = 1024
KT = D // P
TT = SEQ // P
D_DN, DN_H = 512, 4
ATT_H, HD = 8, 64
D_IN = 4 * D_DN + 2 * DN_H + 4 * 512
IN2 = 4352
DFF = 2816
FT = DFF // P
N_BUCKETS, MAX_DISTANCE = 32, 2048
BLK = 2048
EPS = 1e-6
MASK = -1e30
SWA_SLOPES = [2.0 ** -(h + 1) for h in range(8)]
DIFF_SLOPES = [2.0 ** (-2 * (h + 1)) for h in range(4)]
LAM_INIT = 0.8 - 0.6 * math.exp(0.0)

ROWS_A = {"norm_w": 0, "norm1_g": 8, "norm2_g": 16, "final_g": 24, "c": 32, "dn_norm_w": 40,
          "subln": 41, "q_norm": 42, "k_norm": 43, "conv_w": 44, "conv_b": 92}
NA = 92 + FT
NB = 3 * FT
C_ID, C_ONE, C_INVD, C_INVH, C_BLK, C_TRIU, C_STRIU, C_NM0, C_NMT0, C_LVL = range(10)
N_LVL = 6
NC128 = C_LVL + N_LVL


def t5_bucket(dist):
    max_exact = N_BUCKETS // 2
    d = np.maximum(dist, 1).astype(np.float64)
    large = max_exact + (np.log(d / max_exact) / math.log(MAX_DISTANCE / max_exact)
                         * (N_BUCKETS - max_exact)).astype(np.int32)
    large = np.minimum(large, N_BUCKETS - 1)
    return np.where(dist < max_exact, dist, large).astype(np.int32)


def constants():
    i = np.arange(P)[:, None]
    j = np.arange(P)[None, :]
    c = np.zeros((P, NC128, P), np.float32)
    c[:, C_ID] = i == j
    c[:, C_ONE] = 1.0
    c[:, C_INVD] = 1.0 / D
    c[:, C_INVH] = 1.0 / P
    c[:, C_BLK] = (i // HD == j // HD) / HD
    c[:, C_TRIU] = i <= j
    c[:, C_STRIU] = i < j
    merge = lambda b: (i // (2 * b) == j // (2 * b)) & (i // b == j // b + 1)
    c[:, C_NM0] = -1.0 * merge(1)
    c[:, C_NMT0] = -1.0 * merge(1).T
    for n in range(N_LVL):
        c[:, C_LVL + n] = merge(2 << n)
    d = i - (np.arange(SEQ)[None, :] - 3 * P)
    alibi = np.where(d >= 0, -d, MASK).astype(np.float32)
    d2 = d[:, 2 * P:]
    window = np.where((d2 >= 0) & (d2 < P), -d2, MASK).astype(np.float32)
    dist = SEQ - 1 - np.arange(SEQ + P)
    onehot = np.zeros((N_BUCKETS, SEQ + P), np.float32)
    ok = dist >= 0
    onehot[t5_bucket(dist[ok]), np.arange(SEQ + P)[ok]] = 1.0
    times = (dist <= 128) * 1 + (dist % 4 == 0) * 1 + (dist % 16 == 0) * 1
    logm = np.where(ok & (times > 0), np.log(np.maximum(times, 1)), MASK).astype(np.float32)
    select = np.zeros((P, 95), np.float32)
    select[:, 47] = 1.0
    return {"k_mats": c.reshape(P, NC128 * P), "k_alibi": np.concatenate([alibi, window], 1),
            "k_onehot": onehot, "k_logm": logm[None], "k_select": select}


def build(nc, a, out, toep):
    with ExitStack() as ctx:
        top = [0]

        def at(name, shape, dt=F32, offset=None):
            size = 4 * int(np.prod(shape[1:]))
            if offset is None:
                offset = top[0]
                top[0] += (size + 31) // 32 * 32
            return nc.alloc_sbuf_tensor_at(name, shape, dt, offset=offset), offset + (size + 31) // 32 * 32

        def sb(name, shape, dt=F32):
            return at(name, shape, dt)[0]

        top[0] = (nc.sbuf_base + 31) // 32 * 32
        raw = [sb(f"raw{s}", [P, BLK]) for s in range(2)]
        whi = [sb(f"whi{s}", [P, BLK], F32R) for s in range(2)]
        wlo = [sb(f"wlo{s}", [P, BLK], F32R) for s in range(2)]
        split_at = top[0]
        hh = sb("h_hi", [P, KT, SEQ], F32R)
        hl = sb("h_lo", [P, KT, SEQ], F32R)
        xT = sb("x_res", [P, KT, SEQ])
        mats = sb("mats", [P, NC128, P])
        colA = sb("colA", [P, NA])
        colB = sb("colB", [P, NB])
        modc = sb("modc", [P, 48])
        sc = sb("small", [P, 512])
        U = top[0]

        def m(n):
            return mats[:, n, :]

        ident = m(C_ID)
        eps = sc[:, 0:1]
        lams = sc[:, 1:8]
        sinks = sc[:, 8:16]
        dtb, alog = sc[:, 16:20], sc[:, 20:24]
        qcol, kcol, nw1, dncol, subcol = sc[:, 24:25], sc[:, 25:26], sc[:, 26:34], sc[:, 34:35], sc[:, 35:36]
        g1c, g2c, gfc = sc[:, 36:44], sc[:, 44:52], sc[:, 52:60]
        csil = sc[:, 60:68]
        beta, gdec, gc, egc, tail, bege, glst = (sc[:, 80 + 16 * k:96 + 16 * k] for k in range(7))
        ba_tok = sc[:, 192:224].rearrange("p (c e) -> p c e", c=TT)
        sa, sb_, sr, sl = (sc[:, 224 + 16 * k:240 + 16 * k] for k in range(4))
        ea = sc[:, 288:292]
        mx = [sc[:, 300 + 8 * k:301 + 8 * k] for k in range(4)]
        st = [sc[:, 340 + 8 * k:348 + 8 * k] for k in range(4)]
        select = sc[:, 380:475]

        def col(name, n=0):
            return colA[:, ROWS_A[name] + n:ROWS_A[name] + n + 1]

        top[0] = U
        qkv = sb("dn_qkv", [P, 12, SEQ])
        zs = sb("dn_z", [P, 4, SEQ])
        gate = sb("att_gate", [P, 4, SEQ])
        qk_att = sb("att_qk", [P, 8, SEQ])
        v_att = sb("att_v", [P, 4, SEQ])
        V = top[0]
        x_tok = at("x_tok", [P, TT, D], offset=U)[0]
        h_f1 = [at(f"h_f1{s}", [P, SEQ], offset=U + 16384 + 2048 * s)[0] for s in range(2)]
        baT = at("baT", [2 * DN_H, SEQ], offset=V)[0]
        top[0] = V + 2048
        cv = [sb(f"conv{s}", [P, SEQ]) for s in range(2)]
        sq = [sb(f"sq{s}", [P, SEQ]) for s in range(2)]
        ry = [sb(f"ry{s}", [P, SEQ]) for s in range(2)]
        ryy = [sb(f"ryy{s}", [P, SEQ]) for s in range(2)]
        ada_w = [sb(f"ada_w{s}", [P, D]) for s in range(2)]
        ada_acc = [sb(f"ada_acc{s}", [P, D]) for s in range(2)]
        modrow = sb("modrow", [48, P])
        rowsM = sb("rowsM", [48, P])
        rowsA = sb("rowsA", [NA, P])
        rowsB = sb("rowsB", [NB, P])
        lamrow = sb("lamrow", [P, 4 * HD])
        relT = sb("relT", [N_BUCKETS, ATT_H])
        onehot = sb("onehot", [N_BUCKETS, SEQ + P])
        logm = sb("logm", [ATT_H, SEQ + P])
        brow = sb("brow", [ATT_H, SEQ + P])
        ends = [top[0]]
        top[0] = V
        kbe = sb("dn_kbe", [P, TT, DN_H, P])
        ktail = sb("dn_ktail", [P, TT, DN_H, P])
        vb = sb("dn_vb", [P, TT, DN_H, P])
        attnT = sb("dn_attnT", [P, TT, DN_H, P])
        Dk = [sb(f"dn_D{s}", [P, DN_H, P]) for s in range(2)]
        state = sb("dn_state", [P, DN_H, P])
        toe_at = top[0]
        TOE = 5
        toe = [sb(f"toe{h}", [P, SEQ]) for h in range(TOE)]
        toe += [at(f"toe{h}", [P, SEQ], offset=V + 24576 + 2048 * (h - TOE))[0] for h in range(TOE, ATT_H)]
        ends.append(top[0])
        X = at("dn_X", [P, TT, DN_H, P], offset=split_at)[0]
        XT = at("dn_XT", [P, TT, DN_H, P], offset=split_at + 8192)[0]
        AT = at("dn_AT", [P, TT, DN_H, P], offset=split_at + 16384)[0]
        P1 = at("dn_P1", [P, TT, DN_H, P], offset=split_at + 24576)[0]
        top[0] = V
        s_a1 = [sb(f"s_a1{s}", [P, SEQ]) for s in range(2)]
        p_a1 = [sb(f"p_a1{s}", [P, SEQ]) for s in range(2)]
        pT_a1 = [sb(f"pT_a1{s}", [P, SEQ]) for s in range(2)]
        mixf = [sb(f"mixf{s}", [P, SEQ]) for s in range(2)]
        nsq = [sb(f"nsq{s}", [P, SEQ]) for s in range(2)]
        nry = [sb(f"nry{s}", [P, SEQ]) for s in range(2)]
        nhf = [sb(f"nhf{s}", [P, SEQ]) for s in range(2)]
        top[0] = U
        q_a2 = sb("swa_q", [P, 4, SEQ])
        k_a2 = sb("swa_k", [P, 2, SEQ])
        v_a2 = sb("swa_v", [P, TT, P])
        q_a3 = sb("diff_q", [P, 4, SEQ])
        k_a3 = sb("diff_k", [P, 4, SEQ])
        v_a3 = sb("diff_v", [P, TT, SEQ])
        vf = sb("v_fm", [P, 5, SEQ])
        sg = sb("gates", [P, 16, SEQ])
        s_a3 = [sb(f"s_a3{s}", [P, SEQ]) for s in range(4)]
        p_a3 = [sb(f"p_a3{s}", [P, SEQ]) for s in range(2)]
        pT_a3 = [sb(f"pT_a3{s}", [P, SEQ]) for s in range(2)]
        of = [sb(f"of{s}", [P, SEQ]) for s in range(2)]
        osq = sb("osq", [P, SEQ])
        ory = [sb(f"ory{s}", [P, SEQ]) for s in range(2)]
        ends.append(top[0])
        abase = sb("abase", [P, SEQ + 2 * P])
        ends.append(top[0])
        top[0] = U
        mh = sb("merged_hi", [P, KT, SEQ], F32R)
        ml = sb("merged_lo", [P, KT, SEQ], F32R)
        top[0] = V + 16384
        mA, mD, mS = ([sb(f"m{k}{s}", [P, SEQ]) for s in range(2)] for k in "ADS")
        top[0] = U
        fh = sb("ffn_hi", [P, FT, SEQ], F32R)
        fl = sb("ffn_lo", [P, FT, SEQ], F32R)
        top[0] = V + 16384 + 6 * 2048
        fc = [sb(f"fc{s}", [P, SEQ]) for s in range(2)]
        fg = [sb(f"fg{s}", [P, SEQ]) for s in range(2)]
        ff = [sb(f"ff{s}", [P, SEQ]) for s in range(2)]
        ends.append(top[0])
        top[0] = U
        yT = sb("yT", [P, KT, SEQ])
        y_tok = sb("y_tok", [P, TT, D])
        assert max(ends) <= nc.sbuf_usable_end

        bank = [ctx.enter_context(nc.psum_tensor(f"bank{b}", [P, SEQ], F32)) for b in range(8)]

        def four(ap):
            return ap.rearrange("p (h i) -> p h i", h=4)

        def over(ap, n=P):
            return ap.rearrange("p (h o) -> p h o", o=1).to_broadcast([P, 4, n])

        def each(ap):
            return ap.rearrange("p (o i) -> p o i", o=1).to_broadcast([P, 4, P])

        class Signals(dict):

            def __missing__(self, name):
                self[name] = ctx.enter_context(nc.semaphore(name))
                return self[name]

        S = Signals()

        def before(tag, what):
            n = int(tag[1])
            if tag[0] == "n":
                return n if what == "rs" else KT * n - KT * (n > 0 and what == "aff")
            return (n - 1) * (4 if what in ("out", "hi", "lo") else 32)

        class Chain:

            def __init__(self, eng, name):
                self.eng, self.sem, self.n = eng, S[name], 0

            def __call__(self, ins):
                ins.then_inc(self.sem, 1)
                self.n += 1
                self.eng.wait_ge(self.sem, self.n)

        w_in = a["w_in"][0].rearrange("(k p) c -> p k c", p=P)
        w_out = a["w_out"][0].rearrange("(k p) c -> p k c", p=P)
        w_in2 = a["w_in_2"][0].rearrange("(k p) c -> p k c", p=P)
        w_out2 = a["w_out_2"][0].rearrange("(k p) c -> p k c", p=P)
        w_bs = a["w_branch_swa_2"][0].rearrange("(k p) c -> p k c", p=P)
        w_bd = a["w_branch_diff_2"][0].rearrange("(k p) c -> p k c", p=P)
        w_up = a["w_up_2"][0].rearrange("(k p) c -> p k c", p=P)
        w_dn = a["w_down_2"][0].rearrange("(k p) c -> p k c", p=P)
        N_S1, N_S2, N_S3, N_S4, N_S5, N_S6 = 17, 21, 38, 42, 46, 68
        T_S1, T_S2, T_S3, T_S4, T_S5 = 33, 41, 75, 91, 99
        ADA_STEP = {n: 3 for n in range(16)}
        OFFS = [256 * n for n in range(6)] + [2048] + [1536, 1792] + [2056 + 256 * n for n in range(8)]

        def norm_of(n):
            if n < 4:
                return [2 * n, 2 * n + 1]
            return [8 + 2 * (n - 9), 9 + 2 * (n - 9)] if 9 <= n < 13 else []

        def tiles_of(n):
            return [2 * n, 2 * n + 1] if n < 6 else [12] if n == 6 else [13 + 2 * (n - 7), 14 + 2 * (n - 7)]

        def fold_at(n):
            before = sum(v for k, v in ADA_STEP.items() if k < n - 1)
            after = sum(v for k, v in ADA_STEP.items() if k < n)
            return range(before // 8, after // 8)

        block = ctx.enter_context(nc.Block())

        @block.sync
        def _(sp):
            def weights(n, dsts, i=0):
                s, use = n % 2, n // 2 + i
                if n >= 2:
                    sp.wait_ge(S["hi_ready"], n - 1 + 2 * i)
                    sp.wait_ge(S["lo_ready"], n - 1 + 2 * i)
                for dst, src in dsts(raw[s]):
                    sp.dma_start(dst, src).then_inc(S[f"raw_full{s}"], 16)

            def cols(w, c, width=256):
                def dsts(r):
                    v = r[:, :].rearrange("p (k c) -> p k c", k=KT)
                    return [(v[:, 4 * h:4 * h + 4, 0:width], w[:, 4 * h:4 * h + 4, bass.ds(c, width)])
                            for h in range(2)]
                return dsts

            sp.dma_start(mats[:, C_ID, :], a["k_mats"][:, 0:P]).then_inc(S["x_in_ident"], 16)
            for t in range(TT):
                sp.dma_start(x_tok[:, t, :], a["x"][0, t * P:(t + 1) * P, :]).then_inc(S[f"x_in{t}"], 16)
            for n in range(17):
                if n == 6:
                    weights(n, cols(w_in, OFFS[n], P))
                else:
                    weights(n, cols(w_in, OFFS[n]))
            for j in range(4):
                weights(N_S1 + j, cols(w_out, 256 * j))
            with sp.Fori(0, 8) as i:
                for s in range(2):
                    weights(N_S2 + s, cols(w_in2, 512 * i + 256 * s), i)
            weights(N_S2 + 16, cols(w_in2, 4096))
            for j in range(4):
                def both(r, j=j):
                    v = r[:, :].rearrange("p (g k c) -> p g k c", g=2, k=4)
                    return [(v[:, 0], w_bs[:, :, 256 * j:256 * j + 256]),
                            (v[:, 1], w_bd[:, :, 256 * j:256 * j + 256])]
                weights(N_S3 + j, both)
            for j in range(4):
                weights(N_S4 + j, cols(w_out2, 256 * j))
            with sp.Fori(0, 11) as i:
                for s in range(2):
                    def pair(r, s=s):
                        v = r[:, :].rearrange("p (k g c) -> p k g c", k=KT, g=2)
                        return [(v[:, :, g, :], w_up[:, :, bass.ds(g * DFF + s * P + 2 * P * i, P)])
                                for g in range(2)]
                    weights(N_S5 + s, pair, i)

            def down(n, i=0):
                def rows(r):
                    v = r[:, :].rearrange("p (k c) -> p k c", k=2)
                    j = n - N_S6
                    return [(v[:, h, :], w_dn[:, bass.ds(2 * j + h + 4 * i, 1), :].rearrange("p k c -> p (k c)"))
                            for h in range(2)]
                weights(n, rows, i)

            with sp.Fori(0, 5) as i:
                for s in range(2):
                    down(N_S6 + s, i)
            down(N_S6 + 10)
            for t in range(TT):
                for h in range(2):
                    sp.wait_ge(S[f"y_out{h}"], t + 1)
                    sp.dma_start(out[0, t * P:(t + 1) * P, h * 512:(h + 1) * 512],
                                 y_tok[:, t, h * 512:(h + 1) * 512]).then_inc(S["out_done"], 16)
            sp.wait_ge(S["out_done"], 16 * 2 * TT)

        def start_xt(pool, c):
            pool.wait_ge(S["dn_at"], 2 * c + 1)
            pool.tensor_tensor(XT[:, c], AT[:, c], each(m(C_NMT0)), ALU.mult).then_inc(S["dn_xt0"], 1)
            pool.wait_ge(S["dn_xt0"], 2 * c + 1)
            pool.tensor_tensor(XT[:, c], XT[:, c], each(ident), ALU.add).then_inc(S["dn_xt0"], 1)

        @block.gpsimd
        def _(pool):
            pool.dma_start(relT[:, :], a["rel_bias"].rearrange("h b -> b h"), allow_slow_non_contiguous=True).then_inc(S["in_rel"], 16)
            pool.dma_start(onehot[:, :], a["k_onehot"]).then_inc(S["in_rel"], 16)
            pool.dma_start(logm[:, :], a["k_logm"].to_broadcast([ATT_H, SEQ + P])).then_inc(S["in_rel"], 16)
            pool.dma_start(rowsM[:, :], a["b_ada_2"].rearrange("o (j p) -> (o j) p", p=P)).then_inc(S["in_rowsM"], 16)

            def lo(n, i=0):
                s = n % 2
                pool.wait_ge(S["hi_ready"], n + 1 + 2 * i)
                pool.tensor_tensor(wlo[s][:, :], raw[s][:, :], whi[s][:, :].bitcast(F32), ALU.subtract)\
                    .then_inc(S["lo_ready"], 1)

            def ada_load(p):
                c, kt = divmod(p, KT)
                pool.dma_start(ada_w[p % 2][:, :], a["w_ada_2"][0, kt * P:(kt + 1) * P, c * D:(c + 1) * D])\
                    .then_inc(S[f"ada_in{p % 2}"], 16)

            ada_load(0)
            ada_load(1)
            lo(0)
            p = 2
            for n in range(17):
                lo(n + 1)
                for _ in range(ADA_STEP.get(n, 0)):
                    if p < 48:
                        pool.wait_ge(S["ada_piece"], p - 1)
                        ada_load(p)
                        p += 1
            pool.wait_ge(S["mod_ready"], 1)
            pool.wait_ge(S["toep_out"], 16)
            pool.wait_ge(S["tile_ready"], T_S1)

            def toeplitz(h):
                pool.dma_start(toe[h][:, :], bass.AP(toep.tensor, h * P * (SEQ + P) + P - 1, [[SEQ + P - 1, P], [1, SEQ]]))\
                    .then_inc(S[f"toe_in{h}"], 16)

            for h in range(TOE):
                toeplitz(h)
            for c in range(TT):
                if c == 0:
                    pool.wait_ge(S["g_ready"], 1)
                if c >= 2:
                    pool.wait_ge(S["dn_grow"], c - 1)
                    pool.wait_ge(S["dn_brow"], c - 1)
                pool.tensor_tensor(P1[:, c % 2], over(gdec[:, 4 * c:4 * c + 4]), each(m(C_TRIU)), ALU.mult).then_inc(S["dn_gtri"], 1)
                pool.tensor_tensor(P1[:, 2 + c % 2], over(beta[:, 4 * c:4 * c + 4]), each(ident), ALU.mult).then_inc(S["dn_gtri"], 1)
                if c >= 1:
                    start_xt(pool, c - 1)
            start_xt(pool, TT - 1)
            pool.wait_ge(S["dn_o"], 4)
            for h in range(TOE, ATT_H):
                toeplitz(h)
            pool.wait_ge(S["att_out"], 4)
            pool.dma_start(abase[:, :], a["k_alibi"]).then_inc(S["in_alibi"], 16)
            for n in range(N_S1 + 1, N_S2 + 10):
                lo(n)
            with pool.Fori(0, 4) as i:
                for s in range(2):
                    lo(N_S2 + 10 + s, i)
            for n in range(N_S2 + 18, N_S5 + 1):
                lo(n)
            with pool.Fori(0, 16) as i:
                for s in range(2):
                    lo(N_S5 + 1 + s, i)

        def units_a1():
            for h in range(ATT_H):
                for i in range(TT):
                    r = slice(64 * (h % 2), 64 * (h % 2) + 64)
                    yield dict(maps=[dict(q=qk_att[r, h // 2, i * P:(i + 1) * P], k=qk_att[r, 4 + h // 2, 0:(i + 1) * P],
                                          bias=toe[h][:, (3 - i) * P:], sink=None, slope=1.0)],
                               n=i + 1, v=[v_att[:, j, h * HD:(h + 1) * HD] for j in range(i + 1)],
                               out=(r, slice(i * P, (i + 1) * P)), group=h // 2, last=h % 2 == 1 and i == 3,
                               head=h, new=(h % 2, i) == (0, 0))

        def units_a2():
            for h in range(ATT_H):
                for i in range(TT):
                    r = slice(64 * (h % 2), 64 * (h % 2) + 64)
                    j0 = max(i - 1, 0)
                    yield dict(maps=[dict(q=q_a2[r, h // 2, i * P:(i + 1) * P], k=k_a2[r, h // 4, j0 * P:(i + 1) * P],
                                          bias=abase[:, SEQ + (1 - (i - j0)) * P:SEQ + 2 * P], sink=sinks[:, h:h + 1],
                                          slope=SWA_SLOPES[h])],
                               n=i + 1 - j0, v=[v_a2[:, j, (h // 4) * HD:(h // 4 + 1) * HD] for j in range(j0, i + 1)],
                               out=(r, slice(i * P, (i + 1) * P)), group=h // 2, last=h % 2 == 1 and i == 3,
                               head=h, new=(h % 2, i) == (0, 0))

        def units_a3():
            for h in range(DN_H):
                for i in range(TT):
                    yield dict(maps=[dict(q=q_a3[64 * mp:64 * mp + 64, h, i * P:(i + 1) * P],
                                          k=k_a3[64 * mp:64 * mp + 64, h, 0:(i + 1) * P],
                                          bias=abase[:, (3 - i) * P:SEQ], sink=None, slope=DIFF_SLOPES[h]) for mp in range(2)],
                               n=i + 1, v=[v_a3[:, j, h * P:(h + 1) * P] for j in range(i + 1)],
                               out=(slice(0, P), slice(i * P, (i + 1) * P)), group=h, last=i == 3,
                               head=h, new=i == 0)

        QK, TB, OB = (2, 3), (4, 5), (6, 7)
        bufs = {"a1": (s_a1, p_a1, pT_a1), "a2": (s_a3, p_a3, pT_a3), "a3": (s_a3, p_a3, pT_a3)}

        def tiles_through(n):
            if n < N_S1:
                return tiles_of(n)[-1] + 1
            for first, T, per in ((N_S5, T_S5, 2), (N_S4, T_S4, 2), (N_S3, T_S3, 4), (N_S2, T_S2, 2), (N_S1, T_S1, 2)):
                if n >= first:
                    return T + per * (n - first + 1)

        def slot_free(eng, n, i=0):
            if n >= N_S6 + 2:
                eng.wait_ge(S["block_done"], n - N_S6 - 1 + 2 * i)
            elif n >= 2:
                eng.wait_ge(S["tile_ready"], tiles_through(n - 2) + 4 * i)

        def ring(T):
            return bank[(0, 1, 6, 7)[T % 4]]

        def gate_bank(T):
            return bank[T % 2]

        GATE_T = T_S2 + 18
        GATE_N = N_S2 + 9
        GATE_STEPS = 8 * 2 * KT
        swa_steps = lambda w: min(w + 1, 32)
        diff_steps = lambda w: min(32 + 6 * (w + 1), GATE_STEPS)

        def tiles_done(steps, w):
            return range((steps(w - 1) if w or steps is diff_steps else 0) // KT, steps(w) // KT)

        def branch_out(k):
            return q_a2[:, k, :] if k < 4 else q_a3[:, k - 4, :]

        def evac(eng, T, i=0):
            eng.wait_ge(S[f"evac{T % 4}"], T // 4 + 1 + i)

        @block.tensor
        def _(pe):
            def bank_free(T, i=0):
                if T >= 4:
                    pe.wait_ge(S[f"evac{T % 4}"], T // 4 + i)

            def three(ps, lo, wcol, h_hi, h_lo, start, stop):
                wh, wl = whi[lo][:, wcol:wcol + P], wlo[lo][:, wcol:wcol + P]
                pe.matmul(ps, wh, h_hi, start=start, stop=False)
                pe.matmul(ps, wh, h_lo, start=False, stop=False)
                return pe.matmul(ps, wl, h_hi, start=False, stop=stop)

            def gemm(n, T, us=(0, 1), acts=None, ks=KT, stride=256, first=0, ready=None, i=0):
                ah, al = acts or (hh, hl)
                pe.wait_ge(S["lo_ready"], n + 1 + 2 * i)
                for k, u in enumerate(us):
                    bank_free(T + k, i)
                    for kt in range(ks):
                        if ready and k == 0:
                            pe.wait_ge(ready[0], ready[1] + kt)
                        mm = three(ring(T + k)[:, :], n % 2, kt * stride + u * P + first,
                                   ah[:, kt, :], al[:, kt, :], kt == 0, kt == ks - 1)
                    mm.then_inc(S["tile_ready"], 1)

            def norm_sum(tag, b, kt):
                pe.wait_ge(S["rms_sq"], before(tag, "sq") + kt + 1)
                pe.matmul(bank[b][:, :], m(C_INVD), (sq if tag == "n0" else nsq)[kt % 2][:, :],
                          start=kt == 0, stop=kt == KT - 1).then_inc(S["rms_sum"], 1)

            pe.wait_ge(S["x_in_ident"], 16)
            for t in range(TT):
                pe.wait_ge(S[f"x_in{t}"], 16)
            for kt in range(KT):
                for t in range(TT):
                    mm = pe.transpose(bank[kt][:, t * P:(t + 1) * P], x_tok[:, t, kt * P:(kt + 1) * P], ident)
                mm.then_inc(S["xt_done"], 1)
            pe.wait_ge(S["xT_ready"], 3)
            pe.wait_ge(S["in_rowsA"], 16 * 13)
            pe.transpose(bank[1][:, 0:NA], rowsA[:, :], ident[0:NA, 0:NA]).then_inc(S["vecs_done"], 1)
            pe.wait_ge(S["in_rowsB"], 16)
            pe.transpose(bank[2][:, 0:NB], rowsB[:, :], ident[0:NB, 0:NB]).then_inc(S["vecs_done"], 1)
            pe.wait_ge(S["in_mats"], 16)
            for kt in range(KT):
                norm_sum("n0", 0, kt)
            pe.wait_ge(S["xT_ready"], 5)
            pe.wait_ge(S["in_rel"], 48)
            pe.matmul(bank[3][0:ATT_H, :], relT[:, :], onehot[:, 0:SEQ], start=True, stop=True)
            pe.matmul(bank[4][0:ATT_H, 0:P], relT[:, :], onehot[:, SEQ:], start=True, stop=True)\
                .then_inc(S["rel_done"], 1)

            def fold(c):
                pe.wait_ge(S["ada_piece"], 8 * (c + 1))
                for j in range(8):
                    jj = 8 * c + j
                    mm = pe.matmul(bank[5][0:48, 0:P], select[:, 47 - jj:95 - jj], ada_acc[c % 2][:, j * P:(j + 1) * P],
                                   start=jj == 0, stop=jj == 47)
                mm.then_inc(S["ada_fold"], 1)

            for n in range(17):
                if n == 0:
                    pe.wait_ge(S["rms_hf"], before("n0", "hf") + 1)
                    pe.wait_ge(S["xT_ready"], 8)
                    pe.wait_ge(S["cols_ready"], 2)
                gemm(n, tiles_of(n)[0], (0,) if n == 6 else (0, 1), ready=(S["rms_lo"], before("n0", "lo") + 1) if n == 0 else None)
                if n >= 1:
                    for k in norm_of(n - 1):
                        pe.wait_ge(S["sq_done"], k + 1)
                        if k == 0:
                            pe.wait_ge(S["brow_ready"], 2)
                        if k >= 2:
                            pe.wait_ge(S["nt_done"], k - 1)
                        pe.matmul(bank[2 + k % 2][:, :], m(C_ONE if k < 8 else C_BLK), sq[k % 2][:, :],
                                  start=True, stop=True).then_inc(S["sum_done"], 1)
                if n == 7:
                    evac(pe, 12)
                    pe.wait_ge(S["brow_ready"], 2)
                    for t in range(TT):
                        mm = pe.transpose(bank[4][:, 8 * t:8 * t + 8], baT[:, t * P:(t + 1) * P], ident[0:8, 0:8])
                    mm.then_inc(S["ba_tr"], 1)
                for c in fold_at(n):
                    if c == 0:
                        pe.wait_ge(S["xT_ready"], 8)
                    fold(c)
            for c in fold_at(17):
                fold(c)
            pe.wait_ge(S["modrow_ready"], 1)
            pe.transpose(bank[4][:, 0:48], modrow[:, :], ident[0:48, 0:48]).then_inc(S["mod_tr"], 1)
            pe.wait_ge(S["nt_done"], 16)
            for T in range(29, 33):
                evac(pe, T)
            for t in range(TT):
                for f in range(4):
                    mm = pe.transpose(bank[(2, 3, 6, 7)[t]][:, f * P:(f + 1) * P], v_att[:, f, t * P:(t + 1) * P], ident)
            mm.then_inc(S["v_tr"], 1)

            pe.wait_ge(S["norm_done"], 8)
            pe.wait_ge(S["g_ready"], 1)
            pe.matmul(bank[5][:, 0:16], m(C_TRIU), gdec, start=True, stop=True).then_inc(S["dn_gct"], 1)
            pe.wait_ge(S["v_ready"], 4)
            for c in range(TT):
                pe.wait_ge(S["dn_gtri"], 2 * c + 2)
                if c >= 2:
                    pe.wait_ge(S["dn_exp"], c - 1)
                    pe.wait_ge(S["dn_dtb"], c - 1)
                pe.matmul(bank[c % 2][:, :], m(C_ONE), P1[:, c % 2].rearrange("p h i -> p (h i)"), start=True, stop=True)\
                    .then_inc(S["dn_grow"], 1)
                pe.matmul(bank[2 + c % 2][:, :], m(C_ONE), P1[:, 2 + c % 2].rearrange("p h i -> p (h i)"),
                          start=True, stop=True).then_inc(S["dn_brow"], 1)
                if c == 0:
                    pe.wait_ge(S["dn_egc"], 1)
                    pe.wait_ge(S["mod_ready"], 1)
                if c >= 1:
                    pe.wait_ge(S["dn_at"], 2 * c)
                tok = slice(c * P, (c + 1) * P)
                for h in range(DN_H):
                    pe.matmul(bank[5][:, h * P:(h + 1) * P], qkv[:, 4 + h, tok], qkv[:, 4 + h, tok], start=True, stop=True)
                for h in range(DN_H):
                    mm = pe.matmul(bank[6][:, h * P:(h + 1) * P], qkv[:, 4 + h, tok], qkv[:, h, tok], start=True, stop=True)
                mm.then_inc(S["dn_prod"], 1)
                for b, f in ((4, 4), (7, 8)):
                    if c >= 1:
                        pe.wait_ge(S["dn_kv"], 2 * c if b == 4 else 2 * c)
                    if b == 7 and c >= 1:
                        pe.wait_ge(S["dn_x"], c)
                    for h in range(DN_H):
                        mm = pe.transpose(bank[b][:, h * P:(h + 1) * P], qkv[:, f + h, tok], ident)
                    mm.then_inc(S["dn_ktr"], 1)
                pe.wait_ge(S["dn_at"], 2 * c + 1)
                pe.wait_ge(S["dn_kv"], 2 * c + 2)
                for h in range(DN_H):
                    mm = pe.transpose(bank[7][:, h * P:(h + 1) * P], AT[:, c, h, :], ident)
                mm.then_inc(S["dn_a"], 1)

            def prod1(l, c):
                pe.wait_ge(S["dn_x"] if l == 0 else S["dn_upd"], 4 if l == 0 else 4 * (l - 1) + c + 1)
                if l == 0:
                    pe.wait_ge(S["dn_dtb"], 4)
                    pe.wait_ge(S["dn_xt0"], 8)
                for h in range(DN_H):
                    mm = pe.matmul(bank[c % 2][:, h * P:(h + 1) * P], AT[:, c, h, :], X[:, c, h, :], start=True, stop=True)
                mm.then_inc(S["dn_p1"], 1)

            def prod2(l, c):
                pe.wait_ge(S["dn_p1s"], 4 * l + c + 1)
                if l * 4 + c >= 2:
                    pe.wait_ge(S["dn_upd"], 4 * l + c - 1)
                for h in range(DN_H):
                    if l < N_LVL - 1:
                        pe.matmul(bank[2 + c % 2][:, h * P:(h + 1) * P], XT[:, c, h, :], P1[:, c, h, :], start=True, stop=True)
                for h in range(DN_H):
                    mm = pe.matmul(bank[4 + c % 2][:, h * P:(h + 1) * P], P1[:, c, h, :], XT[:, c, h, :], start=True, stop=True)
                mm.then_inc(S["dn_z"], 1)

            for l in range(N_LVL):
                prod1(l, 0)
                for c in range(TT):
                    if c + 1 < TT:
                        prod1(l, c + 1)
                    prod2(l, c)
            for c in range(TT):
                pe.wait_ge(S["dn_upd"], 4 * (N_LVL - 1) + c + 1)
                if c >= 1:
                    pe.wait_ge(S["dn_u"], c)
                    pe.wait_ge(S["dn_w"], c)
                for h in range(DN_H):
                    pe.matmul(bank[6][:, h * P:(h + 1) * P], XT[:, c, h, :], vb[:, c, h, :], start=True, stop=True)
                for h in range(DN_H):
                    mm = pe.matmul(bank[7][:, h * P:(h + 1) * P], kbe[:, c, h, :], XT[:, c, h, :], start=True, stop=True)
                mm.then_inc(S["dn_uw"], 1)
            for c in range(TT):
                tok = slice(c * P, (c + 1) * P)
                if c >= 1:
                    pe.wait_ge(S["dn_s"], c)
                    for h in range(DN_H):
                        mm = pe.matmul(bank[0][:, h * P:(h + 1) * P], kbe[:, c, h, :], state[:, h, :], start=True, stop=True)
                    mm.then_inc(S["dn_ws"], 1)
                pe.wait_ge(S["dn_vn"], c + 1)
                if c < TT - 1:
                    for h in range(DN_H):
                        mm = pe.matmul(bank[1][:, h * P:(h + 1) * P], ktail[:, c, h, :], P1[:, c % 2, h, :], start=True, stop=True)
                    mm.then_inc(S["dn_su"], 1)
                ob = (4, 5, 6, 7)[c]
                if c == 0:
                    pe.wait_ge(S["dn_u"], 4)
                    pe.wait_ge(S["dn_w"], 4)
                for h in range(DN_H):
                    if c >= 1:
                        pe.matmul(bank[ob][:, h * P:(h + 1) * P], state[:, h, :], qkv[:, h, tok], start=True, stop=False)
                    mm = pe.matmul(bank[ob][:, h * P:(h + 1) * P], P1[:, c % 2, h, :], attnT[:, c, h, :],
                                   start=c == 0, stop=True)
                mm.then_inc(S["dn_o"], 1)
            for c in range(TT):
                pe.wait_ge(S["dn_osq"], c + 1)
                if c >= 2:
                    pe.wait_ge(S["dn_mix"], c - 1)
                pe.matmul(bank[2 + c % 2][:, :], m(C_INVH), Dk[c % 2][:, :, :].rearrange("p h i -> p (h i)"),
                          start=True, stop=True).then_inc(S["dn_osum"], 1)
            pe.wait_ge(S["dn_lo"], 4)

            def attention(tag, units, tail=None):
                units = list(units)
                p_, pT_ = bufs[tag][1:]
                M = len(units[0]["maps"])
                maps = [mp for u in units for mp in u["maps"]]

                def qk(g):
                    if g >= len(maps):
                        return
                    if g >= 2:
                        pe.wait_ge(S["att_s"], before(tag, "s") + g - 1)
                    mp = maps[g]
                    pe.matmul(bank[QK[g % 2]][:, 0:mp["k"].shape[-1]], mp["q"], mp["k"], start=True, stop=True)\
                        .then_inc(S["att_qk"], 1)

                def turn(w):
                    pe.wait_ge(S["att_p"], before(tag, "p") + w + 1)
                    if w >= 2:
                        pe.wait_ge(S["att_pT"], before(tag, "pT") + w - 1)
                    for j in range(units[w]["n"]):
                        mm = pe.transpose(bank[TB[w % 2]][:, j * P:(j + 1) * P], p_[w % 2][:, j * P:(j + 1) * P], ident)
                    mm.then_inc(S["att_t"], 1)

                def values(w):
                    u = units[w]
                    pe.wait_ge(S["att_pT"], before(tag, "pT") + w + 1)
                    if u["new"] and u["group"] >= 2:
                        pe.wait_ge(S["att_out"], before(tag, "out") + u["group"] - 1)
                        if tag == "a3":
                            pe.wait_ge(S["d_mix"], u["group"] - 1)
                    r, c = u["out"]
                    for j in range(u["n"]):
                        mm = pe.matmul(bank[OB[u["group"] % 2]][r, c], u["v"][j], pT_[w % 2][:, j * P:(j + 1) * P],
                                       start=j == 0, stop=j == u["n"] - 1)
                    mm.then_inc(S["att_pv"], 1)

                for g in range(2 * M):
                    qk(g)
                for w in range(len(units)):
                    for g in range(M * (w + 2), M * (w + 3)):
                        qk(g)
                    if w >= 1:
                        values(w - 1)
                    if tail:
                        tail(w)
                    turn(w)
                values(len(units) - 1)
                if tail:
                    for w in range(3):
                        tail(len(units) + w)

            attention("a1", units_a1())

            for j in range(4):
                if j == 0:
                    pe.wait_ge(S["att_lo"], before("a1", "lo") + 4)
                gemm(N_S1 + j, T_S1 + 2 * j)
                for kt in (2 * j - 2, 2 * j - 1):
                    if kt >= 0:
                        norm_sum("n1", 2, kt)
            norm_sum("n1", 2, 6)
            norm_sum("n1", 2, 7)

            gemm(N_S2, T_S2, ready=(S["rms_lo"], before("n1", "lo") + 1))
            for j in range(1, 9):
                gemm(N_S2 + j, T_S2 + 2 * j)

            def gate_steps(steps, w):
                for k in range(steps(w - 1) if w or steps is diff_steps else 0, steps(w)):
                    t, kt = divmod(k, KT)
                    n, T = GATE_N + t // 2, GATE_T + t
                    if kt == 0:
                        pe.wait_ge(S["lo_ready"], n + 1)
                        evac(pe, T - 2)
                    mm = three(gate_bank(T)[:, :], n % 2, kt * 256 + (t % 2) * P, hh[:, kt, :], hl[:, kt, :],
                               kt == 0, kt == KT - 1)
                    if kt == KT - 1:
                        mm.then_inc(S["tile_ready"], 1)

            for T in range(GATE_T - 4, GATE_T):
                evac(pe, T)
            for t in range(TT):
                pe.transpose(bank[6][:, t * P:(t + 1) * P], vf[:, 0, t * P:(t + 1) * P], ident)
            for t in range(TT):
                for f in range(4):
                    mm = pe.transpose(bank[2 + t][:, f * P:(f + 1) * P], vf[:, 1 + f, t * P:(t + 1) * P], ident)
            mm.then_inc(S["v2_tr"], 1)
            pe.wait_ge(S["v2_ready"], 5)
            attention("a2", units_a2(), lambda w: gate_steps(swa_steps, w))

            def diff_norm(w):
                gate_steps(diff_steps, w)
                if w >= 6 and (w - 6) % 4 == 0:
                    h = (w - 6) // 4
                    pe.wait_ge(S["d_sq"], h + 1)
                    pe.matmul(bank[OB[h % 2]][:, :], m(C_INVH), osq[:, :], start=True, stop=True).then_inc(S["d_sum"], 1)

            attention("a3", units_a3(), diff_norm)

            evac(pe, T_S3 - 2)
            evac(pe, T_S3 - 1)
            for j in range(4):
                pe.wait_ge(S["lo_ready"], N_S3 + j + 1)
                for u in range(2):
                    for g in range(2):
                        T = T_S3 + 4 * j + 2 * u + g
                        bank_free(T)
                        for kt in range(4):
                            if T < T_S3 + 2:
                                pe.wait_ge(S["att_lo"], before("a3" if g else "a2", "lo") + kt + 1)
                            mm = three(ring(T)[:, :], (N_S3 + j) % 2, g * 1024 + kt * 256 + u * P,
                                       hh[:, 4 * g + kt, :], hl[:, 4 * g + kt, :], kt == 0, kt == 3)
                        mm.then_inc(S["tile_ready"], 1)
            for j in range(4):
                gemm(N_S4 + j, T_S4 + 2 * j, acts=(mh, ml), ready=(S["mg_lo"], 1) if j == 0 else None)
                for kt in (2 * j - 2, 2 * j - 1):
                    if kt >= 0:
                        norm_sum("n2", 2, kt)
            norm_sum("n2", 2, 6)
            norm_sum("n2", 2, 7)
            pe.wait_ge(S["rms_lo"], before("n2", "lo") + 8)
            with pe.Fori(0, 11) as i:
                for s in range(2):
                    gemm(N_S5 + s, T_S5 + 2 * s, i=i)
            for T in range(T_S5 + 40, T_S5 + 44):
                evac(pe, T)
            pe.wait_ge(S["f_lo"], FT)

            def down(n, i=0, start=False, stop=False):
                pe.wait_ge(S["lo_ready"], n + 1 + 2 * i)
                for t in range(KT):
                    for h in range(2):
                        kt = bass.ds(2 * (n - N_S6) + h + 4 * i, 1)
                        mm = three(bank[t][:, :], n % 2, h * 1024 + t * P,
                                   fh[:, kt, :].rearrange("p k c -> p (k c)"), fl[:, kt, :].rearrange("p k c -> p (k c)"),
                                   start and h == 0, stop and h == 1)
                    if stop:
                        mm.then_inc(S["tile_ready"], 1)
                if not stop:
                    mm.then_inc(S["block_done"], 1)

            down(N_S6, start=True)
            with pe.Fori(0, 4) as i:
                down(N_S6 + 1, i)
                down(N_S6 + 2, i)
            down(N_S6 + 9)
            down(N_S6 + 10, stop=True)
            pe.wait_ge(S["x3_ready"], 1)
            for kt in range(KT):
                norm_sum("n3", 0, kt)
            for t in range(TT):
                for h in range(2):
                    k = 2 * t + h
                    if k == 0:
                        pe.wait_ge(S["x3_ready"], 8)
                    for f in range(4):
                        pe.wait_ge(S["y_ready"], 4 * h + f + 1)
                        mm = pe.transpose(bank[(k + 1) % 8][:, f * P:(f + 1) * P], yT[:, 4 * h + f, t * P:(t + 1) * P], ident)
                    mm.then_inc(S["y_tr"], 1)

        @block.scalar
        def _(act):
            link = Chain(act, "act_chain")

            def rows(name, src):
                n = ROWS_A[name]
                act.dma_start(rowsA[n:n + src.shape[0], :], src).then_inc(S["in_rowsA"], 16)

            vec = lambda ap: ap.rearrange("o (k p) -> (o k) p", p=P)
            rows("norm_w", vec(a["norm_w"]))
            act.dma_start(mats[:, 1:, :].rearrange("p n c -> p (n c)"), a["k_mats"][:, P:]).then_inc(S["in_mats"], 16)
            rows("norm1_g", vec(a["norm1_g_2"]))
            rows("norm2_g", vec(a["norm2_g_2"]))
            rows("final_g", a["final_g_2"].rearrange("(k p) -> k p", p=P))
            rows("c", vec(a["c_2"]))
            rows("dn_norm_w", a["dn_norm_w"])
            rows("subln", a["diff_subln_g_2"])
            rows("conv_w", a["conv_w"][0].rearrange("k (t p) -> (k t) p", p=P))
            rows("conv_b", vec(a["conv_b_2"]))
            for name, ap in (("q_norm", a["q_norm_w"]), ("k_norm", a["k_norm_w"])):
                n = ROWS_A[name]
                for h in range(2):
                    act.dma_start(rowsA[n:n + 1, h * HD:(h + 1) * HD], ap).then_inc(S["in_rowsA"], 16)
            act.dma_start(rowsB[:, :], a["conv_w_2"][0].rearrange("k (t p) -> (k t) p", p=P)).then_inc(S["in_rowsB"], 16)
            act.dma_start(select, a["k_select"]).then_inc(S["in_small"], 16)
            act.dma_start(sinks, a["swa_sinks_2"].to_broadcast([P, 8])).then_inc(S["in_small"], 16)
            act.dma_start(dtb, a["dt_bias"].to_broadcast([P, DN_H])).then_inc(S["in_small"], 16)
            act.dma_start(alog, a["a_log"].to_broadcast([P, DN_H])).then_inc(S["in_small"], 16)
            act.dma_start(lamrow[:, :], a["diff_lambda_2"].rearrange("o f d -> o (f d)").to_broadcast([P, 4 * HD]))\
                .then_inc(S["in_small"], 16)

            def hi(n, i=0):
                s = n % 2
                act.wait_ge(S[f"raw_full{s}"], 32 * (n // 2 + 1) + 32 * i)
                slot_free(act, n, i)
                act.activation(whi[s][:, :], raw[s][:, :], ACT.Copy).then_inc(S["hi_ready"], 1)

            def squares(tag, kt, src, buf):
                if kt >= 2:
                    act.wait_ge(S["rms_sum"], before(tag, "sum") + kt - 1)
                act.activation(buf[kt % 2][:, :], src, ACT.Square).then_inc(S["rms_sq"], 1)

            def rsqrt(ps, y, yy, done):
                act.preload_act_table_set("natural_log_exp_and_others")
                link(act.activation(yy, ps, ACT.Ln, bias=eps))
                link(act.activation(y, yy, ACT.Exp, scale=-0.5))
                act.activation(yy, y, ACT.Square).then_inc(S[done], 1)

            act.wait_ge(S["scal_done"], 1)
            for kt in range(KT):
                act.wait_ge(S["xT_ready"], kt + 1)
                squares("n0", kt, xT[:, kt, :], sq)
            hi(0)
            act.wait_ge(S["rms_sum"], before("n0", "sum") + KT)
            rsqrt(bank[0][:, :], ry[0][:, :], ryy[0][:, :], "rms_rs")
            for kt in range(KT):
                act.wait_ge(S["rms_hf"], before("n0", "hf") + kt + 1)
                act.activation(hh[:, kt, :], h_f1[kt % 2][:, :], ACT.Copy).then_inc(S["rms_hi"], 1)
            act.wait_ge(S["scal_done"], 2)
            act.activation(lams[:, 2:4], lams[:, 0:2], ACT.Exp).then_inc(S["lam_exp"], 1)
            act.wait_ge(S["cols_ready"], 1)
            act.activation(csil, colA[:, ROWS_A["c"]:ROWS_A["c"] + 8], ACT.Silu).then_inc(S["csil_ready"], 1)

            for n in range(17):
                hi(n + 1)
                if n == 1:
                    act.wait_ge(S["brow_ready"], 2)
                    act.dma_start(toep, brow[:, :].rearrange("h (o x) -> h o x", o=1).to_broadcast([ATT_H, P, SEQ + P]))\
                        .then_inc(S["toep_out"], 16)
                ts = tiles_of(n)
                for T in ts:
                    if n < 6:
                        evac(act, T)
                        act.activation(qkv[:, T, :], cv[T % 2][:, :], ACT.Silu).then_inc(S["silu_done"], 1)
                    elif n in (7, 8, 15, 16):
                        act.wait_ge(S["tile_ready"], T + 1)
                        dst = zs[:, T - 13, :] if n < 9 else gate[:, T - 29, :]
                        act.activation(dst, ring(T)[:, :], ACT.Silu).then_inc(S[f"evac{T % 4}"], 1)
                for k, T in zip(norm_of(n), ts):
                    if k >= 2:
                        act.wait_ge(S["sum_done"], k - 1)
                    if n < 6:
                        act.wait_ge(S["silu_done"], T + 1)
                        src = qkv[:, T, :]
                    else:
                        evac(act, T)
                        src = qk_att[:, T - 17, :]
                    act.activation(sq[k % 2][:, :], src, ACT.Square).then_inc(S["sq_done"], 1)
                if n >= 1:
                    for k in norm_of(n - 1):
                        act.wait_ge(S["sum_done"], k + 1)
                        if k >= 2:
                            act.wait_ge(S["norm_done"], k - 1)
                        rsqrt(bank[2 + k % 2][:, :], ry[k % 2][:, :], ryy[k % 2][:, :], "rs_done")
                if n == 9:
                    act.wait_ge(S["ba_pre"], 1)
                    act.activation(ea, alog, ACT.Exp)
                    link(act.activation(sl, sb_, ACT.Exp, scale=-1.0))
                    act.activation(sl, sl, ACT.Ln, bias=1.0)
                    act.activation(beta.rearrange("p (c h) -> p c h", c=TT), ba_tok[:, :, 0:4], ACT.Sigmoid)\
                        .then_inc(S["ba_act"], 1)

            act.preload_act_table_set("natural_log_exp_and_others")
            act.wait_ge(S["dn_egc"], 1)
            link(act.activation(egc, gc, ACT.Exp))
            for c in range(TT):
                act.wait_ge(S["dn_dsub"], c + 1)
                if c >= 1:
                    act.wait_ge(S["dn_qd"], c)
                act.activation(state[:, :, :], four(bank[c % 2][:, :]), ACT.Exp)
                act.activation(tail[:, 4 * c:4 * c + 4], tail[:, 4 * c:4 * c + 4], ACT.Exp)
                for h in range(DN_H):
                    ins = act.activation(Dk[c % 2][:, h, :], bank[c % 2][:, h * P:(h + 1) * P], ACT.Relu,
                                         bias=gc[:, 4 * c + h:4 * c + h + 1], scale=-1.0)
                link(ins)
                act.activation(Dk[c % 2][:, :, :], Dk[c % 2][:, :, :], ACT.Exp, scale=-1.0).then_inc(S["dn_exp"], 1)
                act.wait_ge(S["bege_ready"], 1)
                act.wait_ge(S["dn_ktr"], 2 * c + 1)
                for h in range(DN_H):
                    ps = bank[4][:, h * P:(h + 1) * P]
                    act.activation(kbe[:, c, h, :], ps, ACT.Copy, scale=bege[:, 4 * c + h:4 * c + h + 1])
                    ins = act.activation(ktail[:, c, h, :], ps, ACT.Copy, scale=tail[:, 4 * c + h:4 * c + h + 1])
                ins.then_inc(S["dn_kv"], 1)
                act.wait_ge(S["dn_ktr"], 2 * c + 2)
                for h in range(DN_H):
                    ins = act.activation(vb[:, c, h, :], bank[7][:, h * P:(h + 1) * P], ACT.Copy,
                                         scale=beta[:, 4 * c + h:4 * c + h + 1])
                ins.then_inc(S["dn_kv"], 1)
            for c in range(TT):
                act.wait_ge(S["dn_uw"], c + 1)
                act.activation(kbe[:, c], four(bank[7][:, :]), ACT.Copy).then_inc(S["dn_w"], 1)

            def osq1(c):
                act.wait_ge(S["dn_o"], c + 1)
                if c >= 2:
                    act.wait_ge(S["dn_osum"], c - 1)
                act.activation(Dk[c % 2][:, :, :], four(bank[4 + c][:, :]), ACT.Square).then_inc(S["dn_osq"], 1)

            osq1(0)
            osq1(1)
            for c in range(TT):
                act.wait_ge(S["dn_osum"], c + 1)
                if c >= 1:
                    act.wait_ge(S["dn_mix"], c)
                rsqrt(four(bank[2 + c % 2][:, :]), P1[:, 2], P1[:, 3], "dn_ors")
                if c + 2 < TT:
                    osq1(c + 2)
                act.wait_ge(S["dn_mix"], c + 1)
                act.activation(hh[:, 0:4, c * P:(c + 1) * P], four(mixf[c % 2][:, :]), ACT.Copy).then_inc(S["dn_hi"], 1)

            def attention(tag, units, tail):
                units = list(units)
                s_, p_, pT_ = bufs[tag]
                M = len(units[0]["maps"])
                maps = [mp for u in units for mp in u["maps"]]

                def exps(w):
                    if w >= len(units):
                        return
                    for g in range(M * w, M * w + M):
                        n = maps[g]["k"].shape[-1]
                        stat = st[g % 4]
                        act.wait_ge(S["att_s"], before(tag, "s") + g + 1)
                        if maps[g]["sink"] is not None:
                            act.activation(stat[:, 4:5], maps[g]["sink"], ACT.Exp, bias=stat[:, 1:2], scale=maps[g]["slope"])
                        act.activation(s_[g % (2 * M)][:, 0:n], s_[g % (2 * M)][:, 0:n], ACT.Exp, bias=stat[:, 1:2], scale=maps[g]["slope"],
                                       accum_out=stat[:, 2:3]).then_inc(S["att_e"], 1)

                exps(0)
                for w in range(len(units) + 4):
                    exps(w + 1)
                    if w < len(units):
                        n = units[w]["n"] * P
                        act.wait_ge(S["att_t"], before(tag, "t") + w + 1)
                        if w >= 2:
                            act.wait_ge(S["att_pv"], before(tag, "pv") + w - 1)
                        act.activation(pT_[w % 2][:, 0:n], bank[TB[w % 2]][:, 0:n], ACT.Copy).then_inc(S["att_pT"], 1)
                    tail(w)

            def split_out(tag, src, first, last_step):
                def tail(w):
                    if w >= last_step and (w - last_step) % per == 0 and (w - last_step) // per < 4:
                        p = (w - last_step) // per
                        act.wait_ge(S["att_out"], before(tag, "out") + p + 1)
                        act.activation(hh[:, first + p, :], src[p % 2][:, :], ACT.Copy).then_inc(S["att_hi"], 1)
                per = 8
                return tail

            attention("a1", units_a1(), split_out("a1", mixf, 4, 9))

            for j in range(4):
                hi(N_S1 + j + 1)
                for kt in (2 * j, 2 * j + 1):
                    evac(act, T_S1 + kt)
                    squares("n1", kt, xT[:, kt, :], nsq)

            def norm_h(tag, shift):
                act.wait_ge(S["rms_sum"], before(tag, "sum") + KT)
                rsqrt(bank[2][:, :], nry[0][:, :], nry[1][:, :], "rms_rs")
                for kt in range(KT):
                    act.wait_ge(S["rms_hf"], before(tag, "hf") + kt + 1)
                    act.activation(nhf[kt % 2][:, :], nhf[kt % 2][:, :], ACT.Identity,
                                   bias=modc[:, shift + kt:shift + kt + 1]).then_inc(S["rms_aff"], 1)
                    act.wait_ge(S["rms_aff"], before(tag, "aff") + kt + 1)
                    act.activation(hh[:, kt, :], nhf[kt % 2][:, :], ACT.Copy).then_inc(S["rms_hi"], 1)

            norm_h("n1", 0)
            for j in range(9):
                hi(N_S2 + j + 1)
                for T in (T_S2 + 2 * j, T_S2 + 2 * j + 1):
                    t = T - T_S2
                    if j < 2:
                        act.wait_ge(S["tile_ready"], T + 1)
                        for k in range(2):
                            r = slice(64 * k, 64 * k + 64)
                            ins = act.activation(q_a2[r, t, :], ring(T)[r, :], ACT.Copy,
                                                 scale=HD ** -0.5 / SWA_SLOPES[2 * t + k])
                        ins.then_inc(S[f"evac{T % 4}"], 1)
                    elif j in (3, 4):
                        act.wait_ge(S["tile_ready"], T + 1)
                        act.activation(q_a3[:, t - 6, :], ring(T)[:, :], ACT.Copy,
                                       scale=HD ** -0.5 / DIFF_SLOPES[t - 6]).then_inc(S[f"evac{T % 4}"], 1)
            hi(GATE_N + 1)

            def gate_tiles(steps, w):
                if 0 <= w < (32 if steps is swa_steps else 16):
                    for t in tiles_done(steps, w):
                        if t % 2 == 0:
                            act.wait_ge(S["tile_ready"], GATE_T + t + 1)
                            act.activation(sg[:, t, :], gate_bank(GATE_T + t)[:, :], ACT.Copy)\
                                .then_inc(S[f"evac{(GATE_T + t) % 4}"], 1)
                        else:
                            hi(GATE_N + t // 2 + 2)

            def swa_tail(w):
                gate_tiles(swa_steps, w)

            act.preload_act_table_set("natural_log_exp_and_others")
            attention("a2", units_a2(), swa_tail)

            def diff_tail(w):
                gate_tiles(diff_steps, w)
                if w >= 5 and (w - 5) % 4 == 0 and (w - 5) // 4 < DN_H:
                    h = (w - 5) // 4
                    act.wait_ge(S["att_out"], before("a3", "out") + h + 1)
                    if h >= 1:
                        act.wait_ge(S["d_sum"], h)
                    act.activation(osq[:, :], of[h % 2][:, :], ACT.Square).then_inc(S["d_sq"], 1)
                if w >= 6 and (w - 6) % 4 == 0 and (w - 6) // 4 < DN_H:
                    h = (w - 6) // 4
                    act.wait_ge(S["d_sum"], h + 1)
                    if h >= 1:
                        act.wait_ge(S["d_mix"], h)
                    rsqrt(bank[OB[h % 2]][:, :], ory[0][:, :], ory[1][:, :], "d_rs")

            attention("a3", units_a3(), diff_tail)
            evac(act, T_S3 - 1)
            evac(act, T_S3 - 2)
            act.wait_ge(S["d_mix"], 4)
            for k in range(KT):
                act.activation(hh[:, k, :], branch_out(k), ACT.Copy).then_inc(S["att_hi"], 1)

            for j in range(4):
                if j >= 1:
                    hi(N_S3 + j + 1)
                for q in (2 * j, 2 * j + 1):
                    pair = sg[:, :, :].rearrange("p (g q) t -> p g q t", g=2)[:, :, q, :]
                    act.activation(pair, pair, ACT.Sigmoid).then_inc(S["sig_ready"], 1)
                for q in (2 * j, 2 * j + 1):
                    act.wait_ge(S["merged_ready"], q + 1)
                    act.activation(mh[:, q, :], mS[q % 2][:, :], ACT.Copy).then_inc(S["mg_hi"], 1)
            for j in range(4):
                hi(N_S4 + j + 1)
                for kt in (2 * j, 2 * j + 1):
                    evac(act, T_S4 + kt)
                    squares("n2", kt, xT[:, kt, :], nsq)
            norm_h("n2", 24)
            with act.Fori(0, 11) as i:
                for s in range(2):
                    hi(N_S5 + s + 1, i)
                    T = T_S5 + 2 * s
                    evac(act, T, i)
                    act.activation(fg[s][:, :], fc[s][:, :], ACT.Gelu).then_inc(S["f_gelu"], 1)
                    evac(act, T + 1, i)
                    act.activation(fh[:, bass.ds(s + 2 * i, 1), :].rearrange("p k c -> p (k c)"), ff[s][:, :], ACT.Copy)\
                        .then_inc(S["f_hi"], 1)
            hi(N_S6 + 1)
            with act.Fori(0, 4) as i:
                for s in range(2):
                    hi(N_S6 + 2 + s, i)
            hi(N_S6 + 10)
            for kt in range(KT):
                act.wait_ge(S["x3_ready"], kt + 1)
                squares("n3", kt, xT[:, kt, :], nsq)
            act.wait_ge(S["rms_sum"], before("n3", "sum") + KT)
            rsqrt(bank[0][:, :], nry[0][:, :], nry[1][:, :], "rms_rs")
            for t in range(TT):
                act.wait_ge(S["y_tr"], 2 * t + 1)
                act.activation(y_tok[:, t, 0:512], bank[(2 * t + 1) % 8][:, :], ACT.Copy).then_inc(S["y_out0"], 1)

        @block.vector
        def _(dve):
            link = Chain(dve, "dve_chain")

            def rest(dst, src, high, done):
                return dve.tensor_tensor(dst, src, high.bitcast(F32), ALU.subtract).then_inc(S[done], 1)

            def newton(ps, y, yy, done=None):
                ins = dve.scalar_tensor_tensor(yy, ps, eps, yy, op0=ALU.add, op1=ALU.mult)
                if done:
                    ins.then_inc(S[done[0]], 1)
                    dve.wait_ge(S[done[0]], done[1])
                else:
                    link(ins)
                link(dve.scalar_tensor_tensor(yy, yy, -3.0, y, op0=ALU.add, op1=ALU.mult))

            dve.memset(eps, EPS).then_inc(S["scal_done"], 1)
            for kt in range(KT):
                dve.wait_ge(S["xt_done"], kt + 1)
                dve.tensor_copy(xT[:, kt, :], bank[kt][:, :]).then_inc(S["xT_ready"], 1)
            dve.wait_ge(S["vecs_done"], 1)
            dve.tensor_copy(colA[:, :], bank[1][:, 0:NA]).then_inc(S["cols_ready"], 1)
            dve.wait_ge(S["vecs_done"], 2)
            dve.tensor_copy(colB[:, :], bank[2][:, 0:NB]).then_inc(S["cols_ready"], 1)
            dve.wait_ge(S["cols_ready"], 2)
            dve.tensor_scalar(nw1, colA[:, 0:8], -0.5, None, ALU.mult)
            dve.tensor_scalar(gfc, colA[:, 24:32], -0.5, None, ALU.mult)
            dve.tensor_scalar(dncol, col("dn_norm_w"), -0.5, None, ALU.mult)
            dve.tensor_scalar(subcol, col("subln"), -0.5 * (1.0 - LAM_INIT), None, ALU.mult)
            dve.tensor_scalar(qcol, col("q_norm"), -0.5 * HD ** -0.5, None, ALU.mult)
            link(dve.tensor_scalar(kcol, col("k_norm"), -0.5, None, ALU.mult))
            dve.wait_ge(S["rms_rs"], before("n0", "rs") + 1)
            newton(bank[0][:, :], ry[0][:, :], ryy[0][:, :])

            def norm_h(tag, g, z, buf):
                for kt in range(KT + 1):
                    if 2 <= kt < KT:
                        dve.wait_ge(S["rms_lo"], before(tag, "lo") + kt - 1)
                    if kt < KT:
                        dve.scalar_tensor_tensor(buf[kt % 2][:, :], xT[:, kt, :], g[:, kt:kt + 1], z,
                                                 op0=ALU.mult, op1=ALU.mult).then_inc(S["rms_hf"], 1)
                    if kt >= 1:
                        dve.wait_ge(S["rms_hi"], before(tag, "hi") + kt)
                        rest(hl[:, kt - 1, :], buf[(kt - 1) % 2][:, :], hh[:, kt - 1, :], "rms_lo")

            norm_h("n0", nw1, ryy[0][:, :], h_f1)
            dve.wait_ge(S["rel_done"], 1)
            dve.tensor_tensor(brow[:, 0:SEQ], bank[3][0:ATT_H, :], logm[:, 0:SEQ], ALU.add).then_inc(S["brow_ready"], 1)
            dve.tensor_tensor(brow[:, SEQ:], bank[4][0:ATT_H, 0:P], logm[:, SEQ:], ALU.add).then_inc(S["brow_ready"], 1)
            dve.wait_ge(S["in_small"], 16 * 5)
            for h in range(ATT_H):
                dve.tensor_scalar(sinks[:, h:h + 1], sinks[:, h:h + 1], 1.0 / SWA_SLOPES[h], None, ALU.mult)
            for k in range(2):
                ins = dve.tensor_tensor_reduce(out=lamrow[:, 128 * k:128 * k + 64], in0=lamrow[:, 128 * k:128 * k + 64],
                                               in1=lamrow[:, 128 * k + 64:128 * k + 128], scale=1.0, scalar=0.0,
                                               op0=ALU.mult, op1=ALU.add, accum_out=lams[:, k:k + 1])
            ins.then_inc(S["scal_done"], 1)
            dve.wait_ge(S["lam_exp"], 1)
            link(dve.tensor_tensor(lams[:, 4:5], lams[:, 2:3], lams[:, 3:4], ALU.subtract))
            link(dve.tensor_scalar(lams[:, 5:6], lams[:, 4:5], -1.0, -LAM_INIT, ALU.mult, ALU.add))
            dve.wait_ge(S["csil_ready"], 1)
            piece = [0]

            def ada():
                p = piece[0]
                piece[0] += 1
                c, kt = divmod(p, KT)
                dve.wait_ge(S[f"ada_in{p % 2}"], 16 * (p // 2 + 1))
                acc = ada_acc[c % 2][:, :]
                if kt == 0:
                    if c >= 2:
                        dve.wait_ge(S["ada_fold"], c - 1)
                    ins = dve.tensor_scalar(acc, ada_w[p % 2][:, :], csil[:, 0:1], None, ALU.mult)
                else:
                    dve.wait_ge(S["ada_piece"], p)
                    ins = dve.scalar_tensor_tensor(acc, ada_w[p % 2][:, :], csil[:, kt:kt + 1], acc, op0=ALU.mult, op1=ALU.add)
                ins.then_inc(S["ada_piece"], 1)

            for n in range(17):
                for T in tiles_of(n):
                    if ADA_STEP.get(n, 0):
                        ada()
                    ps = ring(T)
                    if n < 6:
                        y = cv[T % 2]
                        dve.wait_ge(S["tile_ready"], T + 1)
                        if T >= 2:
                            dve.wait_ge(S["silu_done"], T - 1)
                        link(dve.tensor_scalar(y[:, :], ps[:, :], col("conv_w", 36 + T), None, ALU.mult))
                        for k in range(1, 4):
                            ins = dve.scalar_tensor_tensor(y[:, k:], ps[:, 0:SEQ - k], col("conv_w", 12 * (3 - k) + T), y[:, k:],
                                                           op0=ALU.mult, op1=ALU.add)
                            if k < 3:
                                link(ins)
                        ins.then_inc(S[f"evac{T % 4}"], 1)
                    elif n == 6:
                        dve.wait_ge(S["tile_ready"], T + 1)
                        dve.tensor_copy(baT[:, :], ps[0:8, :]).then_inc(S[f"evac{T % 4}"], 1)
                    elif 9 <= n < 15:
                        dve.wait_ge(S["tile_ready"], T + 1)
                        dst = qk_att[:, T - 17, :] if n < 13 else v_att[:, T - 25, :]
                        dve.tensor_copy(dst, ps[:, :]).then_inc(S[f"evac{T % 4}"], 1)
                for _ in range(ADA_STEP.get(n, 0) - len(tiles_of(n))):
                    ada()
                if n >= 1:
                    for k in norm_of(n - 1):
                        dve.wait_ge(S["rs_done"], k + 1)
                        newton(bank[2 + k % 2][:, :], ry[k % 2][:, :], ryy[k % 2][:, :], ("nt_done", k + 1))
                        if k < 8:
                            t, g = qkv[:, k, :], -0.5 * P ** -0.5 if k < 4 else -0.5
                        else:
                            t, g = qk_att[:, k - 8, :], qcol if k < 12 else kcol
                        dve.scalar_tensor_tensor(t, t, g, ryy[k % 2][:, :], op0=ALU.mult, op1=ALU.mult)\
                            .then_inc(S["norm_done"], 1)
                if n == 8:
                    dve.wait_ge(S["ba_tr"], 1)
                    link(dve.tensor_copy(ba_tok, bank[4][:, 0:32].rearrange("p (c e) -> p c e", c=TT)))
                    x4 = lambda ap: ap.rearrange("p (c h) -> p c h", c=TT)
                    link(dve.tensor_tensor(x4(sa), ba_tok[:, :, 4:8],
                                           dtb.rearrange("p (o h) -> p o h", o=1).to_broadcast([P, TT, DN_H]), ALU.add))
                    dve.tensor_scalar(sr, sa, 0.0, None, ALU.max)
                    link(dve.tensor_scalar(sb_, sa, -1.0, None, ALU.mult))
                    dve.tensor_tensor(sb_, sb_, sa, ALU.max).then_inc(S["ba_pre"], 1)
                if n == 10:
                    dve.wait_ge(S["ba_act"], 1)
                    link(dve.tensor_tensor(sr, sr, sl, ALU.add))
                    dve.scalar_tensor_tensor(x4(gdec), x4(sr), -1.0,
                                             ea.rearrange("p (o h) -> p o h", o=1).to_broadcast([P, TT, DN_H]),
                                             op0=ALU.mult, op1=ALU.mult).then_inc(S["g_ready"], 1)
            dve.wait_ge(S["ada_fold"], 6)
            dve.wait_ge(S["in_rowsM"], 16)
            dve.tensor_tensor(modrow[:, :], bank[5][0:48, 0:P], rowsM[:, :], ALU.add).then_inc(S["modrow_ready"], 1)
            dve.wait_ge(S["mod_tr"], 1)
            link(dve.tensor_copy(modc[:, :], bank[4][:, 0:48]))
            for g, row, scale in ((g1c, ROWS_A["norm1_g"], 8), (g2c, ROWS_A["norm2_g"], 32)):
                link(dve.scalar_tensor_tensor(g, modc[:, scale:scale + 8], 1.0, colA[:, row:row + 8], op0=ALU.add, op1=ALU.mult))
                ins = dve.tensor_scalar(g, g, -0.5, None, ALU.mult)
            ins.then_inc(S["mod_ready"], 1)
            dve.wait_ge(S["v_tr"], 1)
            for t in range(TT):
                dve.tensor_copy(v_att[:, t, :], bank[(2, 3, 6, 7)[t]][:, :]).then_inc(S["v_ready"], 1)

            dve.wait_ge(S["toep_out"], 16)
            dve.wait_ge(S["tile_ready"], 33)
            dve.wait_ge(S["dn_gct"], 1)
            dve.tensor_copy(gc, bank[5][:, 0:16]).then_inc(S["dn_egc"], 1)

            dve.wait_ge(S["dn_egc"], 1)
            for c in range(TT):
                four_c = slice(4 * c, 4 * c + 4)
                tok = slice(c * P, (c + 1) * P)
                dve.wait_ge(S["dn_grow"], c + 1)
                last = four(bank[c % 2][:, :])[:, :, P - 1:P].rearrange("p h o -> p (h o)")
                dve.tensor_tensor(tail[:, four_c], last, gc[:, four_c], ALU.subtract).then_inc(S["dn_dsub"], 1)
                dve.wait_ge(S["dn_exp"], c + 1)
                if c == 0:
                    dve.tensor_tensor(bege, beta, egc, ALU.mult).then_inc(S["bege_ready"], 1)
                link(dve.tensor_tensor(Dk[c % 2][:, :, :], Dk[c % 2][:, :, :], each(m(C_TRIU)), ALU.mult))
                dve.wait_ge(S["dn_brow"], c + 1)
                dve.tensor_tensor(attnT[:, c], four(bank[2 + c % 2][:, :]), Dk[c % 2][:, :, :], ALU.mult).then_inc(S["dn_dtb"], 1)
                dve.wait_ge(S["dn_dtb"], c + 1)
                link(dve.tensor_tensor(attnT[:, c], attnT[:, c], each(m(C_STRIU)), ALU.mult))
                dve.wait_ge(S["dn_prod"], c + 1)
                dve.tensor_tensor(AT[:, c], four(bank[5][:, :]), attnT[:, c], ALU.mult).then_inc(S["dn_at"], 1)
                dve.wait_ge(S["dn_at"], 2 * c + 1)
                dve.tensor_tensor(attnT[:, c], four(bank[6][:, :]), Dk[c % 2][:, :, :], ALU.mult).then_inc(S["dn_at"], 1)
                dve.tensor_copy(glst[:, four_c], state[:, :, P - 1:P].rearrange("p h o -> p (h o)"))
                dve.tensor_tensor(qkv[:, 0:4, tok], qkv[:, 0:4, tok], state[:, :, :], ALU.mult).then_inc(S["dn_qd"], 1)
                dve.wait_ge(S["dn_a"], c + 1)
                link(dve.tensor_tensor(X[:, c], four(bank[7][:, :]), each(m(C_NM0)), ALU.mult))
                dve.tensor_tensor(X[:, c], X[:, c], each(ident), ALU.add).then_inc(S["dn_x"], 1)

            def masked(l, c):
                dve.wait_ge(S["dn_p1"], 4 * l + c + 1)
                dve.tensor_tensor(P1[:, c], four(bank[c % 2][:, :]), each(m(C_LVL + l)), ALU.mult).then_inc(S["dn_p1s"], 1)

            def update(l, c):
                dve.wait_ge(S["dn_z"], 4 * l + c + 1)
                if l < N_LVL - 1:
                    dve.tensor_tensor(X[:, c], X[:, c], four(bank[2 + c % 2][:, :]), ALU.subtract)
                dve.tensor_tensor(XT[:, c], XT[:, c], four(bank[4 + c % 2][:, :]), ALU.subtract).then_inc(S["dn_upd"], 1)

            for l in range(N_LVL):
                masked(l, 0)
                for c in range(TT):
                    if c + 1 < TT:
                        masked(l, c + 1)
                    update(l, c)
            for c in range(TT):
                dve.wait_ge(S["dn_uw"], c + 1)
                dve.tensor_copy(vb[:, c], four(bank[6][:, :])).then_inc(S["dn_u"], 1)
            dve.wait_ge(S["dn_u"], 4)
            for c in range(TT):
                if c == 0:
                    dve.tensor_copy(P1[:, 0], vb[:, 0]).then_inc(S["dn_vn"], 1)
                else:
                    dve.wait_ge(S["dn_ws"], c)
                    dve.tensor_tensor(P1[:, c % 2], vb[:, c], four(bank[0][:, :]), ALU.subtract).then_inc(S["dn_vn"], 1)
                if c < TT - 1:
                    dve.wait_ge(S["dn_su"], c + 1)
                    if c == 0:
                        dve.tensor_copy(state[:, :, :], four(bank[1][:, :])).then_inc(S["dn_s"], 1)
                    else:
                        dve.wait_ge(S["dn_o"], c + 1)
                        link(dve.tensor_tensor(state[:, :, :], state[:, :, :], over(glst[:, 4 * c:4 * c + 4]), ALU.mult))
                        dve.tensor_tensor(state[:, :, :], state[:, :, :], four(bank[1][:, :]), ALU.add).then_inc(S["dn_s"], 1)
                    dve.wait_ge(S["dn_s"], c + 1)
            for c in range(TT):
                tok = slice(c * P, (c + 1) * P)
                dve.wait_ge(S["dn_ors"], c + 1)
                newton(four(bank[2 + c % 2][:, :]), P1[:, 2], P1[:, 3])
                if c >= 2:
                    dve.wait_ge(S["dn_hi"], c - 1)
                mx4 = four(mixf[c % 2][:, :])
                link(dve.scalar_tensor_tensor(mx4, four(bank[4 + c][:, :]), dncol, P1[:, 3], op0=ALU.mult, op1=ALU.mult))
                dve.tensor_tensor(mx4, mx4, zs[:, 0:4, tok], ALU.mult).then_inc(S["dn_mix"], 1)
                dve.wait_ge(S["dn_hi"], c + 1)
                rest(hl[:, 0:4, tok], mx4, hh[:, 0:4, tok], "dn_lo")

            def attention(tag, units, bias_wait, tail):
                units = list(units)
                s_, p_, pT_ = bufs[tag]
                M = len(units[0]["maps"])
                maps = [mp for u in units for mp in u["maps"]]

                def scores(w):
                    if w >= len(units):
                        return
                    if w >= 2:
                        dve.wait_ge(S["att_p"], before(tag, "p") + w - 1)
                    for g in range(M * w, M * w + M):
                        mp = maps[g]
                        n = mp["k"].shape[-1]
                        stat = st[g % 4]
                        if g % (TT * M) == 0:
                            bias_wait(units[w]["head"])
                        dve.wait_ge(S["att_qk"], before(tag, "qk") + g + 1)
                        link(dve.tensor_tensor_reduce(out=s_[g % (2 * M)][:, 0:n], in0=bank[QK[g % 2]][:, 0:n], in1=mp["bias"],
                                                      scale=1.0, scalar=-3e38, op0=ALU.add, op1=ALU.max, accum_out=stat[:, 0:1]))
                        if mp["sink"] is None:
                            ins = dve.tensor_scalar(stat[:, 1:2], stat[:, 0:1], -mp["slope"], None, ALU.mult)
                        else:
                            ins = dve.tensor_scalar(stat[:, 1:2], stat[:, 0:1], mp["sink"], -mp["slope"], ALU.max, ALU.mult)
                        ins.then_inc(S["att_s"], 1)

                def probs(w):
                    n = units[w]["n"] * P
                    p = p_[w % 2][:, 0:n]
                    for k in range(M):
                        g = M * w + k
                        stat = st[g % 4]
                        s = s_[g % (2 * M)][:, 0:n]
                        dve.wait_ge(S["att_e"], before(tag, "e") + g + 1)
                        if maps[g]["sink"] is not None:
                            link(dve.tensor_tensor(stat[:, 2:3], stat[:, 2:3], stat[:, 4:5], ALU.add))
                        link(dve.reciprocal(stat[:, 3:4], stat[:, 2:3]))
                        if k == 0:
                            if w >= 2:
                                dve.wait_ge(S["att_t"], before(tag, "t") + w - 1)
                            ins = dve.tensor_scalar(p, s, stat[:, 3:4], None, ALU.mult)
                            if M == 2:
                                link(ins)
                        else:
                            link(dve.tensor_tensor(stat[:, 5:6], stat[:, 3:4], lams[:, 5:6], ALU.mult))
                            ins = dve.scalar_tensor_tensor(p, s, stat[:, 5:6], p, op0=ALU.mult, op1=ALU.add)
                    ins.then_inc(S["att_p"], 1)

                scores(0)
                scores(1)
                for w in range(len(units) + 4):
                    if w < len(units):
                        probs(w)
                    scores(w + 2)
                    tail(w)

            def tail1(w):
                if w >= 9 and (w - 9) % 8 == 0:
                    p = (w - 9) // 8
                    dve.wait_ge(S["att_pv"], before("a1", "pv") + 8 * p + 8)
                    if p >= 2:
                        dve.wait_ge(S["att_hi"], before("a1", "hi") + p - 1)
                    dve.tensor_tensor(mixf[p % 2][:, :], bank[OB[p % 2]][:, :], gate[:, p, :], ALU.mult).then_inc(S["att_out"], 1)
                if w >= 10 and (w - 10) % 8 == 0:
                    p = (w - 10) // 8
                    dve.wait_ge(S["att_hi"], before("a1", "hi") + p + 1)
                    rest(hl[:, 4 + p, :], mixf[p % 2][:, :], hh[:, 4 + p, :], "att_lo")

            attention("a1", units_a1(), lambda h: dve.wait_ge(S[f"toe_in{h}"], 16), tail1)

            for j in range(4):
                for kt in (2 * j, 2 * j + 1):
                    T = T_S1 + kt
                    dve.wait_ge(S["tile_ready"], T + 1)
                    dve.tensor_tensor(xT[:, kt, :], xT[:, kt, :], ring(T)[:, :], ALU.add).then_inc(S[f"evac{T % 4}"], 1)
            dve.wait_ge(S["rms_rs"], before("n1", "rs") + 1)
            newton(bank[2][:, :], nry[0][:, :], nry[1][:, :])
            norm_h2 = lambda tag, g: norm_h(tag, g, nry[1][:, :], nhf)
            norm_h2("n1", g1c)
            for j in range(9):
                for T in (T_S2 + 2 * j, T_S2 + 2 * j + 1):
                    t = T - T_S2
                    ps = ring(T)
                    if j in (2, 5, 6, 7, 8):
                        dve.wait_ge(S["tile_ready"], T + 1)
                    if t == 4:
                        for g in range(2):
                            for half in range(2):
                                ins = dve.tensor_copy(k_a2[64 * half:64 * half + 64, g, :], ps[64 * g:64 * g + 64, :])
                        ins.then_inc(S[f"evac{T % 4}"], 1)
                    elif t == 5 or j in (5, 6, 7, 8):
                        dst = vf[:, 0, :] if t == 5 else k_a3[:, t - 10, :] if t < 14 else vf[:, t - 13, :]
                        dve.tensor_copy(dst, ps[:, :]).then_inc(S[f"evac{T % 4}"], 1)
            dve.wait_ge(S["v2_tr"], 1)
            dve.tensor_copy(v_a2[:, :, :], four(bank[6][:, :])).then_inc(S["v2_ready"], 1)
            for t in range(TT):
                dve.tensor_copy(v_a3[:, t, :], bank[2 + t][:, :]).then_inc(S["v2_ready"], 1)

            def tail2(w):
                gate_tiles(swa_steps, w - 1)
                if w >= 9 and (w - 9) % 8 == 0:
                    p = (w - 9) // 8
                    dve.wait_ge(S["att_pv"], before("a2", "pv") + 8 * p + 8)
                    dve.tensor_copy(branch_out(p), bank[OB[p % 2]][:, :]).then_inc(S["att_out"], 1)

            def gate_tiles(steps, w):
                if 0 <= w < (32 if steps is swa_steps else 16):
                    for t in tiles_done(steps, w):
                        if t % 2 == 1:
                            dve.wait_ge(S["tile_ready"], GATE_T + t + 1)
                            dve.tensor_copy(sg[:, t, :], gate_bank(GATE_T + t)[:, :]).then_inc(S[f"evac{(GATE_T + t) % 4}"], 1)

            attention("a2", units_a2(), lambda h: dve.wait_ge(S["in_alibi"], 16), tail2)

            def tail3(w):
                gate_tiles(diff_steps, w - 1)
                if w >= 5 and (w - 5) % 4 == 0 and (w - 5) // 4 < DN_H:
                    h = (w - 5) // 4
                    dve.wait_ge(S["att_pv"], before("a3", "pv") + 4 * h + 4)
                    if h >= 2:
                        dve.wait_ge(S["d_mix"], h - 1)
                    dve.tensor_copy(of[h % 2][:, :], bank[OB[h % 2]][:, :]).then_inc(S["att_out"], 1)
                if w >= 7 and (w - 7) % 4 == 0 and (w - 7) // 4 < DN_H:
                    h = (w - 7) // 4
                    dve.wait_ge(S["d_rs"], h + 1)
                    newton(bank[OB[h % 2]][:, :], ory[0][:, :], ory[1][:, :])
                    dve.scalar_tensor_tensor(branch_out(4 + h), of[h % 2][:, :], subcol, ory[1][:, :], op0=ALU.mult, op1=ALU.mult)\
                        .then_inc(S["d_mix"], 1)

            attention("a3", units_a3(), lambda h: None, tail3)
            for k in range(KT):
                dve.wait_ge(S["att_hi"], before("a2", "hi") + k + 1)
                rest(hl[:, k, :], branch_out(k), hh[:, k, :], "att_lo")

            for j in range(4):
                for q in (2 * j, 2 * j + 1):
                    dve.wait_ge(S["sig_ready"], q + 1)
                    for g, buf in ((0, mA), (1, mD)):
                        T = T_S3 + 2 * q + g
                        dve.wait_ge(S["tile_ready"], T + 1)
                        dve.tensor_tensor(buf[q % 2][:, :], ring(T)[:, :], sg[:, 8 * g + q, :], ALU.mult)\
                            .then_inc(S[f"evac{T % 4}"], 1)
                    evac(dve, T_S3 + 2 * q)
                    evac(dve, T_S3 + 2 * q + 1)
                    dve.tensor_tensor(mS[q % 2][:, :], mA[q % 2][:, :], mD[q % 2][:, :], ALU.add).then_inc(S["merged_ready"], 1)
                    dve.wait_ge(S["mg_hi"], q + 1)
                    rest(ml[:, q, :], mS[q % 2][:, :], mh[:, q, :], "mg_lo")
            for j in range(4):
                for kt in (2 * j, 2 * j + 1):
                    T = T_S4 + kt
                    dve.wait_ge(S["tile_ready"], T + 1)
                    dve.scalar_tensor_tensor(xT[:, kt, :], ring(T)[:, :], modc[:, 16 + kt:17 + kt], xT[:, kt, :],
                                             op0=ALU.mult, op1=ALU.add).then_inc(S[f"evac{T % 4}"], 1)
            dve.wait_ge(S["rms_rs"], before("n2", "rs") + 1)
            newton(bank[2][:, :], nry[0][:, :], nry[1][:, :])
            norm_h2("n2", g2c)
            with dve.Fori(0, 11) as i:
                for s in range(2):
                    T = T_S5 + 2 * s
                    pa, pg = ring(T), ring(T + 1)
                    cw = lambda tap: colB[:, bass.ds(tap * FT + s + 2 * i, 1)]
                    dve.wait_ge(S["tile_ready"], T + 1 + 4 * i)
                    dve.tensor_scalar(fc[s][:, :], pa[:, :], cw(2), colA[:, bass.ds(ROWS_A["conv_b"] + s + 2 * i, 1)],
                                      ALU.mult, ALU.add).then_inc(S["f_chain"], 1)
                    dve.wait_ge(S["f_chain"], 2 * s + 1 + 4 * i)
                    dve.scalar_tensor_tensor(fc[s][:, 1:], pa[:, 0:SEQ - 1], cw(1), fc[s][:, 1:], op0=ALU.mult, op1=ALU.add)\
                        .then_inc(S["f_chain"], 1)
                    dve.wait_ge(S["f_chain"], 2 * s + 2 + 4 * i)
                    dve.scalar_tensor_tensor(fc[s][:, 2:], pa[:, 0:SEQ - 2], cw(0), fc[s][:, 2:], op0=ALU.mult, op1=ALU.add)\
                        .then_inc(S[f"evac{T % 4}"], 1)
                    dve.wait_ge(S["tile_ready"], T + 2 + 4 * i)
                    dve.wait_ge(S["f_gelu"], s + 1 + 2 * i)
                    dve.tensor_tensor(ff[s][:, :], pg[:, :], fg[s][:, :], ALU.mult).then_inc(S[f"evac{(T + 1) % 4}"], 1)
                    dve.wait_ge(S["f_hi"], s + 1 + 2 * i)
                    j = bass.ds(s + 2 * i, 1)
                    rest(fl[:, j, :].rearrange("p k c -> p (k c)"), ff[s][:, :], fh[:, j, :].rearrange("p k c -> p (k c)"), "f_lo")
            for kt in range(KT):
                dve.wait_ge(S["tile_ready"], T_S5 + 44 + kt + 1)
                dve.scalar_tensor_tensor(xT[:, kt, :], bank[kt][:, :], modc[:, 40 + kt:41 + kt], xT[:, kt, :],
                                         op0=ALU.mult, op1=ALU.add).then_inc(S["x3_ready"], 1)
            dve.wait_ge(S["rms_rs"], before("n3", "rs") + 1)
            newton(bank[0][:, :], nry[0][:, :], nry[1][:, :])
            for kt in range(KT):
                dve.scalar_tensor_tensor(yT[:, kt, :], xT[:, kt, :], gfc[:, kt:kt + 1], nry[1][:, :], op0=ALU.mult, op1=ALU.mult)\
                    .then_inc(S["y_ready"], 1)
            for t in range(TT):
                dve.wait_ge(S["y_tr"], 2 * t + 2)
                dve.tensor_copy(y_tok[:, t, 512:1024], bank[(2 * t + 2) % 8][:, :]).then_inc(S["y_out1"], 1)


INPUTS = ["x", "norm_w", "w_in", "conv_w", "a_log", "dt_bias", "dn_norm_w", "q_norm_w", "k_norm_w", "rel_bias",
          "w_out", "c_2", "w_ada_2", "b_ada_2", "norm1_g_2", "w_in_2", "swa_sinks_2", "diff_lambda_2",
          "diff_subln_g_2", "w_branch_swa_2", "w_branch_diff_2", "w_out_2", "norm2_g_2", "w_up_2", "conv_w_2",
          "conv_b_2", "w_down_2", "final_g_2"]


def kernel(**inputs):
    import concourse.bacc as bacc
    from concourse.bass_utils import run_bass_kernel_spmd

    nc = bacc.Bacc("TRN2", target_bir_lowering=False, num_devices=1, dynamic_dma_scratch_size=2048)
    arrays = {n: np.ascontiguousarray(inputs[n]) for n in INPUTS}
    arrays.update(constants())
    aps = {n: nc.dram_tensor(n, v.shape, mybir.dt.from_np(v.dtype), kind="ExternalInput").ap() for n, v in arrays.items()}
    out = nc.dram_tensor("out", (1, SEQ, D), F32, kind="ExternalOutput").ap()
    toep = nc.dram_tensor("bias_rows", (ATT_H, P, SEQ + P), F32, kind="Internal").ap()
    build(nc, aps, out, toep)
    r = run_bass_kernel_spmd(nc, [arrays], core_ids=[0])
    return r.results[0]["out"]
```

```python
import math
from contextlib import ExitStack

import numpy as np
import concourse.bass as bass
from concourse import mybir

F32 = mybir.dt.float32
F32R = mybir.dt.float32r
ACT = mybir.ActivationFunctionType
ALU = mybir.AluOpType

P = 128
SEQ = 512
D = 1024
KT = D // P
TT = SEQ // P
D_DN, DN_H = 512, 4
ATT_H, HD = 8, 64
D_IN = 4 * D_DN + 2 * DN_H + 4 * 512
IN2 = 4352
DFF = 2816
FT = DFF // P
N_BUCKETS, MAX_DISTANCE = 32, 2048
BLK = 2048
EPS = 1e-6
MASK = -1e30
SWA_SLOPES = [2.0 ** -(h + 1) for h in range(8)]
DIFF_SLOPES = [2.0 ** (-2 * (h + 1)) for h in range(4)]
LAM_INIT = 0.8 - 0.6 * math.exp(0.0)

ROWS_A = {"norm_w": 0, "norm1_g": 8, "norm2_g": 16, "final_g": 24, "c": 32, "dn_norm_w": 40,
          "subln": 41, "q_norm": 42, "k_norm": 43, "conv_w": 44, "conv_b": 92}
NA = 92 + FT
NB = 3 * FT
C_ID, C_ONE, C_INVD, C_INVH, C_BLK, C_TRIU, C_STRIL, C_NM0, C_NMT0, C_LVL = range(10)
N_LVL = 6
NC128 = C_LVL + N_LVL


def t5_bucket(dist):
    max_exact = N_BUCKETS // 2
    d = np.maximum(dist, 1).astype(np.float64)
    large = max_exact + (np.log(d / max_exact) / math.log(MAX_DISTANCE / max_exact)
                         * (N_BUCKETS - max_exact)).astype(np.int32)
    large = np.minimum(large, N_BUCKETS - 1)
    return np.where(dist < max_exact, dist, large).astype(np.int32)


def constants():
    i = np.arange(P)[:, None]
    j = np.arange(P)[None, :]
    c = np.zeros((P, NC128, P), np.float32)
    c[:, C_ID] = i == j
    c[:, C_ONE] = 1.0
    c[:, C_INVD] = 1.0 / D
    c[:, C_INVH] = 1.0 / P
    c[:, C_BLK] = (i // HD == j // HD) / HD
    c[:, C_TRIU] = i <= j
    c[:, C_STRIL] = i > j
    merge = lambda b: (i // (2 * b) == j // (2 * b)) & (i // b == j // b + 1)
    c[:, C_NM0] = -1.0 * merge(1)
    c[:, C_NMT0] = -1.0 * merge(1).T
    for n in range(N_LVL):
        c[:, C_LVL + n] = merge(2 << n)
    d = i - (np.arange(SEQ)[None, :] - 3 * P)
    alibi = np.where(d >= 0, -d, MASK).astype(np.float32)
    d2 = d[:, 2 * P:]
    window = np.where((d2 >= 0) & (d2 < P), -d2, MASK).astype(np.float32)
    dist = SEQ - 1 - np.arange(SEQ + P)
    onehot = np.zeros((N_BUCKETS, SEQ + P), np.float32)
    ok = dist >= 0
    onehot[t5_bucket(dist[ok]), np.arange(SEQ + P)[ok]] = 1.0
    times = (dist <= 128) * 1 + (dist % 4 == 0) * 1 + (dist % 16 == 0) * 1
    logm = np.where(ok & (times > 0), np.log(np.maximum(times, 1)), MASK).astype(np.float32)
    select = np.zeros((P, 95), np.float32)
    select[:, 47] = 1.0
    return {"k_mats": c.reshape(P, NC128 * P), "k_alibi": np.concatenate([alibi, window], 1),
            "k_onehot": onehot, "k_logm": logm[None], "k_select": select}


def build(nc, a, out, toep):
    with ExitStack() as ctx:
        top = [0]

        def at(name, shape, dt=F32, offset=None):
            size = 4 * int(np.prod(shape[1:]))
            if offset is None:
                offset = top[0]
                top[0] += (size + 31) // 32 * 32
            return nc.alloc_sbuf_tensor_at(name, shape, dt, offset=offset), offset + (size + 31) // 32 * 32

        def sb(name, shape, dt=F32):
            return at(name, shape, dt)[0]

        top[0] = (nc.sbuf_base + 31) // 32 * 32
        raw = [sb(f"raw{s}", [P, BLK]) for s in range(2)]
        whi = [sb(f"whi{s}", [P, BLK], F32R) for s in range(2)]
        wlo = [sb(f"wlo{s}", [P, BLK], F32R) for s in range(2)]
        split_at = top[0]
        hh = sb("h_hi", [P, KT, SEQ], F32R)
        hl = sb("h_lo", [P, KT, SEQ], F32R)
        xT = sb("x_res", [P, KT, SEQ])
        mats = sb("mats", [P, NC128, P])
        colA = sb("colA", [P, NA])
        colB = sb("colB", [P, NB])
        modc = sb("modc", [P, 48])
        sc = sb("small", [P, 512])
        U = top[0]

        def m(n):
            return mats[:, n, :]

        ident = m(C_ID)
        eps = sc[:, 0:1]
        lams = sc[:, 1:8]
        sinks = sc[:, 8:16]
        dtb, alog = sc[:, 16:20], sc[:, 20:24]
        qcol, kcol, nw1, dncol, subcol = sc[:, 24:25], sc[:, 25:26], sc[:, 26:34], sc[:, 34:35], sc[:, 35:36]
        g1c, g2c, gfc = sc[:, 36:44], sc[:, 44:52], sc[:, 52:60]
        csil = sc[:, 60:68]
        beta, gdec, gc, egc, tail, bege, glst = (sc[:, 80 + 16 * k:96 + 16 * k] for k in range(7))
        ba_tok = sc[:, 192:224].rearrange("p (c e) -> p c e", c=TT)
        sa, sb_, sr, sl = (sc[:, 224 + 16 * k:240 + 16 * k] for k in range(4))
        ea = sc[:, 288:292]
        mx = [sc[:, 300 + 8 * k:301 + 8 * k] for k in range(4)]
        st = [sc[:, 340 + 8 * k:348 + 8 * k] for k in range(4)]
        select = sc[:, 380:475]

        def col(name, n=0):
            return colA[:, ROWS_A[name] + n:ROWS_A[name] + n + 1]

        top[0] = U
        qkv = sb("dn_qkv", [P, 12, SEQ])
        zs = sb("dn_z", [P, 4, SEQ])
        gate = sb("att_gate", [P, 4, SEQ])
        qk_att = sb("att_qk", [P, 8, SEQ])
        v_att = sb("att_v", [P, 4, SEQ])
        V = top[0]
        x_tok = at("x_tok", [P, TT, D], offset=U)[0]
        h_f1 = [at(f"h_f1{s}", [P, SEQ], offset=U + 16384 + 2048 * s)[0] for s in range(2)]
        baT = at("baT", [2 * DN_H, SEQ], offset=V)[0]
        top[0] = V + 2048
        cv = [sb(f"conv{s}", [P, SEQ]) for s in range(2)]
        sq = [sb(f"sq{s}", [P, SEQ]) for s in range(2)]
        ry = [sb(f"ry{s}", [P, SEQ]) for s in range(2)]
        ryy = [sb(f"ryy{s}", [P, SEQ]) for s in range(2)]
        ada_w = [sb(f"ada_w{s}", [P, D]) for s in range(2)]
        ada_acc = [sb(f"ada_acc{s}", [P, D]) for s in range(2)]
        toe_at = top[0]
        rowsA = sb("rowsA", [NA, P])
        rowsB = sb("rowsB", [NB, P])
        lamrow = sb("lamrow", [P, 4 * HD])
        relT = sb("relT", [N_BUCKETS, ATT_H])
        onehot = sb("onehot", [N_BUCKETS, SEQ + P])
        logm = sb("logm", [ATT_H, SEQ + P])
        brow = sb("brow", [ATT_H, SEQ + P])
        ends = [top[0]]
        top[0] = toe_at
        toe = [sb(f"toe{h}", [P, SEQ]) for h in range(ATT_H)]
        assert top[0] >= ends[0]
        modrow = sb("modrow", [48, P])
        rowsM = sb("rowsM", [48, P])
        ends.append(top[0])
        top[0] = V
        kbe = sb("dn_kbe", [P, TT, DN_H, P])
        ktail = sb("dn_ktail", [P, TT, DN_H, P])
        vb = sb("dn_vb", [P, TT, DN_H, P])
        attnT = sb("dn_attnT", [P, TT, DN_H, P])
        Dk = [sb(f"dn_D{s}", [P, DN_H, P]) for s in range(2)]
        state = sb("dn_state", [P, DN_H, P])
        ends.append(top[0])
        X = at("dn_X", [P, TT, DN_H, P], offset=split_at)[0]
        XT = at("dn_XT", [P, TT, DN_H, P], offset=split_at + 8192)[0]
        AT = at("dn_AT", [P, TT, DN_H, P], offset=split_at + 24576)[0]
        P1 = at("dn_P1", [P, TT, DN_H, P], offset=split_at + 16384)[0]
        top[0] = V
        mixf = [sb(f"mixf{s}", [P, SEQ]) for s in range(2)]
        s_a1 = [sb(f"s_a1{s}", [P, SEQ]) for s in range(2)]
        p_a1 = [sb(f"p_a1{s}", [P, SEQ]) for s in range(2)]
        pT_a1 = [sb(f"pT_a1{s}", [P, SEQ]) for s in range(2)]
        nsq = [sb(f"nsq{s}", [P, SEQ]) for s in range(2)]
        nry = [sb(f"nry{s}", [P, SEQ]) for s in range(2)]
        nhf = [sb(f"nhf{s}", [P, SEQ]) for s in range(2)]
        top[0] = U
        q_a2 = sb("swa_q", [P, 4, SEQ])
        k_a2 = sb("swa_k", [P, 2, SEQ])
        v_a2 = sb("swa_v", [P, TT, P])
        q_a3 = sb("diff_q", [P, 4, SEQ])
        k_a3 = sb("diff_k", [P, 4, SEQ])
        v_a3 = sb("diff_v", [P, TT, SEQ])
        vf = sb("v_fm", [P, 5, SEQ])
        sg = sb("gates", [P, 16, SEQ])
        s_a3 = [sb(f"s_a3{s}", [P, SEQ]) for s in range(4)]
        p_a3 = [sb(f"p_a3{s}", [P, SEQ]) for s in range(2)]
        pT_a3 = [sb(f"pT_a3{s}", [P, SEQ]) for s in range(2)]
        of = [sb(f"of{s}", [P, SEQ]) for s in range(2)]
        osq = sb("osq", [P, SEQ])
        ory = [sb(f"ory{s}", [P, SEQ]) for s in range(2)]
        ends.append(top[0])
        abase = sb("abase", [P, SEQ + 2 * P])
        ends.append(top[0])
        top[0] = U
        mh = sb("merged_hi", [P, KT, SEQ], F32R)
        ml = sb("merged_lo", [P, KT, SEQ], F32R)
        top[0] = V + 16384
        mA, mD, mS = ([sb(f"m{k}{s}", [P, SEQ]) for s in range(2)] for k in "ADS")
        top[0] = U
        fh = sb("ffn_hi", [P, FT, SEQ], F32R)
        fl = sb("ffn_lo", [P, FT, SEQ], F32R)
        top[0] = V + 16384 + 6 * 2048
        fc = [sb(f"fc{s}", [P, SEQ]) for s in range(2)]
        fg = [sb(f"fg{s}", [P, SEQ]) for s in range(2)]
        ff = [sb(f"ff{s}", [P, SEQ]) for s in range(2)]
        ends.append(top[0])
        top[0] = U
        yT = sb("yT", [P, KT, SEQ])
        y_tok = sb("y_tok", [P, TT, D])
        assert max(ends) <= nc.sbuf_usable_end

        bank = [ctx.enter_context(nc.psum_tensor(f"bank{b}", [P, SEQ], F32)) for b in range(8)]

        def four(ap):
            return ap.rearrange("p (h i) -> p h i", h=4)

        def over(ap, n=P):
            return ap.rearrange("p (h o) -> p h o", o=1).to_broadcast([P, 4, n])

        def each(ap):
            return ap.rearrange("p (o i) -> p o i", o=1).to_broadcast([P, 4, P])

        class Signals(dict):

            def __missing__(self, name):
                self[name] = ctx.enter_context(nc.semaphore(name))
                return self[name]

        S = Signals()

        def before(tag, what):
            n = int(tag[1])
            if tag[0] == "n":
                return n if what == "rs" else KT * n - KT * (n > 0 and what == "aff")
            return (n - 1) * (4 if what in ("out", "hi", "lo") else 32)

        class Chain:

            def __init__(self, eng, name):
                self.eng, self.sem, self.n = eng, S[name], 0

            def __call__(self, ins):
                ins.then_inc(self.sem, 1)
                self.n += 1
                self.eng.wait_ge(self.sem, self.n)

        w_in = a["w_in"][0].rearrange("(k p) c -> p k c", p=P)
        w_out = a["w_out"][0].rearrange("(k p) c -> p k c", p=P)
        w_in2 = a["w_in_2"][0].rearrange("(k p) c -> p k c", p=P)
        w_out2 = a["w_out_2"][0].rearrange("(k p) c -> p k c", p=P)
        w_bs = a["w_branch_swa_2"][0].rearrange("(k p) c -> p k c", p=P)
        w_bd = a["w_branch_diff_2"][0].rearrange("(k p) c -> p k c", p=P)
        w_up = a["w_up_2"][0].rearrange("(k p) c -> p k c", p=P)
        w_dn = a["w_down_2"][0].rearrange("(k p) c -> p k c", p=P)
        N_S1, N_S2, N_S3, N_S4, N_S5, N_S6 = 17, 21, 38, 42, 46, 68
        T_S1, T_S2, T_S3, T_S4, T_S5 = 33, 41, 75, 91, 99
        ADA_STEP = {n: 1 for n in range(1, 7)} | {n: 3 for n in range(7, 12)}
        ADA_S0 = sum(ADA_STEP.values())
        OFFS = [2048] + [256 * n for n in range(6)] + [2056 + 256 * n for n in range(6)] + [1536, 1792] \
            + [2056 + 256 * n for n in (6, 7)]
        S0_BLOCKS = 13

        def norm_of(n):
            if 1 <= n < 5:
                return [2 * n - 2, 2 * n - 1]
            return [8 + 2 * (n - 7), 9 + 2 * (n - 7)] if 7 <= n < 11 else []

        def used(buf, n):
            return buf[:, :] if n else buf[:, :].rearrange("p (k c) -> p k c", k=KT)[:, :, 0:P]

        def tiles_of(n):
            return [0] if n == 0 else [2 * n - 1, 2 * n] if n < 7 else [13 + 2 * (n - 7), 14 + 2 * (n - 7)]

        def fold_at(n):
            before = sum(v for k, v in ADA_STEP.items() if k < n - 1)
            after = sum(v for k, v in ADA_STEP.items() if k < n)
            return range(before // 8, after // 8)

        block = ctx.enter_context(nc.Block())

        @block.sync
        def _(sp):
            def weights(n, dsts, i=0):
                s, use = n % 2, n // 2 + i
                if n >= 2:
                    sp.wait_ge(S["hi_ready"], n - 1 + 2 * i)
                    sp.wait_ge(S["lo_ready"], n - 1 + 2 * i)
                for dst, src in dsts(raw[s]):
                    sp.dma_start(dst, src).then_inc(S[f"raw_full{s}"], 16)

            def cols(w, c, width=256):
                def dsts(r):
                    v = r[:, :].rearrange("p (k c) -> p k c", k=KT)
                    return [(v[:, 4 * h:4 * h + 4, 0:width], w[:, 4 * h:4 * h + 4, bass.ds(c, width)])
                            for h in range(2)]
                return dsts

            sp.dma_start(mats[:, C_ID, :], a["k_mats"][:, 0:P]).then_inc(S["x_in_ident"], 16)
            for t in range(TT):
                sp.dma_start(x_tok[:, t, :], a["x"][0, t * P:(t + 1) * P, :]).then_inc(S[f"x_in{t}"], 16)
            for n in range(17):
                if n == 0:
                    weights(n, cols(w_in, OFFS[n], P))
                else:
                    weights(n, cols(w_in, OFFS[n]))
            for j in range(4):
                weights(N_S1 + j, cols(w_out, 256 * j))
            with sp.Fori(0, 8) as i:
                for s in range(2):
                    weights(N_S2 + s, cols(w_in2, 512 * i + 256 * s), i)
            weights(N_S2 + 16, cols(w_in2, 4096))
            for j in range(4):
                def both(r, j=j):
                    v = r[:, :].rearrange("p (g k c) -> p g k c", g=2, k=4)
                    return [(v[:, 0], w_bs[:, :, 256 * j:256 * j + 256]),
                            (v[:, 1], w_bd[:, :, 256 * j:256 * j + 256])]
                weights(N_S3 + j, both)
            for j in range(4):
                weights(N_S4 + j, cols(w_out2, 256 * j))
            with sp.Fori(0, 11) as i:
                for s in range(2):
                    def pair(r, s=s):
                        v = r[:, :].rearrange("p (k g c) -> p k g c", k=KT, g=2)
                        return [(v[:, :, g, :], w_up[:, :, bass.ds(g * DFF + s * P + 2 * P * i, P)])
                                for g in range(2)]
                    weights(N_S5 + s, pair, i)

            def down(n, i=0):
                def rows(r):
                    v = r[:, :].rearrange("p (k c) -> p k c", k=2)
                    j = n - N_S6
                    return [(v[:, h, :], w_dn[:, bass.ds(2 * j + h + 4 * i, 1), :].rearrange("p k c -> p (k c)"))
                            for h in range(2)]
                weights(n, rows, i)

            with sp.Fori(0, 5) as i:
                for s in range(2):
                    down(N_S6 + s, i)
            down(N_S6 + 10)
            for t in range(TT):
                for h in range(2):
                    sp.wait_ge(S[f"y_out{h}"], t + 1)
                    sp.dma_start(out[0, t * P:(t + 1) * P, h * 512:(h + 1) * 512],
                                 y_tok[:, t, h * 512:(h + 1) * 512]).then_inc(S["out_done"], 16)
            sp.wait_ge(S["out_done"], 16 * 2 * TT)

        def start_xt(pool, c):
            pool.wait_ge(S["dn_at"], 2 * c + 1)
            pool.tensor_tensor(XT[:, c], AT[:, c], each(m(C_NMT0)), ALU.mult).then_inc(S["dn_xt0"], 1)
            pool.wait_ge(S["dn_xt0"], 2 * c + 1)
            pool.tensor_tensor(XT[:, c], XT[:, c], each(ident), ALU.add).then_inc(S["dn_xt0"], 1)

        @block.gpsimd
        def _(pool):
            pool.dma_start(relT[:, :], a["rel_bias"].rearrange("h b -> b h"), allow_slow_non_contiguous=True).then_inc(S["in_rel"], 16)
            pool.dma_start(onehot[:, :], a["k_onehot"]).then_inc(S["in_rel"], 16)
            pool.dma_start(logm[:, :], a["k_logm"].to_broadcast([ATT_H, SEQ + P])).then_inc(S["in_rel"], 16)
            pool.dma_start(rowsM[:, :], a["b_ada_2"].rearrange("o (j p) -> (o j) p", p=P)).then_inc(S["in_rowsM"], 16)

            def lo(n, i=0):
                s = n % 2
                pool.wait_ge(S["hi_ready"], n + 1 + 2 * i)
                pool.tensor_tensor(used(wlo[s], n), used(raw[s], n), used(whi[s], n).bitcast(F32), ALU.subtract)\
                    .then_inc(S["lo_ready"], 1)

            def ada_load(p):
                c, kt = divmod(p, KT)
                pool.dma_start(ada_w[p % 2][:, :], a["w_ada_2"][0, kt * P:(kt + 1) * P, c * D:(c + 1) * D])\
                    .then_inc(S[f"ada_in{p % 2}"], 16)

            pool.wait_ge(S["x_in3"], 16)
            ada_load(0)
            ada_load(1)
            lo(0)
            pieces = [2]

            def ada_next():
                if pieces[0] < 48:
                    pool.wait_ge(S["ada_piece"], pieces[0] - 1)
                    ada_load(pieces[0])
                    pieces[0] += 1

            for n in range(S0_BLOCKS):
                lo(n + 1)
                if n == 3:
                    pool.wait_ge(S["toep_out"], 16)
                    pool.wait_ge(S["cols_ready"], 2)
                    pool.wait_ge(S["scal_done"], 2)
                if 3 <= n < 3 + ATT_H:
                    h = n - 3
                    pool.dma_start(toe[h][:, :],
                                   bass.AP(toep.tensor, h * P * (SEQ + P) + P - 1, [[SEQ + P - 1, P], [1, SEQ]]))\
                        .then_inc(S[f"toe_in{h}"], 16)
                for _ in range(ADA_STEP.get(n - 1, 0)):
                    ada_next()
            lo(S0_BLOCKS + 1)
            for w in range(8):
                ada_next()
            for b in range(3):
                lo(S0_BLOCKS + 2 + b)
                for w in range(8):
                    ada_next()
            pool.wait_ge(S["tile_ready"], T_S1)
            for c in range(TT):
                if c == 0:
                    pool.wait_ge(S["g_ready"], 1)
                    pool.wait_ge(S["in_masks"], 16)
                if c >= 2:
                    pool.wait_ge(S["dn_grow"], c - 1)
                    pool.wait_ge(S["dn_brow"], c - 1)
                pool.tensor_tensor(P1[:, c % 2], over(gdec[:, 4 * c:4 * c + 4]), each(m(C_TRIU)), ALU.mult).then_inc(S["dn_gtri"], 1)
                pool.tensor_tensor(P1[:, 2 + c % 2], over(beta[:, 4 * c:4 * c + 4]), each(ident), ALU.mult).then_inc(S["dn_gtri"], 1)
                if c == 1:
                    lo(N_S1 + 1)
                if c >= 1:
                    start_xt(pool, c - 1)
            start_xt(pool, TT - 1)
            pool.wait_ge(S["gate_silu"], 2)
            for p in range(4):
                pool.tensor_tensor(qk_att[:, p, :], qk_att[:, p, :], gate[:, p, :], ALU.mult).then_inc(S["att_mix"], 1)
            for p in range(4):
                pool.wait_ge(S["att_hi"], p + 1)
                pool.tensor_tensor(hl[:, 4 + p, :], qk_att[:, p, :], hh[:, 4 + p, :].bitcast(F32), ALU.subtract)\
                    .then_inc(S["att_lo"], 1)
            for e in range(TT):
                tok = slice(e * P, (e + 1) * P)
                mx4 = four(mixf[e % 2][:, :])
                pool.wait_ge(S["dn_scaled"], e + 1)
                pool.tensor_tensor(mx4, mx4, zs[:, 0:4, tok], ALU.mult).then_inc(S["dn_mix"], 1)
                pool.wait_ge(S["dn_hi"], e + 1)
                pool.tensor_tensor(hl[:, 0:4, tok], mx4, hh[:, 0:4, tok].bitcast(F32), ALU.subtract).then_inc(S["dn_lo"], 1)
            pool.wait_ge(S["att_out"], 4)
            pool.dma_start(abase[:, :], a["k_alibi"]).then_inc(S["in_alibi"], 16)
            for n in range(N_S1 + 2, N_S2 + 10):
                lo(n)
            with pool.Fori(0, 4) as i:
                for s in range(2):
                    lo(N_S2 + 10 + s, i)
            for n in range(N_S2 + 18, N_S5 + 1):
                lo(n)
            with pool.Fori(0, 16) as i:
                for s in range(2):
                    lo(N_S5 + 1 + s, i)

        def units_a1():
            for h in range(ATT_H):
                for i in range(TT):
                    r = slice(64 * (h % 2), 64 * (h % 2) + 64)
                    yield dict(maps=[dict(q=qk_att[r, h // 2, i * P:(i + 1) * P], k=qk_att[r, 4 + h // 2, 0:(i + 1) * P],
                                          bias=toe[h][:, (3 - i) * P:], sink=None, slope=1.0)],
                               n=i + 1, v=[v_att[:, j, h * HD:(h + 1) * HD] for j in range(i + 1)],
                               out=(r, slice(i * P, (i + 1) * P)), group=h // 2, last=h % 2 == 1 and i == 3,
                               head=h, new=(h % 2, i) == (0, 0))

        def units_a2():
            for h in range(ATT_H):
                for i in range(TT):
                    r = slice(64 * (h % 2), 64 * (h % 2) + 64)
                    j0 = max(i - 1, 0)
                    yield dict(maps=[dict(q=q_a2[r, h // 2, i * P:(i + 1) * P], k=k_a2[r, h // 4, j0 * P:(i + 1) * P],
                                          bias=abase[:, SEQ + (1 - (i - j0)) * P:SEQ + 2 * P], sink=sinks[:, h:h + 1],
                                          slope=SWA_SLOPES[h])],
                               n=i + 1 - j0, v=[v_a2[:, j, (h // 4) * HD:(h // 4 + 1) * HD] for j in range(j0, i + 1)],
                               out=(r, slice(i * P, (i + 1) * P)), group=h // 2, last=h % 2 == 1 and i == 3,
                               head=h, new=(h % 2, i) == (0, 0))

        def units_a3():
            for h in range(DN_H):
                for i in range(TT):
                    yield dict(maps=[dict(q=q_a3[64 * mp:64 * mp + 64, h, i * P:(i + 1) * P],
                                          k=k_a3[64 * mp:64 * mp + 64, h, 0:(i + 1) * P],
                                          bias=abase[:, (3 - i) * P:SEQ], sink=None, slope=DIFF_SLOPES[h]) for mp in range(2)],
                               n=i + 1, v=[v_a3[:, j, h * P:(h + 1) * P] for j in range(i + 1)],
                               out=(slice(0, P), slice(i * P, (i + 1) * P)), group=h, last=i == 3,
                               head=h, new=i == 0)

        QK, TB, OB = (2, 3), (4, 5), {"a1": (6, 6), "a2": (6, 7), "a3": (6, 7)}
        bufs = {"a1": (s_a1, p_a1, pT_a1), "a2": (s_a3, p_a3, pT_a3), "a3": (s_a3, p_a3, pT_a3)}

        def tiles_through(n):
            if n < N_S1:
                return tiles_of(n)[-1] + 1
            for first, T, per in ((N_S5, T_S5, 2), (N_S4, T_S4, 2), (N_S3, T_S3, 4), (N_S2, T_S2, 2), (N_S1, T_S1, 2)):
                if n >= first:
                    return T + per * (n - first + 1)

        def slot_free(eng, n, i=0):
            if n >= N_S6 + 2:
                eng.wait_ge(S["block_done"], n - N_S6 - 1 + 2 * i)
            elif n >= 2:
                eng.wait_ge(S["tile_ready"], tiles_through(n - 2) + 4 * i)

        def ring(T):
            return bank[(0, 1, 5, 6)[T % 4]]

        def gate_bank(T):
            return bank[T % 2]

        GATE_T = T_S2 + 18
        dil_steps = lambda w: min(2 * (w + 1), 4 * 2 * KT)
        swa_steps = lambda w: min(w + 1, 32)
        diff_steps = lambda w: min(32 + 6 * (w + 1), 8 * 2 * KT)
        FILL = {dil_steps: (S0_BLOCKS, 25, 32), swa_steps: (N_S2 + 9, GATE_T, 32), diff_steps: (N_S2 + 9, GATE_T, 16)}

        def steps_before(steps, w):
            return steps(w - 1) if w or steps is diff_steps else 0

        def tiles_done(steps, w):
            _, T, units = FILL[steps]
            if 0 <= w < units:
                for t in range(steps_before(steps, w) // KT, steps(w) // KT):
                    if steps is dil_steps:
                        yield t, T + t, zs[:, t, :] if t < 4 else gate[:, t - 4, :]
                    else:
                        yield t, T + t, sg[:, t, :]

        def branch_out(k):
            return q_a2[:, k, :] if k < 4 else q_a3[:, k - 4, :]

        def evac(eng, T, i=0):
            eng.wait_ge(S[f"evac{T % 4}"], T // 4 + 1 + i)

        @block.tensor
        def _(pe):
            def bank_free(T, i=0):
                if T >= 4:
                    pe.wait_ge(S[f"evac{T % 4}"], T // 4 + i)

            def three(ps, lo, wcol, h_hi, h_lo, start, stop):
                wh, wl = whi[lo][:, wcol:wcol + P], wlo[lo][:, wcol:wcol + P]
                pe.matmul(ps, wh, h_hi, start=start, stop=False)
                pe.matmul(ps, wh, h_lo, start=False, stop=False)
                return pe.matmul(ps, wl, h_hi, start=False, stop=stop)

            def gemm(n, T, us=(0, 1), acts=None, ks=KT, stride=256, first=0, ready=None, i=0):
                ah, al = acts or (hh, hl)
                pe.wait_ge(S["lo_ready"], n + 1 + 2 * i)
                if ready:
                    for k in range(len(us)):
                        bank_free(T + k, i)
                    order = list(range(ks)) if isinstance(ready, tuple) else [4, 5, 6, 7, 0, 1, 2, 3]
                    for kt in order:
                        if isinstance(ready, tuple):
                            pe.wait_ge(ready[0], ready[1] + kt)
                        elif kt in ready:
                            pe.wait_ge(*ready[kt])
                        for k, u in enumerate(us):
                            mm = three(ring(T + k)[:, :], n % 2, kt * stride + u * P + first,
                                       ah[:, kt, :], al[:, kt, :], kt == order[0], kt == order[-1])
                            if kt == order[-1]:
                                mm.then_inc(S["tile_ready"], 1)
                    return
                for k, u in enumerate(us):
                    bank_free(T + k, i)
                    for kt in range(ks):
                        mm = three(ring(T + k)[:, :], n % 2, kt * stride + u * P + first,
                                   ah[:, kt, :], al[:, kt, :], kt == 0, kt == ks - 1)
                    mm.then_inc(S["tile_ready"], 1)

            def norm_sum(tag, b, kt):
                pe.wait_ge(S["rms_sq"], before(tag, "sq") + kt + 1)
                pe.matmul(bank[b][:, :], m(C_INVD), (sq if tag == "n0" else nsq)[kt % 2][:, :],
                          start=kt == 0, stop=kt == KT - 1).then_inc(S["rms_sum"], 1)

            def gate_steps(steps, w):
                for k in range(steps_before(steps, w), steps(w)):
                    t, kt = divmod(k, KT)
                    n, T = FILL[steps][0] + t // 2, FILL[steps][1] + t
                    if kt == 0:
                        pe.wait_ge(S["lo_ready"], n + 1)
                        evac(pe, T - 2)
                    mm = three(gate_bank(T)[:, :], n % 2, kt * 256 + (t % 2) * P, hh[:, kt, :], hl[:, kt, :],
                               kt == 0, kt == KT - 1)
                    if kt == KT - 1:
                        mm.then_inc(S["tile_ready"], 1)

            pe.wait_ge(S["x_in_ident"], 16)
            for t in range(TT):
                pe.wait_ge(S[f"x_in{t}"], 16)
                for kt in range(KT):
                    mm = pe.transpose(bank[kt][:, t * P:(t + 1) * P], x_tok[:, t, kt * P:(kt + 1) * P], ident)
                    if t == TT - 1:
                        mm.then_inc(S["xt_done"], 1)
            pe.wait_ge(S["xT_ready"], 3)
            pe.wait_ge(S["in_rowsA"], 16 * 13)
            pe.transpose(bank[1][:, 0:NA], rowsA[:, :], ident[0:NA, 0:NA]).then_inc(S["vecs_done"], 1)
            pe.wait_ge(S["in_rowsB"], 16)
            pe.transpose(bank[2][:, 0:NB], rowsB[:, :], ident[0:NB, 0:NB]).then_inc(S["vecs_done"], 1)
            pe.wait_ge(S["in_mats"], 16)
            for kt in range(KT):
                norm_sum("n0", 0, kt)
            pe.wait_ge(S["xT_ready"], 5)
            pe.wait_ge(S["in_rel"], 48)
            pe.matmul(bank[3][0:ATT_H, :], relT[:, :], onehot[:, 0:SEQ], start=True, stop=True)
            pe.matmul(bank[4][0:ATT_H, 0:P], relT[:, :], onehot[:, SEQ:], start=True, stop=True)\
                .then_inc(S["rel_done"], 1)

            def fold(c):
                pe.wait_ge(S["ada_piece"], 8 * (c + 1))
                for j in range(8):
                    jj = 8 * c + j
                    mm = pe.matmul(bank[7][0:48, 0:P], select[:, 47 - jj:95 - jj], ada_acc[c % 2][:, j * P:(j + 1) * P],
                                   start=jj == 0, stop=jj == 47)
                mm.then_inc(S["ada_fold"], 1)

            for n in range(S0_BLOCKS):
                if n == 0:
                    pe.wait_ge(S["rms_hf"], before("n0", "hf") + 1)
                    pe.wait_ge(S["xT_ready"], 8)
                    pe.wait_ge(S["cols_ready"], 2)
                gemm(n, tiles_of(n)[0], (0,) if n == 0 else (0, 1), ready=(S["rms_lo"], before("n0", "lo") + 1) if n == 0 else None)
                if n >= 1:
                    for k in norm_of(n - 1):
                        pe.wait_ge(S["sq_done"], k + 1)
                        if k == 0:
                            pe.wait_ge(S["brow_ready"], 2)
                        if k >= 2:
                            pe.wait_ge(S["nt_done"], k - 1)
                        pe.matmul(bank[2 + k % 2][:, :], m(C_ONE if k < 8 else C_BLK), sq[k % 2][:, :],
                                  start=True, stop=True).then_inc(S["sum_done"], 1)
                if n == 1:
                    evac(pe, 0)
                    pe.wait_ge(S["brow_ready"], 2)
                    for t in range(TT):
                        mm = pe.transpose(bank[4][:, 8 * t:8 * t + 8], baT[:, t * P:(t + 1) * P], ident[0:8, 0:8])
                    mm.then_inc(S["ba_tr"], 1)
                for c in fold_at(n):
                    if c == 0:
                        pe.wait_ge(S["xT_ready"], 8)
                    fold(c)
            pe.wait_ge(S["nt_done"], 16)
            pe.wait_ge(S["ba_pre"], 1)
            for T in range(21, 25):
                evac(pe, T)
            for t in range(TT):
                for f in range(4):
                    mm = pe.transpose(bank[2 + t][:, f * P:(f + 1) * P], v_att[:, f, t * P:(t + 1) * P], ident)
            mm.then_inc(S["v_tr"], 1)
            pe.wait_ge(S["v_ready"], 4)
            pe.wait_ge(S["norm_done"], 16)

            def dilated_fill(w):
                gate_steps(dil_steps, w)
                for c in range(ADA_S0 // 8, 6):
                    if w == 8 * (c + 1) - ADA_S0 + 1:
                        fold(c)

            def attention(tag, units, tail=None):
                units = list(units)
                p_, pT_ = bufs[tag][1:]
                M = len(units[0]["maps"])
                maps = [mp for u in units for mp in u["maps"]]

                def qk(g):
                    if g >= len(maps):
                        return
                    if g >= 2:
                        pe.wait_ge(S["att_s"], before(tag, "s") + g - 1)
                    mp = maps[g]
                    pe.matmul(bank[QK[g % 2]][:, 0:mp["k"].shape[-1]], mp["q"], mp["k"], start=True, stop=True)\
                        .then_inc(S["att_qk"], 1)

                def turn(w):
                    pe.wait_ge(S["att_p"], before(tag, "p") + w + 1)
                    if w >= 2:
                        pe.wait_ge(S["att_pT"], before(tag, "pT") + w - 1)
                    for j in range(units[w]["n"]):
                        mm = pe.transpose(bank[TB[w % 2]][:, j * P:(j + 1) * P], p_[w % 2][:, j * P:(j + 1) * P], ident)
                    mm.then_inc(S["att_t"], 1)

                def values(w):
                    u = units[w]
                    pe.wait_ge(S["att_pT"], before(tag, "pT") + w + 1)
                    if u["new"] and tag == "a1" and u["group"] >= 1:
                        pe.wait_ge(S["att_out"], u["group"])
                    elif u["new"] and u["group"] >= 2:
                        pe.wait_ge(S["att_out"], before(tag, "out") + u["group"] - 1)
                        if tag == "a3":
                            pe.wait_ge(S["d_mix"], u["group"] - 1)
                    r, c = u["out"]
                    for j in range(u["n"]):
                        mm = pe.matmul(bank[OB[tag][u["group"] % 2]][r, c], u["v"][j], pT_[w % 2][:, j * P:(j + 1) * P],
                                       start=j == 0, stop=j == u["n"] - 1)
                    mm.then_inc(S["att_pv"], 1)

                for g in range(2 * M):
                    qk(g)
                for w in range(len(units)):
                    for g in range(M * (w + 2), M * (w + 3)):
                        qk(g)
                    if tail:
                        tail(w)
                    if w >= 1:
                        values(w - 1)
                    turn(w)
                values(len(units) - 1)
                if tail:
                    for w in range(3):
                        tail(len(units) + w)

            attention("a1", units_a1(), dilated_fill)

            pe.wait_ge(S["modrow_ready"], 1)
            pe.transpose(bank[4][:, 0:48], modrow[:, :], ident[0:48, 0:48]).then_inc(S["mod_tr"], 1)

            pe.wait_ge(S["g_ready"], 1)
            pe.wait_ge(S["in_masks"], 16)
            for T in range(29, 33):
                evac(pe, T)
            pe.matmul(bank[5][:, 0:16], m(C_TRIU), gdec, start=True, stop=True).then_inc(S["dn_gct"], 1)
            def broadcasts(c):
                pe.wait_ge(S["dn_gtri"], 2 * c + 2)
                if c >= 2:
                    pe.wait_ge(S["dn_exp"], c - 1)
                    pe.wait_ge(S["dn_dtb"], c - 1)
                pe.matmul(bank[c % 2][:, :], m(C_ONE), P1[:, c % 2].rearrange("p h i -> p (h i)"), start=True, stop=True)\
                    .then_inc(S["dn_grow"], 1)
                pe.matmul(bank[2 + c % 2][:, :], m(C_STRIL), P1[:, 2 + c % 2].rearrange("p h i -> p (h i)"),
                          start=True, stop=True).then_inc(S["dn_brow"], 1)
            broadcasts(0)
            for c in range(TT):
                if c == 0:
                    pe.wait_ge(S["dn_egc"], 1)
                    pe.wait_ge(S["mod_ready"], 1)
                if c >= 1:
                    pe.wait_ge(S["dn_at"], 2 * c)
                tok = slice(c * P, (c + 1) * P)
                for h in range(DN_H):
                    pe.matmul(bank[5][:, h * P:(h + 1) * P], qkv[:, 4 + h, tok], qkv[:, 4 + h, tok], start=True, stop=True)
                for h in range(DN_H):
                    mm = pe.matmul(bank[6][:, h * P:(h + 1) * P], qkv[:, 4 + h, tok], qkv[:, h, tok], start=True, stop=True)
                mm.then_inc(S["dn_prod"], 1)
                for b, f in ((4, 4), (7, 8)):
                    if c >= 1:
                        pe.wait_ge(S["dn_kv"], 2 * c if b == 4 else 2 * c)
                    if b == 7 and c >= 1:
                        pe.wait_ge(S["dn_x"], c)
                    for h in range(DN_H):
                        mm = pe.transpose(bank[b][:, h * P:(h + 1) * P], qkv[:, f + h, tok], ident)
                    mm.then_inc(S["dn_ktr"], 1)
                if c + 1 < TT:
                    broadcasts(c + 1)
                pe.wait_ge(S["dn_at"], 2 * c + 1)
                pe.wait_ge(S["dn_kv"], 2 * c + 2)
                for h in range(DN_H):
                    mm = pe.transpose(bank[7][:, h * P:(h + 1) * P], AT[:, c, h, :], ident)
                mm.then_inc(S["dn_a"], 1)

            def prod1(l, c):
                pe.wait_ge(S["dn_x"] if l == 0 else S["dn_upd"], 4 if l == 0 else 4 * (l - 1) + c + 1)
                if l == 0:
                    pe.wait_ge(S["dn_dtb"], 4)
                    pe.wait_ge(S["dn_xt0"], 8)
                for h in range(DN_H):
                    mm = pe.matmul(bank[c % 2][:, h * P:(h + 1) * P], AT[:, c, h, :], X[:, c, h, :], start=True, stop=True)
                mm.then_inc(S["dn_p1"], 1)

            def prod2(l, c):
                pe.wait_ge(S["dn_p1s"], 4 * l + c + 1)
                if l * 4 + c >= 2:
                    pe.wait_ge(S["dn_upd"], 4 * l + c - 1)
                for h in range(DN_H):
                    if l < N_LVL - 1:
                        pe.matmul(bank[2 + c % 2][:, h * P:(h + 1) * P], XT[:, c, h, :], P1[:, c, h, :], start=True, stop=True)
                for h in range(DN_H):
                    mm = pe.matmul(bank[4 + c % 2][:, h * P:(h + 1) * P], P1[:, c, h, :], XT[:, c, h, :], start=True, stop=True)
                mm.then_inc(S["dn_z"], 1)

            for l in range(N_LVL):
                prod1(l, 0)
                for c in range(TT):
                    if c + 1 < TT:
                        prod1(l, c + 1)
                    prod2(l, c)
            for c in range(TT):
                pe.wait_ge(S["dn_upd"], 4 * (N_LVL - 1) + c + 1)
                if c >= 1:
                    pe.wait_ge(S["dn_u"], c)
                    pe.wait_ge(S["dn_w"], c)
                for h in range(DN_H):
                    pe.matmul(bank[6][:, h * P:(h + 1) * P], XT[:, c, h, :], vb[:, c, h, :], start=True, stop=True)
                for h in range(DN_H):
                    mm = pe.matmul(bank[7][:, h * P:(h + 1) * P], kbe[:, c, h, :], XT[:, c, h, :], start=True, stop=True)
                mm.then_inc(S["dn_uw"], 1)
            def out_sum(c):
                pe.wait_ge(S["dn_osq"], c + 1)
                if c >= 2:
                    pe.wait_ge(S["dn_scaled"], c - 1)
                pe.matmul(bank[2 + c % 2][:, :], m(C_INVH), Dk[c % 2][:, :, :].rearrange("p h i -> p (h i)"),
                          start=True, stop=True).then_inc(S["dn_osum"], 1)

            for c in range(TT):
                tok = slice(c * P, (c + 1) * P)
                if c >= 1:
                    pe.wait_ge(S["dn_s"], c)
                    for h in range(DN_H):
                        mm = pe.matmul(bank[0][:, h * P:(h + 1) * P], kbe[:, c, h, :], state[:, h, :], start=True, stop=True)
                    mm.then_inc(S["dn_ws"], 1)
                pe.wait_ge(*((S["dn_vn"], c) if c else (S["dn_u"], 4)))
                if c < TT - 1:
                    for h in range(DN_H):
                        mm = pe.matmul(bank[1][:, h * P:(h + 1) * P], ktail[:, c, h, :], vb[:, c, h, :], start=True, stop=True)
                    mm.then_inc(S["dn_su"], 1)
                ob = (4, 5, 6, 7)[c]
                if c == 0:
                    pe.wait_ge(S["dn_u"], 4)
                    pe.wait_ge(S["dn_w"], 4)
                for h in range(DN_H):
                    if c >= 1:
                        pe.matmul(bank[ob][:, h * P:(h + 1) * P], state[:, h, :], qkv[:, h, tok], start=True, stop=False)
                    mm = pe.matmul(bank[ob][:, h * P:(h + 1) * P], vb[:, c, h, :], attnT[:, c, h, :],
                                   start=c == 0, stop=True)
                mm.then_inc(S["dn_o"], 1)
                if c >= 1:
                    out_sum(c - 1)
            out_sum(TT - 1)
            for j in range(4):
                gemm(N_S1 + j, T_S1 + 2 * j, ready=None if j else {4: (S["att_lo"], 4), 0: (S["dn_lo"], 4)})
                for kt in (2 * j - 2, 2 * j - 1):
                    if kt >= 0:
                        norm_sum("n1", 2, kt)
            norm_sum("n1", 2, 6)
            norm_sum("n1", 2, 7)

            gemm(N_S2, T_S2, ready=(S["rms_lo"], before("n1", "lo") + 1))
            for j in range(1, 9):
                gemm(N_S2 + j, T_S2 + 2 * j)


            for T in range(GATE_T - 4, GATE_T):
                evac(pe, T)
            for t in range(TT):
                pe.transpose(bank[6][:, t * P:(t + 1) * P], vf[:, 0, t * P:(t + 1) * P], ident)
            for t in range(TT):
                for f in range(4):
                    mm = pe.transpose(bank[2 + t][:, f * P:(f + 1) * P], vf[:, 1 + f, t * P:(t + 1) * P], ident)
            mm.then_inc(S["v2_tr"], 1)
            pe.wait_ge(S["v2_ready"], 5)
            attention("a2", units_a2(), lambda w: gate_steps(swa_steps, w))

            def diff_norm(w):
                gate_steps(diff_steps, w)
                if w >= 6 and (w - 6) % 4 == 0:
                    h = (w - 6) // 4
                    pe.wait_ge(S["d_sq"], h + 1)
                    pe.matmul(bank[OB["a3"][h % 2]][:, :], m(C_INVH), osq[:, :], start=True, stop=True).then_inc(S["d_sum"], 1)

            attention("a3", units_a3(), diff_norm)

            evac(pe, T_S3 - 2)
            evac(pe, T_S3 - 1)
            for j in range(4):
                pe.wait_ge(S["lo_ready"], N_S3 + j + 1)
                for u in range(2):
                    for g in range(2):
                        T = T_S3 + 4 * j + 2 * u + g
                        bank_free(T)
                        for kt in range(4):
                            if T < T_S3 + 2:
                                pe.wait_ge(S["att_lo"], before("a3" if g else "a2", "lo") + kt + 1)
                            mm = three(ring(T)[:, :], (N_S3 + j) % 2, g * 1024 + kt * 256 + u * P,
                                       hh[:, 4 * g + kt, :], hl[:, 4 * g + kt, :], kt == 0, kt == 3)
                        mm.then_inc(S["tile_ready"], 1)
            for j in range(4):
                gemm(N_S4 + j, T_S4 + 2 * j, acts=(mh, ml), ready=(S["mg_lo"], 1) if j == 0 else None)
                for kt in (2 * j - 2, 2 * j - 1):
                    if kt >= 0:
                        norm_sum("n2", 2, kt)
            norm_sum("n2", 2, 6)
            norm_sum("n2", 2, 7)
            gemm(N_S5, T_S5, ready=(S["rms_lo"], before("n2", "lo") + 1))
            gemm(N_S5 + 1, T_S5 + 2)
            with pe.Fori(0, 10) as i:
                for s in range(2):
                    gemm(N_S5 + 2 + s, T_S5 + 4 + 2 * s, i=i)
            for T in range(T_S5 + 40, T_S5 + 44):
                evac(pe, T)
            pe.wait_ge(S["f_lo"], FT)

            def down(n, i=0, start=False, stop=False):
                pe.wait_ge(S["lo_ready"], n + 1 + 2 * i)
                for t in range(KT):
                    for h in range(2):
                        kt = bass.ds(2 * (n - N_S6) + h + 4 * i, 1)
                        mm = three(bank[t][:, :], n % 2, h * 1024 + t * P,
                                   fh[:, kt, :].rearrange("p k c -> p (k c)"), fl[:, kt, :].rearrange("p k c -> p (k c)"),
                                   start and h == 0, stop and h == 1)
                    if stop:
                        mm.then_inc(S["tile_ready"], 1)
                if not stop:
                    mm.then_inc(S["block_done"], 1)

            down(N_S6, start=True)
            with pe.Fori(0, 4) as i:
                down(N_S6 + 1, i)
                down(N_S6 + 2, i)
            down(N_S6 + 9)
            down(N_S6 + 10, stop=True)
            pe.wait_ge(S["x3_ready"], 1)
            for kt in range(KT):
                norm_sum("n3", 0, kt)
            for t in range(TT):
                for h in range(2):
                    k = 2 * t + h
                    if k == 0:
                        pe.wait_ge(S["x3_ready"], 8)
                    for f in range(4):
                        pe.wait_ge(S["y_ready"], 4 * h + f + 1)
                        mm = pe.transpose(bank[(k + 1) % 8][:, f * P:(f + 1) * P], yT[:, 4 * h + f, t * P:(t + 1) * P], ident)
                    mm.then_inc(S["y_tr"], 1)

        @block.scalar
        def _(act):
            link = Chain(act, "act_chain")

            def rows(name, src):
                n = ROWS_A[name]
                act.dma_start(rowsA[n:n + src.shape[0], :], src).then_inc(S["in_rowsA"], 16)

            vec = lambda ap: ap.rearrange("o (k p) -> (o k) p", p=P)
            rows("norm_w", vec(a["norm_w"]))
            act.dma_start(mats[:, 1:C_BLK + 1, :].rearrange("p n c -> p (n c)"), a["k_mats"][:, P:(C_BLK + 1) * P])\
                .then_inc(S["in_mats"], 16)
            rows("norm1_g", vec(a["norm1_g_2"]))
            rows("norm2_g", vec(a["norm2_g_2"]))
            rows("final_g", a["final_g_2"].rearrange("(k p) -> k p", p=P))
            rows("c", vec(a["c_2"]))
            rows("dn_norm_w", a["dn_norm_w"])
            rows("subln", a["diff_subln_g_2"])
            rows("conv_w", a["conv_w"][0].rearrange("k (t p) -> (k t) p", p=P))
            rows("conv_b", vec(a["conv_b_2"]))
            for name, ap in (("q_norm", a["q_norm_w"]), ("k_norm", a["k_norm_w"])):
                n = ROWS_A[name]
                for h in range(2):
                    act.dma_start(rowsA[n:n + 1, h * HD:(h + 1) * HD], ap).then_inc(S["in_rowsA"], 16)
            act.dma_start(rowsB[:, :], a["conv_w_2"][0].rearrange("k (t p) -> (k t) p", p=P)).then_inc(S["in_rowsB"], 16)
            act.dma_start(select, a["k_select"]).then_inc(S["in_small"], 16)
            act.dma_start(sinks, a["swa_sinks_2"].to_broadcast([P, 8])).then_inc(S["in_small"], 16)
            act.dma_start(dtb, a["dt_bias"].to_broadcast([P, DN_H])).then_inc(S["in_small"], 16)
            act.dma_start(alog, a["a_log"].to_broadcast([P, DN_H])).then_inc(S["in_small"], 16)
            act.dma_start(lamrow[:, :], a["diff_lambda_2"].rearrange("o f d -> o (f d)").to_broadcast([P, 4 * HD]))\
                .then_inc(S["in_small"], 16)

            act.wait_ge(S["x_in3"], 16)
            act.dma_start(mats[:, C_BLK + 1:, :].rearrange("p n c -> p (n c)"), a["k_mats"][:, (C_BLK + 1) * P:])\
                .then_inc(S["in_masks"], 16)

            def hi(n, i=0):
                s = n % 2
                act.wait_ge(S[f"raw_full{s}"], 32 * (n // 2 + 1) + 32 * i)
                slot_free(act, n, i)
                act.activation(used(whi[s], n), used(raw[s], n), ACT.Copy).then_inc(S["hi_ready"], 1)

            def squares(tag, kt, src, buf):
                if kt >= 2:
                    act.wait_ge(S["rms_sum"], before(tag, "sum") + kt - 1)
                act.activation(buf[kt % 2][:, :], src, ACT.Square).then_inc(S["rms_sq"], 1)

            def ln_exp():
                act.preload_act_table_set("natural_log_exp_and_others")

            def rsqrt(ps, y, yy, done):
                link(act.activation(yy, ps, ACT.Ln, bias=eps))
                link(act.activation(y, yy, ACT.Exp, scale=-0.5))
                act.activation(yy, y, ACT.Square).then_inc(S[done], 1)

            act.wait_ge(S["scal_done"], 1)
            ln_exp()
            for kt in range(KT):
                act.wait_ge(S["xT_ready"], kt + 1)
                squares("n0", kt, xT[:, kt, :], sq)
            hi(0)
            act.wait_ge(S["rms_sum"], before("n0", "sum") + KT)
            rsqrt(bank[0][:, :], ry[0][:, :], ryy[0][:, :], "rms_rs")
            hi(1)
            for kt in range(KT):
                act.wait_ge(S["rms_hf"], before("n0", "hf") + kt + 1)
                act.activation(hh[:, kt, :], h_f1[kt % 2][:, :], ACT.Copy).then_inc(S["rms_hi"], 1)
            act.wait_ge(S["scal_done"], 2)
            act.activation(lams[:, 2:4], lams[:, 0:2], ACT.Exp).then_inc(S["lam_exp"], 1)
            act.wait_ge(S["cols_ready"], 1)
            act.activation(csil, colA[:, ROWS_A["c"]:ROWS_A["c"] + 8], ACT.Silu).then_inc(S["csil_ready"], 1)

            for n in range(S0_BLOCKS):
                if n == 1:
                    act.wait_ge(S["brow_ready"], 2)
                    act.dma_start(toep, brow[:, :].rearrange("h (o x) -> h o x", o=1).to_broadcast([ATT_H, P, SEQ + P]))\
                        .then_inc(S["toep_out"], 16)
                ts = tiles_of(n)
                for T in ts:
                    if T == ts[-1]:
                        hi(n + 2)
                    if 1 <= n < 7:
                        evac(act, T)
                        act.activation(qkv[:, T - 1, :], cv[T % 2][:, :], ACT.Silu).then_inc(S["silu_done"], 1)
                for k, T in zip(norm_of(n), ts):
                    if k >= 2:
                        act.wait_ge(S["sum_done"], k - 1)
                    if n < 7:
                        act.wait_ge(S["silu_done"], T)
                        src = qkv[:, T - 1, :]
                    else:
                        evac(act, T)
                        src = qk_att[:, T - 13, :]
                    act.activation(sq[k % 2][:, :], src, ACT.Square).then_inc(S["sq_done"], 1)
                if n >= 1:
                    for k in norm_of(n - 1):
                        act.wait_ge(S["sum_done"], k + 1)
                        if k >= 2:
                            act.wait_ge(S["norm_done"], k - 1)
                        ln_exp()
                        rsqrt(bank[2 + k % 2][:, :], ry[k % 2][:, :], ryy[k % 2][:, :], "rs_done")
                if n == 4:
                    act.wait_ge(S["ba_pre"], 1)
                    act.activation(ea, alog, ACT.Exp)
                    link(act.activation(sl, sb_, ACT.Exp, scale=-1.0))
                    act.activation(sl, sl, ACT.Ln, bias=1.0)
                    act.activation(beta.rearrange("p (c h) -> p c h", c=TT), ba_tok[:, :, 0:4], ACT.Sigmoid)\
                        .then_inc(S["ba_act"], 1)

            act.preload_act_table_set("natural_log_exp_and_others")

            def attention(tag, units, tail):
                units = list(units)
                s_, p_, pT_ = bufs[tag]
                M = len(units[0]["maps"])
                maps = [mp for u in units for mp in u["maps"]]

                def exps(w):
                    if w >= len(units):
                        return
                    for g in range(M * w, M * w + M):
                        n = maps[g]["k"].shape[-1]
                        stat = st[g % 4]
                        act.wait_ge(S["att_s"], before(tag, "s") + g + 1)
                        if maps[g]["sink"] is not None:
                            act.activation(stat[:, 4:5], maps[g]["sink"], ACT.Exp, bias=stat[:, 1:2], scale=maps[g]["slope"])
                        act.activation(s_[g % (2 * M)][:, 0:n], s_[g % (2 * M)][:, 0:n], ACT.Exp, bias=stat[:, 1:2], scale=maps[g]["slope"],
                                       accum_out=stat[:, 2:3]).then_inc(S["att_e"], 1)

                exps(0)
                for w in range(len(units) + 4):
                    exps(w + 1)
                    if w < len(units):
                        n = units[w]["n"] * P
                        act.wait_ge(S["att_t"], before(tag, "t") + w + 1)
                        if w >= 2:
                            act.wait_ge(S["att_pv"], before(tag, "pv") + w - 1)
                        act.activation(pT_[w % 2][:, 0:n], bank[TB[w % 2]][:, 0:n], ACT.Copy).then_inc(S["att_pT"], 1)
                    tail(w)

            def gate_tiles(steps, w):
                for t, T, dst in tiles_done(steps, w):
                    if t % 2 == 0:
                        act.wait_ge(S["tile_ready"], T + 1)
                        act.activation(dst, gate_bank(T)[:, :], ACT.Copy).then_inc(S[f"evac{T % 4}"], 1)
                    else:
                        hi(FILL[steps][0] + t // 2 + 2)

            attention("a1", units_a1(), lambda w: gate_tiles(dil_steps, w))

            act.preload_act_table_set("natural_log_exp_and_others")
            act.wait_ge(S["dn_egc"], 1)
            link(act.activation(egc, gc, ACT.Exp))
            for c in range(TT):
                act.wait_ge(S["dn_dsub"], c + 1)
                if c >= 1:
                    act.wait_ge(S["dn_qd"], c)
                act.activation(state[:, :, :], four(bank[c % 2][:, :]), ACT.Exp)
                act.activation(tail[:, 4 * c:4 * c + 4], tail[:, 4 * c:4 * c + 4], ACT.Exp)
                for h in range(DN_H):
                    ins = act.activation(Dk[c % 2][:, h, :], bank[c % 2][:, h * P:(h + 1) * P], ACT.Relu,
                                         bias=gc[:, 4 * c + h:4 * c + h + 1], scale=-1.0)
                link(ins)
                act.activation(Dk[c % 2][:, :, :], Dk[c % 2][:, :, :], ACT.Exp, scale=-1.0).then_inc(S["dn_exp"], 1)
                act.wait_ge(S["bege_ready"], 1)
                act.wait_ge(S["dn_ktr"], 2 * c + 1)
                for h in range(DN_H):
                    ps = bank[4][:, h * P:(h + 1) * P]
                    act.activation(kbe[:, c, h, :], ps, ACT.Copy, scale=bege[:, 4 * c + h:4 * c + h + 1])
                    ins = act.activation(ktail[:, c, h, :], ps, ACT.Copy, scale=tail[:, 4 * c + h:4 * c + h + 1])
                ins.then_inc(S["dn_kv"], 1)
                act.wait_ge(S["dn_ktr"], 2 * c + 2)
                for h in range(DN_H):
                    ins = act.activation(vb[:, c, h, :], bank[7][:, h * P:(h + 1) * P], ACT.Copy,
                                         scale=beta[:, 4 * c + h:4 * c + h + 1])
                ins.then_inc(S["dn_kv"], 1)
            for T in range(29, 33):
                evac(act, T)
            act.activation(zs[:, :, :], zs[:, :, :], ACT.Silu).then_inc(S["gate_silu"], 1)
            act.activation(gate[:, :, :], gate[:, :, :], ACT.Silu).then_inc(S["gate_silu"], 1)
            act.preload_act_table_set("natural_log_exp_and_others")
            for c in range(TT):
                act.wait_ge(S["dn_uw"], c + 1)
                act.activation(kbe[:, c], four(bank[7][:, :]), ACT.Copy).then_inc(S["dn_w"], 1)

            for p in range(4):
                act.wait_ge(S["att_mix"], p + 1)
                act.activation(hh[:, 4 + p, :], qk_att[:, p, :], ACT.Copy).then_inc(S["att_hi"], 1)
            for c in range(TT + 2):
                if c < TT:
                    act.wait_ge(S["dn_o"], c + 1)
                    if c >= 2:
                        act.wait_ge(S["dn_osum"], c - 1)
                    act.activation(Dk[c % 2][:, :, :], four(bank[4 + c][:, :]), ACT.Square).then_inc(S["dn_osq"], 1)
                if 1 <= c <= TT:
                    e = c - 1
                    act.wait_ge(S["dn_osum"], e + 1)
                    if e >= 2:
                        act.wait_ge(S["dn_scaled"], e - 1)
                    rsqrt(four(bank[2 + e % 2][:, :]), ktail[:, 2 * (e % 2)], ktail[:, 2 * (e % 2) + 1], "dn_ors")
                if c >= 2:
                    e = c - 2
                    act.wait_ge(S["dn_mix"], e + 1)
                    act.activation(hh[:, 0:4, e * P:(e + 1) * P], four(mixf[e % 2][:, :]), ACT.Copy).then_inc(S["dn_hi"], 1)

            for j in range(4):
                if j >= 1:
                    hi(N_S1 + j + 1)
                for kt in (2 * j, 2 * j + 1):
                    evac(act, T_S1 + kt)
                    squares("n1", kt, xT[:, kt, :], nsq)

            def norm_h(tag, shift, n):
                act.wait_ge(S["rms_sum"], before(tag, "sum") + KT)
                rsqrt(bank[2][:, :], nry[0][:, :], nry[1][:, :], "rms_rs")
                hi(n)
                for kt in range(KT):
                    act.wait_ge(S["rms_hf"], before(tag, "hf") + kt + 1)
                    act.activation(nhf[kt % 2][:, :], nhf[kt % 2][:, :], ACT.Identity,
                                   bias=modc[:, shift + kt:shift + kt + 1]).then_inc(S["rms_aff"], 1)
                    act.wait_ge(S["rms_aff"], before(tag, "aff") + kt + 1)
                    act.activation(hh[:, kt, :], nhf[kt % 2][:, :], ACT.Copy).then_inc(S["rms_hi"], 1)

            norm_h("n1", 0, N_S2 + 1)
            for j in range(9):
                if j >= 1:
                    hi(N_S2 + j + 1)
                for T in (T_S2 + 2 * j, T_S2 + 2 * j + 1):
                    t = T - T_S2
                    if j < 2:
                        act.wait_ge(S["tile_ready"], T + 1)
                        for k in range(2):
                            r = slice(64 * k, 64 * k + 64)
                            ins = act.activation(q_a2[r, t, :], ring(T)[r, :], ACT.Copy,
                                                 scale=HD ** -0.5 / SWA_SLOPES[2 * t + k])
                        ins.then_inc(S[f"evac{T % 4}"], 1)
                    elif j in (3, 4):
                        act.wait_ge(S["tile_ready"], T + 1)
                        act.activation(q_a3[:, t - 6, :], ring(T)[:, :], ACT.Copy,
                                       scale=HD ** -0.5 / DIFF_SLOPES[t - 6]).then_inc(S[f"evac{T % 4}"], 1)
            hi(N_S2 + 10)

            def swa_tail(w):
                gate_tiles(swa_steps, w)

            act.preload_act_table_set("natural_log_exp_and_others")
            attention("a2", units_a2(), swa_tail)

            def diff_tail(w):
                gate_tiles(diff_steps, w)
                if w == 16:
                    evac(act, T_S3 - 1)
                    evac(act, T_S3 - 2)
                    for k in range(4):
                        act.activation(hh[:, k, :], branch_out(k), ACT.Copy).then_inc(S["att_hi"], 1)
                if w >= 5 and (w - 5) % 4 == 0 and (w - 5) // 4 < DN_H:
                    h = (w - 5) // 4
                    act.wait_ge(S["att_out"], before("a3", "out") + h + 1)
                    if h >= 1:
                        act.wait_ge(S["d_sum"], h)
                    act.activation(osq[:, :], of[h % 2][:, :], ACT.Square).then_inc(S["d_sq"], 1)
                if w >= 6 and (w - 6) % 4 == 0 and (w - 6) // 4 < DN_H:
                    h = (w - 6) // 4
                    act.wait_ge(S["d_sum"], h + 1)
                    if h >= 1:
                        act.wait_ge(S["d_mix"], h)
                    rsqrt(bank[OB["a3"][h % 2]][:, :], ory[0][:, :], ory[1][:, :], "d_rs")

            attention("a3", units_a3(), diff_tail)
            act.wait_ge(S["d_mix"], 4)
            for k in range(4, KT):
                act.activation(hh[:, k, :], branch_out(k), ACT.Copy).then_inc(S["att_hi"], 1)

            for j in range(4):
                if j >= 1:
                    hi(N_S3 + j + 1)
                for q in (2 * j, 2 * j + 1):
                    pair = sg[:, :, :].rearrange("p (g q) t -> p g q t", g=2)[:, :, q, :]
                    act.activation(pair, pair, ACT.Sigmoid).then_inc(S["sig_ready"], 1)
                for q in (2 * j, 2 * j + 1):
                    act.wait_ge(S["merged_ready"], q + 1)
                    act.activation(mh[:, q, :], mS[q % 2][:, :], ACT.Copy).then_inc(S["mg_hi"], 1)
            ln_exp()
            for j in range(4):
                hi(N_S4 + j + 1)
                for kt in (2 * j, 2 * j + 1):
                    evac(act, T_S4 + kt)
                    squares("n2", kt, xT[:, kt, :], nsq)
            norm_h("n2", 24, N_S5 + 1)
            with act.Fori(0, 11) as i:
                for s in range(2):
                    T = T_S5 + 2 * s
                    evac(act, T, i)
                    act.activation(fg[s][:, :], fc[s][:, :], ACT.Gelu).then_inc(S["f_gelu"], 1)
                    hi(N_S5 + s + 2, i)
                    evac(act, T + 1, i)
                    act.activation(fh[:, bass.ds(s + 2 * i, 1), :].rearrange("p k c -> p (k c)"), ff[s][:, :], ACT.Copy)\
                        .then_inc(S["f_hi"], 1)
            with act.Fori(0, 4) as i:
                for s in range(2):
                    hi(N_S6 + 2 + s, i)
            hi(N_S6 + 10)
            ln_exp()
            for kt in range(KT):
                act.wait_ge(S["x3_ready"], kt + 1)
                squares("n3", kt, xT[:, kt, :], nsq)
            act.wait_ge(S["rms_sum"], before("n3", "sum") + KT)
            rsqrt(bank[0][:, :], nry[0][:, :], nry[1][:, :], "rms_rs")
            for t in range(TT):
                act.wait_ge(S["y_tr"], 2 * t + 1)
                act.activation(y_tok[:, t, 0:512], bank[(2 * t + 1) % 8][:, :], ACT.Copy).then_inc(S["y_out0"], 1)

        @block.vector
        def _(dve):
            link = Chain(dve, "dve_chain")

            def rest(dst, src, high, done):
                return dve.tensor_tensor(dst, src, high.bitcast(F32), ALU.subtract).then_inc(S[done], 1)

            def newton(ps, y, yy, done=None):
                ins = dve.scalar_tensor_tensor(yy, ps, eps, yy, op0=ALU.add, op1=ALU.mult)
                if done:
                    ins.then_inc(S[done[0]], 1)
                    dve.wait_ge(S[done[0]], done[1])
                else:
                    link(ins)
                link(dve.scalar_tensor_tensor(yy, yy, -3.0, y, op0=ALU.add, op1=ALU.mult))

            dve.memset(eps, EPS).then_inc(S["scal_done"], 1)
            for kt in range(KT):
                dve.wait_ge(S["xt_done"], kt + 1)
                dve.tensor_copy(xT[:, kt, :], bank[kt][:, :]).then_inc(S["xT_ready"], 1)
            dve.wait_ge(S["vecs_done"], 1)
            dve.tensor_copy(colA[:, :], bank[1][:, 0:NA]).then_inc(S["cols_ready"], 1)
            dve.wait_ge(S["vecs_done"], 2)
            dve.tensor_copy(colB[:, :], bank[2][:, 0:NB]).then_inc(S["cols_ready"], 1)
            dve.wait_ge(S["cols_ready"], 2)
            dve.tensor_scalar(nw1, colA[:, 0:8], -0.5, None, ALU.mult)
            dve.tensor_scalar(gfc, colA[:, 24:32], -0.5, None, ALU.mult)
            dve.tensor_scalar(dncol, col("dn_norm_w"), -0.5, None, ALU.mult)
            dve.tensor_scalar(subcol, col("subln"), -0.5 * (1.0 - LAM_INIT), None, ALU.mult)
            dve.tensor_scalar(qcol, col("q_norm"), -0.5 * HD ** -0.5, None, ALU.mult)
            link(dve.tensor_scalar(kcol, col("k_norm"), -0.5, None, ALU.mult))
            dve.wait_ge(S["rms_rs"], before("n0", "rs") + 1)
            newton(bank[0][:, :], ry[0][:, :], ryy[0][:, :])

            def norm_h(tag, g, z, buf):
                for kt in range(KT + 1):
                    if 2 <= kt < KT:
                        dve.wait_ge(S["rms_lo"], before(tag, "lo") + kt - 1)
                    if kt < KT:
                        dve.scalar_tensor_tensor(buf[kt % 2][:, :], xT[:, kt, :], g[:, kt:kt + 1], z,
                                                 op0=ALU.mult, op1=ALU.mult).then_inc(S["rms_hf"], 1)
                    if kt >= 1:
                        dve.wait_ge(S["rms_hi"], before(tag, "hi") + kt)
                        rest(hl[:, kt - 1, :], buf[(kt - 1) % 2][:, :], hh[:, kt - 1, :], "rms_lo")

            norm_h("n0", nw1, ryy[0][:, :], h_f1)
            dve.wait_ge(S["rel_done"], 1)
            dve.tensor_tensor(brow[:, 0:SEQ], bank[3][0:ATT_H, :], logm[:, 0:SEQ], ALU.add).then_inc(S["brow_ready"], 1)
            dve.tensor_tensor(brow[:, SEQ:], bank[4][0:ATT_H, 0:P], logm[:, SEQ:], ALU.add).then_inc(S["brow_ready"], 1)
            dve.wait_ge(S["in_small"], 16 * 5)
            for h in range(ATT_H):
                dve.tensor_scalar(sinks[:, h:h + 1], sinks[:, h:h + 1], 1.0 / SWA_SLOPES[h], None, ALU.mult)
            for k in range(2):
                ins = dve.tensor_tensor_reduce(out=lamrow[:, 128 * k:128 * k + 64], in0=lamrow[:, 128 * k:128 * k + 64],
                                               in1=lamrow[:, 128 * k + 64:128 * k + 128], scale=1.0, scalar=0.0,
                                               op0=ALU.mult, op1=ALU.add, accum_out=lams[:, k:k + 1])
            ins.then_inc(S["scal_done"], 1)
            dve.wait_ge(S["lam_exp"], 1)
            link(dve.tensor_tensor(lams[:, 4:5], lams[:, 2:3], lams[:, 3:4], ALU.subtract))
            link(dve.tensor_scalar(lams[:, 5:6], lams[:, 4:5], -1.0, -LAM_INIT, ALU.mult, ALU.add))
            dve.wait_ge(S["csil_ready"], 1)
            piece = [0]

            def ada():
                p = piece[0]
                piece[0] += 1
                c, kt = divmod(p, KT)
                dve.wait_ge(S[f"ada_in{p % 2}"], 16 * (p // 2 + 1))
                acc = ada_acc[c % 2][:, :]
                if kt == 0:
                    if c >= 2:
                        dve.wait_ge(S["ada_fold"], c - 1)
                    ins = dve.tensor_scalar(acc, ada_w[p % 2][:, :], csil[:, 0:1], None, ALU.mult)
                else:
                    dve.wait_ge(S["ada_piece"], p)
                    ins = dve.scalar_tensor_tensor(acc, ada_w[p % 2][:, :], csil[:, kt:kt + 1], acc, op0=ALU.mult, op1=ALU.add)
                ins.then_inc(S["ada_piece"], 1)

            for n in range(S0_BLOCKS):
                for T in tiles_of(n):
                    ps = ring(T)
                    if 1 <= n < 7:
                        y = cv[T % 2]
                        dve.wait_ge(S["tile_ready"], T + 1)
                        q = T - 1
                        if q >= 2:
                            dve.wait_ge(S["silu_done"], q - 1)
                        link(dve.tensor_scalar(y[:, :], ps[:, :], col("conv_w", 36 + q), None, ALU.mult))
                        for k in range(1, 4):
                            ins = dve.scalar_tensor_tensor(y[:, k:], ps[:, 0:SEQ - k], col("conv_w", 12 * (3 - k) + q), y[:, k:],
                                                           op0=ALU.mult, op1=ALU.add)
                            if k < 3:
                                link(ins)
                        ins.then_inc(S[f"evac{T % 4}"], 1)
                    elif n == 0:
                        dve.wait_ge(S["tile_ready"], T + 1)
                        dve.tensor_copy(baT[:, :], ps[0:8, :]).then_inc(S[f"evac{T % 4}"], 1)
                    else:
                        dve.wait_ge(S["tile_ready"], T + 1)
                        dst = qk_att[:, T - 13, :] if n < 11 else v_att[:, T - 21, :]
                        dve.tensor_copy(dst, ps[:, :]).then_inc(S[f"evac{T % 4}"], 1)
                for _ in range(ADA_STEP.get(n, 0)):
                    ada()
                if n >= 1:
                    for k in norm_of(n - 1):
                        dve.wait_ge(S["rs_done"], k + 1)
                        newton(bank[2 + k % 2][:, :], ry[k % 2][:, :], ryy[k % 2][:, :], ("nt_done", k + 1))
                        if k < 8:
                            t, g = qkv[:, k, :], -0.5 * P ** -0.5 if k < 4 else -0.5
                        else:
                            t, g = qk_att[:, k - 8, :], qcol if k < 12 else kcol
                        dve.scalar_tensor_tensor(t, t, g, ryy[k % 2][:, :], op0=ALU.mult, op1=ALU.mult)\
                            .then_inc(S["norm_done"], 1)
                if n == 3:
                    dve.wait_ge(S["ba_tr"], 1)
                    link(dve.tensor_copy(ba_tok, bank[4][:, 0:32].rearrange("p (c e) -> p c e", c=TT)))
                    x4 = lambda ap: ap.rearrange("p (c h) -> p c h", c=TT)
                    link(dve.tensor_tensor(x4(sa), ba_tok[:, :, 4:8],
                                           dtb.rearrange("p (o h) -> p o h", o=1).to_broadcast([P, TT, DN_H]), ALU.add))
                    dve.tensor_scalar(sr, sa, 0.0, None, ALU.max)
                    link(dve.tensor_scalar(sb_, sa, -1.0, None, ALU.mult))
                    dve.tensor_tensor(sb_, sb_, sa, ALU.max).then_inc(S["ba_pre"], 1)
                if n == 5:
                    dve.wait_ge(S["ba_act"], 1)
                    link(dve.tensor_tensor(sr, sr, sl, ALU.add))
                    dve.scalar_tensor_tensor(x4(gdec), x4(sr), -1.0,
                                             ea.rearrange("p (o h) -> p o h", o=1).to_broadcast([P, TT, DN_H]),
                                             op0=ALU.mult, op1=ALU.mult).then_inc(S["g_ready"], 1)
            dve.wait_ge(S["v_tr"], 1)
            for t in range(TT):
                dve.tensor_copy(v_att[:, t, :], bank[2 + t][:, :]).then_inc(S["v_ready"], 1)

            def attention(tag, units, bias_wait, tail):
                units = list(units)
                s_, p_, pT_ = bufs[tag]
                M = len(units[0]["maps"])
                maps = [mp for u in units for mp in u["maps"]]

                def scores(w):
                    if w >= len(units):
                        return
                    if w >= 2:
                        dve.wait_ge(S["att_p"], before(tag, "p") + w - 1)
                    for g in range(M * w, M * w + M):
                        mp = maps[g]
                        n = mp["k"].shape[-1]
                        stat = st[g % 4]
                        if g % (TT * M) == 0:
                            bias_wait(units[w]["head"])
                        dve.wait_ge(S["att_qk"], before(tag, "qk") + g + 1)
                        link(dve.tensor_tensor_reduce(out=s_[g % (2 * M)][:, 0:n], in0=bank[QK[g % 2]][:, 0:n], in1=mp["bias"],
                                                      scale=1.0, scalar=-3e38, op0=ALU.add, op1=ALU.max, accum_out=stat[:, 0:1]))
                        if mp["sink"] is None:
                            ins = dve.tensor_scalar(stat[:, 1:2], stat[:, 0:1], -mp["slope"], None, ALU.mult)
                        else:
                            ins = dve.tensor_scalar(stat[:, 1:2], stat[:, 0:1], mp["sink"], -mp["slope"], ALU.max, ALU.mult)
                        ins.then_inc(S["att_s"], 1)

                def probs(w):
                    n = units[w]["n"] * P
                    p = p_[w % 2][:, 0:n]
                    for k in range(M):
                        g = M * w + k
                        stat = st[g % 4]
                        s = s_[g % (2 * M)][:, 0:n]
                        dve.wait_ge(S["att_e"], before(tag, "e") + g + 1)
                        if maps[g]["sink"] is not None:
                            link(dve.tensor_tensor(stat[:, 2:3], stat[:, 2:3], stat[:, 4:5], ALU.add))
                        link(dve.reciprocal(stat[:, 3:4], stat[:, 2:3]))
                        if k == 0:
                            if w >= 2:
                                dve.wait_ge(S["att_t"], before(tag, "t") + w - 1)
                            ins = dve.tensor_scalar(p, s, stat[:, 3:4], None, ALU.mult)
                            if M == 2:
                                link(ins)
                        else:
                            link(dve.tensor_tensor(stat[:, 5:6], stat[:, 3:4], lams[:, 5:6], ALU.mult))
                            ins = dve.scalar_tensor_tensor(p, s, stat[:, 5:6], p, op0=ALU.mult, op1=ALU.add)
                    ins.then_inc(S["att_p"], 1)

                scores(0)
                scores(1)
                for w in range(len(units) + 4):
                    if w < len(units):
                        probs(w)
                    scores(w + 2)
                    tail(w)

            def gate_tiles(steps, w):
                for t, T, dst in tiles_done(steps, w):
                    if t % 2 == 1:
                        dve.wait_ge(S["tile_ready"], T + 1)
                        dve.tensor_copy(dst, gate_bank(T)[:, :]).then_inc(S[f"evac{T % 4}"], 1)

            def tail1(w):
                if piece[0] < 48:
                    ada()
                gate_tiles(dil_steps, w - 1)
                if w >= 8 and w % 8 == 0:
                    p = w // 8 - 1
                    dve.wait_ge(S["att_pv"], 8 * p + 8)
                    dve.tensor_copy(qk_att[:, p, :], bank[6][:, :]).then_inc(S["att_out"], 1)

            attention("a1", units_a1(), lambda h: dve.wait_ge(S[f"toe_in{h}"], 16), tail1)

            dve.wait_ge(S["ada_fold"], 6)
            dve.wait_ge(S["in_rowsM"], 16)
            dve.tensor_tensor(modrow[:, :], bank[7][0:48, 0:P], rowsM[:, :], ALU.add).then_inc(S["modrow_ready"], 1)
            dve.wait_ge(S["mod_tr"], 1)
            link(dve.tensor_copy(modc[:, :], bank[4][:, 0:48]))
            for g, row, scale in ((g1c, ROWS_A["norm1_g"], 8), (g2c, ROWS_A["norm2_g"], 32)):
                link(dve.scalar_tensor_tensor(g, modc[:, scale:scale + 8], 1.0, colA[:, row:row + 8], op0=ALU.add, op1=ALU.mult))
                ins = dve.tensor_scalar(g, g, -0.5, None, ALU.mult)
            ins.then_inc(S["mod_ready"], 1)
            dve.wait_ge(S["toep_out"], 16)
            dve.wait_ge(S["tile_ready"], 33)
            dve.wait_ge(S["dn_gct"], 1)
            dve.tensor_copy(gc, bank[5][:, 0:16]).then_inc(S["dn_egc"], 1)

            dve.wait_ge(S["dn_egc"], 1)
            for c in range(TT):
                four_c = slice(4 * c, 4 * c + 4)
                tok = slice(c * P, (c + 1) * P)
                dve.wait_ge(S["dn_grow"], c + 1)
                last = four(bank[c % 2][:, :])[:, :, P - 1:P].rearrange("p h o -> p (h o)")
                dve.tensor_tensor(tail[:, four_c], last, gc[:, four_c], ALU.subtract).then_inc(S["dn_dsub"], 1)
                dve.wait_ge(S["dn_exp"], c + 1)
                if c == 0:
                    dve.tensor_tensor(bege, beta, egc, ALU.mult).then_inc(S["bege_ready"], 1)
                link(dve.tensor_tensor(Dk[c % 2][:, :, :], Dk[c % 2][:, :, :], each(m(C_TRIU)), ALU.mult))
                dve.wait_ge(S["dn_brow"], c + 1)
                dve.tensor_tensor(attnT[:, c], four(bank[2 + c % 2][:, :]), Dk[c % 2][:, :, :], ALU.mult).then_inc(S["dn_dtb"], 1)
                dve.wait_ge(S["dn_dtb"], c + 1)
                dve.wait_ge(S["dn_prod"], c + 1)
                dve.tensor_tensor(AT[:, c], four(bank[5][:, :]), attnT[:, c], ALU.mult).then_inc(S["dn_at"], 1)
                dve.wait_ge(S["dn_at"], 2 * c + 1)
                dve.tensor_tensor(attnT[:, c], four(bank[6][:, :]), Dk[c % 2][:, :, :], ALU.mult).then_inc(S["dn_at"], 1)
                dve.tensor_copy(glst[:, four_c], state[:, :, P - 1:P].rearrange("p h o -> p (h o)"))
                dve.tensor_tensor(qkv[:, 0:4, tok], qkv[:, 0:4, tok], state[:, :, :], ALU.mult).then_inc(S["dn_qd"], 1)
                dve.wait_ge(S["dn_a"], c + 1)
                link(dve.tensor_tensor(X[:, c], four(bank[7][:, :]), each(m(C_NM0)), ALU.mult))
                dve.tensor_tensor(X[:, c], X[:, c], each(ident), ALU.add).then_inc(S["dn_x"], 1)

            def masked(l, c):
                dve.wait_ge(S["dn_p1"], 4 * l + c + 1)
                dve.tensor_tensor(P1[:, c], four(bank[c % 2][:, :]), each(m(C_LVL + l)), ALU.mult).then_inc(S["dn_p1s"], 1)

            def update(l, c):
                dve.wait_ge(S["dn_z"], 4 * l + c + 1)
                if l < N_LVL - 1:
                    dve.tensor_tensor(X[:, c], X[:, c], four(bank[2 + c % 2][:, :]), ALU.subtract)
                dve.tensor_tensor(XT[:, c], XT[:, c], four(bank[4 + c % 2][:, :]), ALU.subtract).then_inc(S["dn_upd"], 1)

            for l in range(N_LVL):
                masked(l, 0)
                for c in range(TT):
                    if c + 1 < TT:
                        masked(l, c + 1)
                    update(l, c)
            for c in range(TT):
                dve.wait_ge(S["dn_uw"], c + 1)
                dve.tensor_copy(vb[:, c], four(bank[6][:, :])).then_inc(S["dn_u"], 1)
            dve.wait_ge(S["dn_u"], 4)
            dve.wait_ge(S["gate_silu"], 1)
            for c in range(TT + 2):
                if c < TT:
                    if c >= 1:
                        dve.wait_ge(S["dn_ws"], c)
                        dve.tensor_tensor(vb[:, c], vb[:, c], four(bank[0][:, :]), ALU.subtract).then_inc(S["dn_vn"], 1)
                if c < TT - 1:
                    dve.wait_ge(S["dn_su"], c + 1)
                    if c == 0:
                        dve.tensor_copy(state[:, :, :], four(bank[1][:, :])).then_inc(S["dn_s"], 1)
                    else:
                        dve.wait_ge(S["dn_o"], c + 1)
                        for h in range(DN_H):
                            ins = dve.scalar_tensor_tensor(state[:, h, :], state[:, h, :], glst[:, 4 * c + h:4 * c + h + 1],
                                                           bank[1][:, h * P:(h + 1) * P], op0=ALU.mult, op1=ALU.add)
                        ins.then_inc(S["dn_s"], 1)
                    dve.wait_ge(S["dn_s"], c + 1)
                if c >= 2:
                    e = c - 2
                    y, yy = ktail[:, 2 * (e % 2)], ktail[:, 2 * (e % 2) + 1]
                    dve.wait_ge(S["dn_ors"], e + 1)
                    newton(four(bank[2 + e % 2][:, :]), y, yy)
                    if e >= 2:
                        dve.wait_ge(S["dn_lo"], e - 1)
                    dve.scalar_tensor_tensor(four(mixf[e % 2][:, :]), four(bank[4 + e][:, :]), dncol, yy,
                                             op0=ALU.mult, op1=ALU.mult).then_inc(S["dn_scaled"], 1)

            for j in range(4):
                for kt in (2 * j, 2 * j + 1):
                    T = T_S1 + kt
                    dve.wait_ge(S["tile_ready"], T + 1)
                    dve.tensor_tensor(xT[:, kt, :], xT[:, kt, :], ring(T)[:, :], ALU.add).then_inc(S[f"evac{T % 4}"], 1)
            dve.wait_ge(S["rms_rs"], before("n1", "rs") + 1)
            newton(bank[2][:, :], nry[0][:, :], nry[1][:, :])
            norm_h2 = lambda tag, g: norm_h(tag, g, nry[1][:, :], nhf)
            norm_h2("n1", g1c)
            for j in range(9):
                for T in (T_S2 + 2 * j, T_S2 + 2 * j + 1):
                    t = T - T_S2
                    ps = ring(T)
                    if j in (2, 5, 6, 7, 8):
                        dve.wait_ge(S["tile_ready"], T + 1)
                    if t == 4:
                        for g in range(2):
                            for half in range(2):
                                ins = dve.tensor_copy(k_a2[64 * half:64 * half + 64, g, :], ps[64 * g:64 * g + 64, :])
                        ins.then_inc(S[f"evac{T % 4}"], 1)
                    elif t == 5 or j in (5, 6, 7, 8):
                        dst = vf[:, 0, :] if t == 5 else k_a3[:, t - 10, :] if t < 14 else vf[:, t - 13, :]
                        dve.tensor_copy(dst, ps[:, :]).then_inc(S[f"evac{T % 4}"], 1)
            dve.wait_ge(S["v2_tr"], 1)
            dve.tensor_copy(v_a2[:, :, :], four(bank[6][:, :])).then_inc(S["v2_ready"], 1)
            for t in range(TT):
                dve.tensor_copy(v_a3[:, t, :], bank[2 + t][:, :]).then_inc(S["v2_ready"], 1)

            def tail2(w):
                gate_tiles(swa_steps, w - 1)
                if w >= 9 and (w - 9) % 8 == 0:
                    p = (w - 9) // 8
                    dve.wait_ge(S["att_pv"], before("a2", "pv") + 8 * p + 8)
                    dve.tensor_copy(branch_out(p), bank[OB["a2"][p % 2]][:, :]).then_inc(S["att_out"], 1)

            attention("a2", units_a2(), lambda h: dve.wait_ge(S["in_alibi"], 16), tail2)

            def split_branches(k0, k1):
                for k in range(k0, k1):
                    dve.wait_ge(S["att_hi"], before("a2", "hi") + k + 1)
                    rest(hl[:, k, :], branch_out(k), hh[:, k, :], "att_lo")

            def tail3(w):
                gate_tiles(diff_steps, w - 1)
                if w == 18:
                    split_branches(0, 4)
                if w >= 5 and (w - 5) % 4 == 0 and (w - 5) // 4 < DN_H:
                    h = (w - 5) // 4
                    dve.wait_ge(S["att_pv"], before("a3", "pv") + 4 * h + 4)
                    if h >= 2:
                        dve.wait_ge(S["d_mix"], h - 1)
                    dve.tensor_copy(of[h % 2][:, :], bank[OB["a3"][h % 2]][:, :]).then_inc(S["att_out"], 1)
                if w >= 7 and (w - 7) % 4 == 0 and (w - 7) // 4 < DN_H:
                    h = (w - 7) // 4
                    dve.wait_ge(S["d_rs"], h + 1)
                    newton(bank[OB["a3"][h % 2]][:, :], ory[0][:, :], ory[1][:, :])
                    dve.scalar_tensor_tensor(branch_out(4 + h), of[h % 2][:, :], subcol, ory[1][:, :], op0=ALU.mult, op1=ALU.mult)\
                        .then_inc(S["d_mix"], 1)

            attention("a3", units_a3(), lambda h: None, tail3)
            split_branches(4, KT)

            for j in range(4):
                for q in (2 * j, 2 * j + 1):
                    dve.wait_ge(S["sig_ready"], q + 1)
                    for g, buf in ((0, mA), (1, mD)):
                        T = T_S3 + 2 * q + g
                        dve.wait_ge(S["tile_ready"], T + 1)
                        dve.tensor_tensor(buf[q % 2][:, :], ring(T)[:, :], sg[:, 8 * g + q, :], ALU.mult)\
                            .then_inc(S[f"evac{T % 4}"], 1)
                    evac(dve, T_S3 + 2 * q)
                    evac(dve, T_S3 + 2 * q + 1)
                    dve.tensor_tensor(mS[q % 2][:, :], mA[q % 2][:, :], mD[q % 2][:, :], ALU.add).then_inc(S["merged_ready"], 1)
                    dve.wait_ge(S["mg_hi"], q + 1)
                    rest(ml[:, q, :], mS[q % 2][:, :], mh[:, q, :], "mg_lo")
            for j in range(4):
                for kt in (2 * j, 2 * j + 1):
                    T = T_S4 + kt
                    dve.wait_ge(S["tile_ready"], T + 1)
                    dve.scalar_tensor_tensor(xT[:, kt, :], ring(T)[:, :], modc[:, 16 + kt:17 + kt], xT[:, kt, :],
                                             op0=ALU.mult, op1=ALU.add).then_inc(S[f"evac{T % 4}"], 1)
            dve.wait_ge(S["rms_rs"], before("n2", "rs") + 1)
            newton(bank[2][:, :], nry[0][:, :], nry[1][:, :])
            norm_h2("n2", g2c)
            with dve.Fori(0, 11) as i:
                for s in range(2):
                    T = T_S5 + 2 * s
                    pa, pg = ring(T), ring(T + 1)
                    cw = lambda tap: colB[:, bass.ds(tap * FT + s + 2 * i, 1)]
                    dve.wait_ge(S["tile_ready"], T + 1 + 4 * i)
                    dve.tensor_scalar(fc[s][:, :], pa[:, :], cw(2), colA[:, bass.ds(ROWS_A["conv_b"] + s + 2 * i, 1)],
                                      ALU.mult, ALU.add).then_inc(S["f_chain"], 1)
                    dve.wait_ge(S["f_chain"], 2 * s + 1 + 4 * i)
                    dve.scalar_tensor_tensor(fc[s][:, 1:], pa[:, 0:SEQ - 1], cw(1), fc[s][:, 1:], op0=ALU.mult, op1=ALU.add)\
                        .then_inc(S["f_chain"], 1)
                    dve.wait_ge(S["f_chain"], 2 * s + 2 + 4 * i)
                    dve.scalar_tensor_tensor(fc[s][:, 2:], pa[:, 0:SEQ - 2], cw(0), fc[s][:, 2:], op0=ALU.mult, op1=ALU.add)\
                        .then_inc(S[f"evac{T % 4}"], 1)
                    dve.wait_ge(S["tile_ready"], T + 2 + 4 * i)
                    dve.wait_ge(S["f_gelu"], s + 1 + 2 * i)
                    dve.tensor_tensor(ff[s][:, :], pg[:, :], fg[s][:, :], ALU.mult).then_inc(S[f"evac{(T + 1) % 4}"], 1)
                    dve.wait_ge(S["f_hi"], s + 1 + 2 * i)
                    j = bass.ds(s + 2 * i, 1)
                    rest(fl[:, j, :].rearrange("p k c -> p (k c)"), ff[s][:, :], fh[:, j, :].rearrange("p k c -> p (k c)"), "f_lo")
            for kt in range(KT):
                dve.wait_ge(S["tile_ready"], T_S5 + 44 + kt + 1)
                dve.scalar_tensor_tensor(xT[:, kt, :], bank[kt][:, :], modc[:, 40 + kt:41 + kt], xT[:, kt, :],
                                         op0=ALU.mult, op1=ALU.add).then_inc(S["x3_ready"], 1)
            dve.wait_ge(S["rms_rs"], before("n3", "rs") + 1)
            newton(bank[0][:, :], nry[0][:, :], nry[1][:, :])
            for kt in range(KT):
                dve.scalar_tensor_tensor(yT[:, kt, :], xT[:, kt, :], gfc[:, kt:kt + 1], nry[1][:, :], op0=ALU.mult, op1=ALU.mult)\
                    .then_inc(S["y_ready"], 1)
            for t in range(TT):
                dve.wait_ge(S["y_tr"], 2 * t + 2)
                dve.tensor_copy(y_tok[:, t, 512:1024], bank[(2 * t + 2) % 8][:, :]).then_inc(S["y_out1"], 1)


INPUTS = ["x", "norm_w", "w_in", "conv_w", "a_log", "dt_bias", "dn_norm_w", "q_norm_w", "k_norm_w", "rel_bias",
          "w_out", "c_2", "w_ada_2", "b_ada_2", "norm1_g_2", "w_in_2", "swa_sinks_2", "diff_lambda_2",
          "diff_subln_g_2", "w_branch_swa_2", "w_branch_diff_2", "w_out_2", "norm2_g_2", "w_up_2", "conv_w_2",
          "conv_b_2", "w_down_2", "final_g_2"]


def kernel(**inputs):
    import concourse.bacc as bacc
    from concourse.bass_utils import run_bass_kernel_spmd

    nc = bacc.Bacc("TRN2", target_bir_lowering=False, num_devices=1, dynamic_dma_scratch_size=2048)
    arrays = {n: np.ascontiguousarray(inputs[n]) for n in INPUTS}
    arrays.update(constants())
    aps = {n: nc.dram_tensor(n, v.shape, mybir.dt.from_np(v.dtype), kind="ExternalInput").ap() for n, v in arrays.items()}
    out = nc.dram_tensor("out", (1, SEQ, D), F32, kind="ExternalOutput").ap()
    toep = nc.dram_tensor("bias_rows", (ATT_H, P, SEQ + P), F32, kind="Internal").ap()
    build(nc, aps, out, toep)
    r = run_bass_kernel_spmd(nc, [arrays], core_ids=[0])
    return r.results[0]["out"]
```
